# Optimizing a Trainium2 kernel written in Bass

```python
import math
import jax, jax.numpy as jnp
from jax import lax
import numpy as np

D_MODEL = 1024
BATCH = 1
SEQ = 256
DEPTH = 2

N_MIXERS = 2
EPS = 1e-6
BLOCK = 128
RET_HEADS = D_MODEL // 256
RET_DK = 256
RET_DV = 2 * RET_DK
RET_QK = RET_HEADS * RET_DK
RET_V = RET_HEADS * RET_DV
RET_IN = 2 * RET_QK + 2 * RET_V
ROPE_BASE = 10000.0
SB_HEADS = D_MODEL // 64
SB_DH = 64
SB_IN = 3 * SB_HEADS * SB_DH
D_FF = 2816
CONV_W = 3


def _rmsnorm(x, g):
    xf = x.astype(jnp.float32)
    y = xf * lax.rsqrt(jnp.mean(xf * xf, axis=-1, keepdims=True) + EPS)
    return (y * g.astype(jnp.float32)).astype(x.dtype)

def _rotary(x, cos, sin):
    x1, x2 = jnp.split(x, 2, axis=-1)
    c = cos[None, :, None, :]
    s = sin[None, :, None, :]
    return jnp.concatenate([x1 * c - x2 * s, x1 * s + x2 * c], axis=-1)

def _retention(h, w_in, w_out):
    B_, S_, _ = h.shape
    nc = S_ // BLOCK
    proj = h @ w_in
    q, k, v, g = jnp.split(proj, [RET_QK, 2 * RET_QK, 2 * RET_QK + RET_V], axis=-1)
    pos = jnp.arange(S_, dtype=jnp.float32)
    inv_freq = ROPE_BASE ** (-jnp.arange(0, RET_DK, 2, dtype=jnp.float32) / RET_DK)
    ang = pos[:, None] * inv_freq[None, :]
    cos, sin = jnp.cos(ang), jnp.sin(ang)
    q = _rotary(q.reshape(B_, S_, RET_HEADS, RET_DK).astype(jnp.float32), cos, sin)
    k = _rotary(k.reshape(B_, S_, RET_HEADS, RET_DK).astype(jnp.float32), cos, sin) * (RET_DK ** -0.5)
    v = v.reshape(B_, S_, RET_HEADS, RET_DV).astype(jnp.float32)
    qc = q.transpose(0, 2, 1, 3).reshape(B_, RET_HEADS, nc, BLOCK, RET_DK)
    kc = k.transpose(0, 2, 1, 3).reshape(B_, RET_HEADS, nc, BLOCK, RET_DK)
    vc = v.transpose(0, 2, 1, 3).reshape(B_, RET_HEADS, nc, BLOCK, RET_DV)
    log_g = jnp.log(1.0 - 2.0 ** (-5.0 - jnp.arange(RET_HEADS, dtype=jnp.float32)))
    cpos = jnp.arange(BLOCK, dtype=jnp.float32)
    diff = cpos[:, None] - cpos[None, :]
    dmat = jnp.where(diff[None] >= 0,
                     jnp.exp(jnp.maximum(diff, 0.0)[None] * log_g[:, None, None]), 0.0)
    scores = jnp.einsum('bhncd,bhnkd->bhnck', qc, kc) * dmat[None, :, None]
    intra = jnp.einsum('bhnck,bhnke->bhnce', scores, vc)
    q_dec = qc * jnp.exp((cpos + 1.0)[None, :] * log_g[:, None])[None, :, None, :, None]
    k_dec = kc * jnp.exp((BLOCK - 1.0 - cpos)[None, :] * log_g[:, None])[None, :, None, :, None]
    chunk_decay = jnp.exp(BLOCK * log_g)[None, :, None, None]

    def step(state, xs):
        qd, kd, vv = xs
        out = jnp.einsum('bhcd,bhde->bhce', qd, state)
        state = chunk_decay * state + jnp.einsum('bhkd,bhke->bhde', kd, vv)
        return state, out

    state0 = jnp.zeros((B_, RET_HEADS, RET_DK, RET_DV), jnp.float32)
    _, cross = lax.scan(step, state0, (jnp.moveaxis(q_dec, 2, 0), jnp.moveaxis(k_dec, 2, 0),
                                       jnp.moveaxis(vc, 2, 0)))
    o = intra + jnp.moveaxis(cross, 0, 2)
    o = o.reshape(B_, RET_HEADS, S_, RET_DV)
    o = o * lax.rsqrt(jnp.mean(o * o, axis=-1, keepdims=True) + EPS)
    o = o.transpose(0, 2, 1, 3).reshape(B_, S_, RET_V)
    y = jax.nn.silu(g.astype(jnp.float32)) * o
    return y.astype(h.dtype) @ w_out

def _stick_breaking(h, w_in, w_out):
    B_, S_, _ = h.shape
    nb = S_ // BLOCK
    scale = 1.0 / math.sqrt(SB_DH)
    proj = h @ w_in
    q, k, v = jnp.split(proj, 3, axis=-1)
    to_heads = lambda a: a.reshape(B_, S_, SB_HEADS, SB_DH).transpose(0, 2, 1, 3).astype(jnp.float32)
    q, k, v = to_heads(q), to_heads(k), to_heads(v)
    outs = []
    for i in range(nb):
        qb = q[:, :, i * BLOCK:(i + 1) * BLOCK]
        t_pos = i * BLOCK + jnp.arange(BLOCK)
        kp = jnp.moveaxis(k[:, :, :(i + 1) * BLOCK].reshape(B_, SB_HEADS, i + 1, BLOCK, SB_DH), 2, 0)
        vp = jnp.moveaxis(v[:, :, :(i + 1) * BLOCK].reshape(B_, SB_HEADS, i + 1, BLOCK, SB_DH), 2, 0)

        def step(carry, xs, qb=qb, t_pos=t_pos):
            suffix, acc = carry
            kb, vb, j = xs
            z = jnp.einsum('bhqd,bhkd->bhqk', qb, kb) * scale
            s_pos = j * BLOCK + jnp.arange(BLOCK)
            mask = s_pos[None, :] < t_pos[:, None]
            log1m = jnp.where(mask, jax.nn.log_sigmoid(-z), 0.0)
            excl = lax.cumsum(log1m, axis=3, reverse=True) - log1m
            log_a = jax.nn.log_sigmoid(z) + excl + suffix[..., None]
            a = jnp.where(mask, jnp.exp(log_a), 0.0)
            acc = acc + jnp.einsum('bhqk,bhkd->bhqd', a, vb)
            suffix = suffix + jnp.sum(log1m, axis=3)
            return (suffix, acc), None

        init = (jnp.zeros((B_, SB_HEADS, BLOCK), jnp.float32),
                jnp.zeros((B_, SB_HEADS, BLOCK, SB_DH), jnp.float32))
        (_, acc), _ = lax.scan(step, init, (kp, vp, jnp.arange(i + 1)), reverse=True)
        outs.append(acc)
    o = jnp.concatenate(outs, axis=2)
    o = o.transpose(0, 2, 1, 3).reshape(B_, S_, SB_HEADS * SB_DH)
    return o.astype(h.dtype) @ w_out

def _conv_ffn(h, w_up, conv_w, conv_b, w_down):
    u = h @ w_up
    u = lax.conv_general_dilated(u, conv_w[:, None, :].astype(u.dtype), window_strides=(1,),
                                 padding=[(CONV_W - 1, 0)],
                                 dimension_numbers=('NWC', 'WIO', 'NWC'),
                                 feature_group_count=2 * D_FF) + conv_b
    gate, val = jnp.split(u, 2, axis=-1)
    return (jax.nn.silu(gate) * val) @ w_down

def first_inputs(seed: int = 0) -> dict:
    key = jax.random.key(seed)
    ks = jax.random.split(key, 16)
    n_ret = (DEPTH + 1) // 2
    n_sb = DEPTH // 2
    nrm = lambda k, shape, fan_in: jax.random.normal(k, shape, jnp.float32) * fan_in ** -0.5
    gain = lambda k, shape: 1.0 + 0.02 * jax.random.normal(k, shape, jnp.float32)
    return {
        "x": jax.random.normal(ks[0], (BATCH, SEQ, D_MODEL), jnp.float32),
        "ret_norm": gain(ks[1], (n_ret, D_MODEL)),
        "ret_w_in": nrm(ks[2], (n_ret, D_MODEL, RET_IN), D_MODEL),
        "ret_w_out": nrm(ks[3], (n_ret, RET_V, D_MODEL), RET_V),
        "sb_norm": gain(ks[4], (n_sb, D_MODEL)),
        "sb_w_in": nrm(ks[5], (n_sb, D_MODEL, SB_IN), D_MODEL),
        "sb_w_out": nrm(ks[6], (n_sb, SB_HEADS * SB_DH, D_MODEL), SB_HEADS * SB_DH),
        "ffn_norm": gain(ks[7], (DEPTH, D_MODEL)),
        "ffn_w_up": nrm(ks[8], (DEPTH, D_MODEL, 2 * D_FF), D_MODEL),
        "ffn_conv_w": nrm(ks[9], (DEPTH, CONV_W, 2 * D_FF), CONV_W),
        "ffn_conv_b": 0.02 * jax.random.normal(ks[10], (DEPTH, 2 * D_FF), jnp.float32),
        "ffn_w_down": nrm(ks[11], (DEPTH, D_FF, D_MODEL), D_FF),
        "final_norm": gain(ks[12], (D_MODEL,)),
    }

def first_block(x, ret_norm, ret_w_in, ret_w_out, sb_norm, sb_w_in, sb_w_out,
              ffn_norm, ffn_w_up, ffn_conv_w, ffn_conv_b, ffn_w_down, final_norm):
    for i in range(DEPTH):
        j = i // N_MIXERS
        if i % N_MIXERS == 0:
            x = x + _retention(_rmsnorm(x, ret_norm[j]), ret_w_in[j], ret_w_out[j])
        else:
            x = x + _stick_breaking(_rmsnorm(x, sb_norm[j]), sb_w_in[j], sb_w_out[j])
        x = x + _conv_ffn(_rmsnorm(x, ffn_norm[i]), ffn_w_up[i], ffn_conv_w[i],
                          ffn_conv_b[i], ffn_w_down[i])
    return _rmsnorm(x, final_norm)


DEPTH_2 = 1

D_MIX = D_MODEL
D_MLSTM = D_MIX // 2
D_MOBA = D_MIX - D_MLSTM
MLSTM_HEADS = 4
MLSTM_HEAD_DIM = D_MLSTM // MLSTM_HEADS
MLSTM_CHUNK = 64
CONV_WIDTH = 4
MOBA_HEADS = 8
MOBA_HEAD_DIM = D_MOBA // MOBA_HEADS
MOBA_BLOCK = 256
MOBA_TOPK = 3
MOBA_Q_CHUNK = 32
N_GROUPS = 4
EXPERTS_PER_GROUP = 8
N_EXPERTS = N_GROUPS * EXPERTS_PER_GROUP
EXPERT_TOPK = 2
D_EXPERT = 512
MOE_ROW_BLOCK = 256
IN_COLS = 4 * D_MLSTM + 2 * MLSTM_HEADS + 3 * D_MOBA


def rms_norm(x, g):
    xf = x.astype(jnp.float32)
    y = xf * lax.rsqrt(jnp.mean(xf * xf, axis=-1, keepdims=True) + EPS)
    return (y * g.astype(jnp.float32)).astype(x.dtype)

def split_heads(a, n_heads):
    b, s, _ = a.shape
    return a.reshape(b, s, n_heads, -1).transpose(0, 2, 1, 3)

def merge_heads(a):
    b, h, s, d = a.shape
    return a.transpose(0, 2, 1, 3).reshape(b, s, h * d)

def causal_depthwise_conv(x, w, b):
    s = x.shape[1]
    xp = jnp.pad(x, ((0, 0), (CONV_WIDTH - 1, 0), (0, 0)))
    y = b
    for j in range(CONV_WIDTH):
        y = y + w[j] * xp[:, j:j + s]
    return y

def mlstm_chunkwise(q, k, v, i_pre, f_pre):
    b, h, s, d = q.shape
    dv = v.shape[-1]
    nc = s // MLSTM_CHUNK
    out_dtype = v.dtype
    qf = q.astype(jnp.float32) * (d ** -0.5)
    kf = k.astype(jnp.float32)
    vf = v.astype(jnp.float32)
    log_i = i_pre.astype(jnp.float32)
    log_f = jax.nn.log_sigmoid(f_pre.astype(jnp.float32))

    def to_chunks(a):
        a = a.reshape(b, h, nc, MLSTM_CHUNK, *a.shape[3:])
        return jnp.moveaxis(a, 2, 0)

    causal = jnp.tril(jnp.ones((MLSTM_CHUNK, MLSTM_CHUNK), dtype=bool))

    def step(carry, inp):
        C, n, m = carry
        qt, kt, vt, it, ft = inp
        cum_f = jnp.cumsum(ft, axis=-1)
        cum_last = cum_f[..., -1]
        dmat = cum_f[..., :, None] - cum_f[..., None, :] + it[..., None, :]
        dmat = jnp.where(causal, dmat, -jnp.inf)
        inter = cum_f + m[..., None]
        m_t = jnp.maximum(inter, jnp.max(dmat, axis=-1))
        w_inter = jnp.exp(inter - m_t)
        sc = jnp.einsum('bhtd,bhsd->bhts', qt, kt) * jnp.exp(dmat - m_t[..., None])
        num = w_inter[..., None] * jnp.einsum('bhtd,bhde->bhte', qt, C) + jnp.einsum('bhts,bhse->bhte', sc, vt)
        den = w_inter * jnp.einsum('bhtd,bhd->bht', qt, n) + jnp.sum(sc, axis=-1)
        h_t = num / jnp.maximum(jnp.abs(den), jnp.exp(-m_t))[..., None]
        g_end = cum_last[..., None] - cum_f + it
        m_new = jnp.maximum(cum_last + m, jnp.max(g_end, axis=-1))
        w_old = jnp.exp(cum_last + m - m_new)
        w_new = jnp.exp(g_end - m_new[..., None])
        C_new = w_old[..., None, None] * C + jnp.einsum('bhs,bhsd,bhse->bhde', w_new, kt, vt)
        n_new = w_old[..., None] * n + jnp.einsum('bhs,bhsd->bhd', w_new, kt)
        return (C_new, n_new, m_new), h_t

    init = (jnp.zeros((b, h, d, dv), jnp.float32), jnp.zeros((b, h, d), jnp.float32),
            jnp.zeros((b, h), jnp.float32))
    _, hs = lax.scan(step, init, (to_chunks(qf), to_chunks(kf), to_chunks(vf),
                                  to_chunks(log_i), to_chunks(log_f)))
    return jnp.moveaxis(hs, 0, 2).reshape(b, h, s, dv).astype(out_dtype)

def moba_attention(q, k, v):
    b, h, s, d = q.shape
    nb = -(-s // MOBA_BLOCK)
    pad = nb * MOBA_BLOCK - s
    kp = jnp.pad(k.astype(jnp.float32), ((0, 0), (0, 0), (0, pad), (0, 0)))
    vp = jnp.pad(v.astype(jnp.float32), ((0, 0), (0, 0), (0, pad), (0, 0)))
    kb = kp.reshape(b, h, nb, MOBA_BLOCK, d)
    vb = vp.reshape(b, h, nb, MOBA_BLOCK, d)
    k_mean = jnp.mean(kb, axis=3)
    scale = d ** -0.5
    n_sel = min(MOBA_TOPK, nb - 1)
    bi = jnp.arange(b)[:, None, None, None]
    hi = jnp.arange(h)[None, :, None, None]
    blk_ids = jnp.arange(nb)

    def chunk(ci):
        t0 = ci * MOBA_Q_CHUNK
        qc = lax.dynamic_slice_in_dim(q, t0, MOBA_Q_CHUNK, axis=2).astype(jnp.float32)
        q_pos = t0 + jnp.arange(MOBA_Q_CHUNK)
        own = t0 // MOBA_BLOCK
        k_own = lax.dynamic_index_in_dim(kb, own, axis=2, keepdims=False)
        v_own = lax.dynamic_index_in_dim(vb, own, axis=2, keepdims=False)
        own_pos = own * MOBA_BLOCK + jnp.arange(MOBA_BLOCK)
        s_own = jnp.einsum('bhqd,bhkd->bhqk', qc, k_own) * scale
        s_own = jnp.where(own_pos[None, :] <= q_pos[:, None], s_own, -jnp.inf)
        if n_sel > 0:
            gate = jnp.einsum('bhqd,bhnd->bhqn', qc, k_mean)
            gate = jnp.where(blk_ids < own, gate, -jnp.inf)
            _, sel = lax.top_k(gate, n_sel)
            valid = sel < own
            k_sel = kb[bi, hi, sel]
            v_sel = vb[bi, hi, sel]
            s_sel = jnp.einsum('bhqd,bhqskd->bhqsk', qc, k_sel) * scale
            s_sel = jnp.where(valid[..., None], s_sel, -jnp.inf)
            p = jax.nn.softmax(jnp.concatenate(
                [s_sel.reshape(b, h, MOBA_Q_CHUNK, n_sel * MOBA_BLOCK), s_own], axis=-1), axis=-1)
            p_sel = p[..., :n_sel * MOBA_BLOCK].reshape(b, h, MOBA_Q_CHUNK, n_sel, MOBA_BLOCK)
            p_own = p[..., n_sel * MOBA_BLOCK:]
            return (jnp.einsum('bhqsk,bhqskd->bhqd', p_sel, v_sel)
                    + jnp.einsum('bhqk,bhkd->bhqd', p_own, v_own))
        p_own = jax.nn.softmax(s_own, axis=-1)
        return jnp.einsum('bhqk,bhkd->bhqd', p_own, v_own)

    outs = lax.map(chunk, jnp.arange(s // MOBA_Q_CHUNK))
    return jnp.moveaxis(outs, 0, 2).reshape(b, h, s, d).astype(q.dtype)

def hierarchical_moe(hx, w_rg, b_rg, w_re, b_re, w_gate, w_up, w_down):
    b, s, dm = hx.shape
    t = b * s
    xt = hx.reshape(t, dm)
    g_prob = jax.nn.softmax((xt @ w_rg).astype(jnp.float32) + b_rg, axis=-1)
    g_w, g_idx = lax.top_k(g_prob, 1)
    e_logits = ((xt @ w_re).astype(jnp.float32) + b_re).reshape(t, N_GROUPS, EXPERTS_PER_GROUP)
    e_logits = jnp.take_along_axis(e_logits, g_idx[:, :, None], axis=1)[:, 0]
    e_top, e_loc = lax.top_k(e_logits, EXPERT_TOPK)
    e_w = jax.nn.softmax(e_top, axis=-1) * g_w
    e_id = g_idx * EXPERTS_PER_GROUP + e_loc

    n_assign = t * EXPERT_TOPK
    flat_e = e_id.reshape(n_assign)
    flat_tok = jnp.repeat(jnp.arange(t), EXPERT_TOPK)
    flat_w = e_w.reshape(n_assign)
    order = jnp.argsort(flat_e)
    se, stok, sw = flat_e[order], flat_tok[order], flat_w[order]
    counts = jnp.zeros((N_EXPERTS,), jnp.int32).at[flat_e].add(1)
    starts = jnp.cumsum(counts) - counts
    padded = (counts + MOE_ROW_BLOCK - 1) // MOE_ROW_BLOCK * MOE_ROW_BLOCK
    pad_ends = jnp.cumsum(padded)
    pad_starts = pad_ends - padded
    dest = pad_starts[se] + (jnp.arange(n_assign) - starts[se])
    n_blocks = -(-n_assign // MOE_ROW_BLOCK) + N_EXPERTS
    rows = n_blocks * MOE_ROW_BLOCK
    x_pad = jnp.zeros((rows, dm), hx.dtype).at[dest].set(xt[stok])
    blk_expert = jnp.minimum(
        jnp.searchsorted(pad_ends, jnp.arange(n_blocks) * MOE_ROW_BLOCK, side='right'), N_EXPERTS - 1)

    def run_block(args):
        xb, e = args
        return (jax.nn.silu(xb @ w_gate[e]) * (xb @ w_up[e])) @ w_down[e]

    y_pad = lax.map(run_block, (x_pad.reshape(n_blocks, MOE_ROW_BLOCK, dm), blk_expert))
    y_sorted = y_pad.reshape(rows, dm)[dest].astype(jnp.float32)
    out = jnp.zeros((t, dm), jnp.float32).at[stok].add(y_sorted * sw[:, None])
    return out.reshape(b, s, dm).astype(hx.dtype)

def second_inputs(seed: int = 0) -> dict:
    key = jax.random.key(seed)
    ks = jax.random.split(key, 24)
    f32 = jnp.float32

    def nrm(k, shape, sc):
        return sc * jax.random.normal(k, shape, f32)

    L = DEPTH_2
    x = nrm(ks[0], (BATCH, SEQ, D_MODEL), 1.0)
    c = nrm(ks[1], (BATCH, D_MODEL), 1.0)
    w_ada = nrm(ks[2], (L, D_MODEL, 6 * D_MODEL), 0.5 * D_MODEL ** -0.5)
    b_ada = nrm(ks[3], (L, 6 * D_MODEL), 0.02)
    g_norm1 = 1.0 + nrm(ks[4], (L, D_MODEL), 0.02)
    w_in = nrm(ks[5], (L, D_MODEL, IN_COLS), D_MODEL ** -0.5)
    w_conv = nrm(ks[6], (L, CONV_WIDTH, 2 * D_MLSTM), CONV_WIDTH ** -0.5)
    b_conv = nrm(ks[7], (L, 2 * D_MLSTM), 0.02)
    b_i = nrm(ks[8], (L, MLSTM_HEADS), 0.1)
    b_f = jnp.linspace(3.0, 6.0, MLSTM_HEADS, dtype=f32) + nrm(ks[9], (L, MLSTM_HEADS), 0.1)
    b_gates = jnp.concatenate([b_i, b_f], axis=-1)
    g_mlstm_head = 1.0 + nrm(ks[10], (L, D_MLSTM), 0.02)
    w_out = nrm(ks[11], (L, D_MIX, D_MODEL), D_MIX ** -0.5)
    g_norm2 = 1.0 + nrm(ks[12], (L, D_MODEL), 0.02)
    w_router_group = nrm(ks[13], (L, D_MODEL, N_GROUPS), D_MODEL ** -0.5)
    b_router_group = nrm(ks[14], (L, N_GROUPS), 0.01)
    w_router_expert = nrm(ks[15], (L, D_MODEL, N_EXPERTS), D_MODEL ** -0.5)
    b_router_expert = nrm(ks[16], (L, N_EXPERTS), 0.01)
    w_expert_gate = nrm(ks[17], (L, N_EXPERTS, D_MODEL, D_EXPERT), D_MODEL ** -0.5)
    w_expert_up = nrm(ks[18], (L, N_EXPERTS, D_MODEL, D_EXPERT), D_MODEL ** -0.5)
    w_expert_down = nrm(ks[19], (L, N_EXPERTS, D_EXPERT, D_MODEL), D_EXPERT ** -0.5)
    g_final = 1.0 + nrm(ks[20], (D_MODEL,), 0.02)
    return {'x': x, 'c': c, 'w_ada': w_ada, 'b_ada': b_ada, 'g_norm1': g_norm1, 'w_in': w_in,
            'w_conv': w_conv, 'b_conv': b_conv, 'b_gates': b_gates, 'g_mlstm_head': g_mlstm_head,
            'w_out': w_out, 'g_norm2': g_norm2, 'w_router_group': w_router_group,
            'b_router_group': b_router_group, 'w_router_expert': w_router_expert,
            'b_router_expert': b_router_expert, 'w_expert_gate': w_expert_gate,
            'w_expert_up': w_expert_up, 'w_expert_down': w_expert_down, 'g_final': g_final}

def second_block(x, c, w_ada, b_ada, g_norm1, w_in, w_conv, b_conv, b_gates, g_mlstm_head,
              w_out, g_norm2, w_router_group, b_router_group, w_router_expert,
              b_router_expert, w_expert_gate, w_expert_up, w_expert_down, g_final):
    split_at = np.cumsum([D_MLSTM, D_MLSTM, D_MLSTM, D_MLSTM, 2 * MLSTM_HEADS, D_MOBA, D_MOBA]).tolist()
    for l in range(DEPTH_2):
        mod = jax.nn.silu(c) @ w_ada[l] + b_ada[l]
        shift1, scale1, gate1, shift2, scale2, gate2 = [m[:, None, :] for m in jnp.split(mod, 6, axis=-1)]

        hn = rms_norm(x, g_norm1[l]) * (1.0 + scale1) + shift1
        proj = hn @ w_in[l]
        q_m, k_m, v_m, o_m, gates, q_a, k_a, v_a = jnp.split(proj, split_at, axis=-1)

        qk = jax.nn.silu(causal_depthwise_conv(jnp.concatenate([q_m, k_m], axis=-1), w_conv[l], b_conv[l]))
        q_m, k_m = jnp.split(qk, 2, axis=-1)
        gates = gates + b_gates[l]
        i_pre = gates[..., :MLSTM_HEADS].transpose(0, 2, 1)
        f_pre = gates[..., MLSTM_HEADS:].transpose(0, 2, 1)
        h_m = mlstm_chunkwise(split_heads(q_m, MLSTM_HEADS), split_heads(k_m, MLSTM_HEADS),
                              split_heads(v_m, MLSTM_HEADS), i_pre, f_pre)
        h_m = rms_norm(h_m, g_mlstm_head[l].reshape(MLSTM_HEADS, 1, MLSTM_HEAD_DIM))
        h_m = merge_heads(h_m) * jax.nn.sigmoid(o_m)

        h_a = merge_heads(moba_attention(split_heads(q_a, MOBA_HEADS), split_heads(k_a, MOBA_HEADS),
                                         split_heads(v_a, MOBA_HEADS)))

        mix = jnp.concatenate([h_m, h_a], axis=-1) @ w_out[l]
        x = x + gate1 * mix

        hn2 = rms_norm(x, g_norm2[l]) * (1.0 + scale2) + shift2
        ffn = hierarchical_moe(hn2, w_router_group[l], b_router_group[l], w_router_expert[l],
                               b_router_expert[l], w_expert_gate[l], w_expert_up[l], w_expert_down[l])
        x = x + gate2 * ffn
    return rms_norm(x, g_final)


def setup_inputs(seed=0):
    out = dict(first_inputs(seed))
    for name, value in second_inputs(seed + 1).items():
        if name != "x":
            out[name + "_2"] = value
    return out


def reference(
    x, ret_norm, ret_w_in, ret_w_out, sb_norm, sb_w_in, sb_w_out, ffn_norm, ffn_w_up,
    ffn_conv_w, ffn_conv_b, ffn_w_down, final_norm, c_2, w_ada_2, b_ada_2, g_norm1_2, w_in_2,
    w_conv_2, b_conv_2, b_gates_2, g_mlstm_head_2, w_out_2, g_norm2_2, w_router_group_2,
    b_router_group_2, w_router_expert_2, b_router_expert_2, w_expert_gate_2, w_expert_up_2,
    w_expert_down_2, g_final_2,
):
    x = first_block(
        x, ret_norm, ret_w_in, ret_w_out, sb_norm, sb_w_in, sb_w_out, ffn_norm, ffn_w_up,
        ffn_conv_w, ffn_conv_b, ffn_w_down, final_norm,
    )
    return second_block(
        x, c_2, w_ada_2, b_ada_2, g_norm1_2, w_in_2, w_conv_2, b_conv_2, b_gates_2,
        g_mlstm_head_2, w_out_2, g_norm2_2, w_router_group_2, b_router_group_2,
        w_router_expert_2, b_router_expert_2, w_expert_gate_2, w_expert_up_2, w_expert_down_2,
        g_final_2,
    )


_drawn_inputs = setup_inputs


def setup_inputs(seed=0):
    import zlib

    import numpy as np

    out = dict(_drawn_inputs(seed))
    spreads = {}
    factors = {'sb_norm': 3.939,
     'b_ada_2': 3.206,
     'g_norm1_2': 8.0,
     'b_conv_2': 128.002,
     'g_mlstm_head_2': 8.0,
     'g_norm2_2': 4.693,
     'b_router_group_2': 64.0,
     'b_router_expert_2': 8.0,
     'g_final_2': 20.82}
    for name, (base, spread) in spreads.items():
        noise = np.random.default_rng([zlib.crc32(name.encode()), seed]).standard_normal(out[name].shape)
        drawn = base * np.exp(spread * noise) if base else spread * noise
        out[name] = __import__('jax').numpy.asarray(drawn.astype(out[name].dtype))
    for name, factor in factors.items():
        out[name] = (out[name] * factor).astype(out[name].dtype)
    return out
```

```python
from contextlib import ExitStack

import numpy as np

import concourse.bass as bass
from concourse import mybir

P = 128
D = 1024
T = 256
NT = T // P
KD = D // P
C = 512
EPS = 1e-6
RH, RDK, RDV = 4, 256, 512
RV = RH * RDV
SH, SDH = 16, 64
FF = 2816
FP = FF // P
LH, LDH = 4, 128
MH, MDH = 8, 64
NE, NG, EPG = 32, 4, 8
DE = 512
KE = DE // P
R = 64
PASSES = T // R
PAIRS = NE // 2
TRI = 3 * P
NEG = -1e30

F32 = mybir.dt.float32
I32 = mybir.dt.int32
U32 = mybir.dt.uint32
ALU = mybir.AluOpType
ACT = mybir.ActivationFunctionType
AX = mybir.AxisListType.X

CONST = {}
_at = 0
for _name, _n in (("ident", P), ("ones", P), ("after", P), ("before", P), ("upto", P), ("future", TRI),
                  ("decay", RH * TRI), ("cos", 2 * T), ("sin", 2 * T), ("iota", T)):
    CONST[_name] = (_at, _at + _n)
    _at += _n
NCONST = _at

SMALL = {}
_at = 0
for _name, _n in (("ret_norm", KD), ("sb_norm", KD), ("ffn_norm", 2 * KD), ("g1", KD), ("g2", KD), ("c", KD),
                  ("b_ada", 6 * KD), ("conv_w", 2 * 2 * FP * 3), ("conv_b", 2 * 2 * FP),
                  ("conv2_w", 2 * LH * 4), ("conv2_b", 2 * LH)):
    SMALL[_name] = (_at, _at + _n)
    _at += _n
NSMALL = _at


def shape_constants():
    i = np.arange(P)
    s, t = i[:, None], i[None, :]
    out = np.zeros((P, NCONST), np.float32)

    def put(name, value):
        a, b = CONST[name]
        out[:, a:b] = value.reshape(P, b - a)

    put("ident", np.eye(P))
    put("ones", np.ones((P, P)))
    put("after", (s > t))
    put("before", (s < t))
    put("upto", (s <= t))
    put("future", np.concatenate([np.where(t > s, NEG, 0.0), np.zeros((P, P)), np.where(t > s, NEG, 0.0)], 1))
    decay = np.zeros((P, RH, TRI))
    for h in range(RH):
        log_g = np.log(1.0 - 2.0 ** (-5.0 - h))
        diag = np.where(s <= t, np.exp((t - s) * log_g), 0.0)
        decay[:, h] = np.concatenate([diag, np.exp((t - s + P) * log_g), diag], 1) * RDK ** -0.5
    put("decay", decay)
    freq = np.float32(10000.0) ** (-np.arange(0, RDK, 2, dtype=np.float32) / np.float32(RDK))
    ang = (freq.astype(np.float32)[:, None] * np.arange(T, dtype=np.float32)[None, :]).astype(np.float64)
    put("cos", np.concatenate([np.cos(ang), np.cos(ang)], 1))
    put("sin", np.concatenate([-np.sin(ang), np.sin(ang)], 1))
    put("iota", np.broadcast_to(np.arange(T), (P, T)))
    return out


def weight_plan(A):
    rows = lambda w: w.rearrange("(k p) n -> p k n", p=P)
    units = []

    def wide(phase, slot, w, c0):
        units.append((phase, slot, [((0, KD), (0, C), rows(w)[:, :, c0:c0 + C])]))

    def down(phase, slot, w, k0, n):
        units.append((phase, slot, [(None, n, rows(w)[:, k0:k0 + n, :])]))

    def ffn_up(l, slots, last):
        w = rows(A["ffn_w_up"][l])
        for u in range(FP // 2):
            s = slots[u % 2]
            units.append((f"up{l}", s, [((0, KD), (0, T), w[:, :, u * T:(u + 1) * T]),
                                        ((0, KD), (T, C), w[:, :, FF + u * T:FF + (u + 1) * T])]))

    def ffn_down(l, slots):
        for u, s in enumerate(slots):
            down(f"down{l}", s, A["ffn_w_down"][l], 4 * u, min(4, FP - 4 * u))

    for u in range(4):
        wide("ret_qk", u % 2, A["ret_w_in"][0], u * C)
    for u in range(8):
        wide("ret_vg", 2 + u % 2, A["ret_w_in"][0], (4 + u) * C)
    for u, s in enumerate((4, 5, 0, 1)):
        down("ret_out", s, A["ret_w_out"][0], 4 * u, 4)
    ffn_up(0, (2, 3), 2)
    ffn_down(0, (4, 5, 0, 1, 3, 2))
    for u in range(4):
        wide("sb_qk", (4, 5)[u % 2], A["sb_w_in"][0], u * C)
    for u, s in enumerate((0, 1)):
        wide("sb_v", s, A["sb_w_in"][0], (4 + u) * C)
    for u, s in enumerate((3, 2)):
        down("sb_out", s, A["sb_w_out"][0], 4 * u, 4)
    ffn_up(1, (4, 5), 4)
    ffn_down(1, (0, 1, 3, 2, 5, 4))
    gates = 4 * LH * LDH
    for c0, s in zip((0, C, gates + 8, gates + 8 + C, 2 * C, 3 * C, gates + 8 + 2 * C), (0, 1, 3, 2, 5, 4, 0)):
        wide("mix_in", s, A["w_in_2"][0], c0)
    for u, s in enumerate((1, 3)):
        down("mix_out", s, A["w_out_2"][0], 4 * u, 4)
    return units


class Link:

    def __init__(self, eng, sem):
        self.eng, self.sem, self.n, self.off = eng, sem, 0, None

    def __call__(self, ins):
        ins.then_inc(self.sem, 1)
        self.n += 1
        self.eng.wait_ge(self.sem, self.n if self.off is None else self.off + self.n)

    def enter(self, i, per):
        self.start, self.per, self.off = self.n, per, i * per

    def leave(self, trips):
        assert self.n - self.start == self.per, (self.n - self.start, self.per)
        self.n, self.off = self.start + trips * self.per, None


def build(nc, A, out):
    units = weight_plan(A)
    phases = {}
    for n, (phase, slot, _) in enumerate(units):
        phases.setdefault(phase, []).append(n)
    holder, before = [None] * 6, []
    for n, (_, slot, _) in enumerate(units):
        before.append(holder[slot])
        holder[slot] = n

    with ExitStack() as ctx:
        def sb(name, shape, dt=F32):
            return ctx.enter_context(nc.sbuf_tensor(name, shape, dt))

        names = set()

        def sem(name):
            assert name not in names
            names.add(name)
            return ctx.enter_context(nc.semaphore(name))

        ring = [sb(f"ring{s}", [P, KD * C]) for s in range(6)]
        wide = [r[:, :].rearrange("p (k n) -> p k n", k=KD) for r in ring]
        tall = [r[:, :].rearrange("p (k n) -> p k n", k=4) for r in ring]
        x = sb("x", [P, NT, D])
        xn = sb("xn", [P, NT, D])
        hT = sb("hT", [P, KD, T])
        const = sb("const", [P, NCONST])
        small = sb("small", [P, NSMALL])
        stat = sb("stat", [P, 64])
        credit = sb("credit", [P, 8])
        rowv = sb("rowv", [P, D])
        mods = sb("mods", [P, 4, KD])
        modr = sb("modr", [P, 4 * KD])
        gates = sb("gates", [P, 2, D])
        ARENA = 14912
        arena = sb("arena", [P, ARENA])

        def carve(start, *dims):
            n = int(np.prod(dims))
            assert start + n <= ARENA, (start, dims)
            v = arena[:, start:start + n]
            if len(dims) == 2:
                v = v.rearrange("p (a b) -> p a b", a=dims[0])
            if len(dims) == 3:
                v = v.rearrange("p (a b c) -> p a b c", a=dims[0], b=dims[1])
            return v

        ps = ctx.enter_context(nc.psum_tensor("ps", [P, 8, C], F32))

        def k_(name):
            a, b = CONST[name]
            return const[:, a:b]

        def s_(name):
            a, b = SMALL[name]
            return small[:, a:b]

        ident, ones, after, before_m, upto = (k_(n) for n in ("ident", "ones", "after", "before", "upto"))
        iota = k_("iota")

        ring_in = [sem(f"ring_in{s}") for s in range(6)]
        x_in, ident_in, const_in, small_in, row_in = sem("x_in"), sem("ident_in"), sem("const_in"), sem("small_in"), sem("row_in")
        out_done = sem("out_done")
        x_new = sem("x_new")
        dve_chain, act_chain, over_chain = sem("dve_chain"), sem("act_chain"), sem("over_chain")
        norm_ss, norm_ms, norm_sd, norm_xn = sem("norm_ss"), sem("norm_ms"), sem("norm_sd"), sem("norm_xn")
        norm_tr, norm_ha, norm_hv = sem("norm_tr"), sem("norm_ha"), sem("norm_hv")

        def update(k):
            return 4 * (k + 1)

        block = ctx.enter_context(nc.Block())

        b_ada = s_("b_ada")
        norm_src = [
            ((x_in, 16, 0), s_("ret_norm"), None),
            ((x_new, update(0), 2), s_("ffn_norm")[:, 0:KD], None),
            ((x_new, update(1), 2), s_("sb_norm"), None),
            ((x_new, update(2), 2), s_("ffn_norm")[:, KD:2 * KD], None),
            ((x_new, update(3), 2), None, None),
            ((x_new, update(3) + 2, 1), mods[:, 0, :], mods[:, 1, :]),
            ((x_new, update(4) + 2, 2), mods[:, 2, :], mods[:, 3, :]),
            ((x_new, update(5) + 2, 0), None, None),
        ]
        N_TR = [0, 1, 2, 3, None, 4, 5, None]

        def norm_act(act, r):
            s, whole, tile = norm_src[r][0]
            nc.scalar.activation(credit[:, 7:8], small[:, 0:1], ACT.Sqrt)
            for t in range(NT):
                act.wait_ge(s, whole if t else whole - tile)
                nc.scalar.activation(xn[:, t, :], x[:, t, :], ACT.Square,
                                     accum_out=stat[:, t:t + 1]).then_inc(norm_ss, 1)
            act.wait_ge(norm_ms, r + 1)
            nc.scalar.activation(stat[:, 4:6], stat[:, 2:4], ACT.Sqrt).then_inc(norm_sd, 1)

        def norm_dve(dve, link, r):
            dve.wait_ge(norm_ss, NT * (r + 1))
            nc.vector.tensor_scalar(stat[:, 2:4], stat[:, 0:2], 1.0 / D, EPS, ALU.mult, ALU.add)\
                .then_inc(norm_ms, 1)
            dve.wait_ge(norm_sd, r + 1)
            link(nc.vector.reciprocal(stat[:, 6:8], stat[:, 4:6]))
            if N_TR[r] is None:
                return
            for t in range(NT):
                nc.vector.tensor_scalar(xn[:, t, :], x[:, t, :], stat[:, 6 + t:7 + t], None, ALU.mult)\
                    .then_inc(norm_xn, 1)

        def norm_pe(pe, r):
            n = N_TR[r]
            pe.wait_ge(norm_xn, NT * (n + 1))
            for j in range(4):
                for k in (2 * j, 2 * j + 1):
                    for t in range(NT):
                        last = nc.tensor.transpose(ps[:, j, (k % 2) * T + t * P:(k % 2) * T + (t + 1) * P],
                                                   xn[:, t, k * P:(k + 1) * P], ident)
                last.then_inc(norm_tr, 1)

        def norm_evict(eng, r, which):
            n, (_, g, b) = N_TR[r], norm_src[r]
            for j in (which, which + 2):
                eng.wait_ge(norm_tr, 4 * n + j + 1)
                for k in (2 * j, 2 * j + 1):
                    src = ps[:, j, (k % 2) * T:(k % 2 + 1) * T]
                    if which == 0:
                        last = nc.scalar.activation(hT[:, k, :], src, ACT.Identity, scale=g[:, k:k + 1],
                                                    bias=0.0 if b is None else b[:, k:k + 1])
                    elif b is None:
                        last = nc.vector.tensor_scalar(hT[:, k, :], src, g[:, k:k + 1], None, ALU.mult)
                    else:
                        last = nc.vector.tensor_scalar(hT[:, k, :], src, g[:, k:k + 1], b[:, k:k + 1],
                                                       ALU.mult, ALU.add)
                last.then_inc(norm_hv if which else norm_ha, 1)

        def normed(pe, r):
            pe.wait_ge(norm_ha, 2 * (N_TR[r] + 1))
            pe.wait_ge(norm_hv, 2 * (N_TR[r] + 1))

        def arrivals(n):
            slot = units[n][1]
            return 16 * sum(len(units[m][2]) for m in range(n + 1) if units[m][1] == slot)

        last_fill = [arrivals(holder[s]) for s in range(6)]

        def arrived(pe, n):
            pe.wait_ge(ring_in[units[n][1]], arrivals(n))

        def arrived_pair(pe, phase, b, i):
            n = phases[phase][b]
            pe.wait_ge(ring_in[units[n][1]], i * (16 * len(units[n][2])) + arrivals(n))

        def by_feature(bank, slot, cols):
            for f, c0 in enumerate(cols):
                for k in range(KD):
                    last = nc.tensor.matmul(ps[:, bank, f * T:(f + 1) * T], wide[slot][:, k, c0:c0 + P],
                                            hT[:, k, :], start=(k == 0), stop=(k == KD - 1))
            return last

        def by_token(bank, slot, t):
            for k in range(KD):
                last = nc.tensor.matmul(ps[:, bank, :], hT[:, k, t * P:(t + 1) * P], wide[slot][:, k, :],
                                        start=(k == 0), stop=(k == KD - 1))
            return last

        def project(pe, phase, src, chunks, done):
            k = 0
            for i, n in enumerate(phases[phase]):
                arrived(pe, n)
                slot = units[n][1]
                for kc in range(min(4, chunks - k)):
                    for t in range(NT):
                        for half in range(2):
                            last = nc.tensor.matmul(ps[:, 4 + 2 * t + half, :], src[:, k, t * P:(t + 1) * P],
                                                    tall[slot][:, kc, half * C:(half + 1) * C],
                                                    start=(k == 0), stop=(k == chunks - 1))
                    k += 1
                last.then_inc(done, 1)

        def gated_residual(link, g, bank, tmp, signal):
            for t in range(NT):
                for half in range(2):
                    last = nc.vector.tensor_tensor(tmp[:, t, half * C:(half + 1) * C], ps[:, bank + 2 * t + half, :],
                                                   gates[:, g, half * C:(half + 1) * C], ALU.mult)
            link(last)
            for t in range(NT):
                ins = nc.vector.tensor_tensor(x[:, t, :], x[:, t, :], tmp[:, t, :], ALU.add)
                if signal:
                    ins.then_inc(x_new, 2)
            if not signal:
                link(ins)

        def residual(dve, done, n):
            dve.wait_ge(done, n)
            for t in range(NT):
                for half in range(2):
                    xs = x[:, t, half * C:(half + 1) * C]
                    nc.vector.tensor_tensor(xs, ps[:, 4 + 2 * t + half, :], xs, ALU.add).then_inc(x_new, 1)

        freed = {}

        def free_by(phase, s, per, base=0):
            for i, n in enumerate(phases[phase]):
                freed[n] = (s, base + per * (i + 1))

        qk = carve(0, 8, C)
        vg = carve(4096, NT, 2 * RV)
        yT = carve(0, 2 * KD, T)
        rot_a, rot_b = xn[:, 0, 0:C], xn[:, 0, C:2 * C]
        r_sc = carve(12288, 2, TRI)
        rqk_mm, rqk_free, rqk_out = sem("rqk_mm"), sem("rqk_free"), sem("rqk_out")
        rvg_mm, rvg_fa, rvg_fv = sem("rvg_mm"), sem("rvg_fa"), sem("rvg_fv")
        rg_silu = sem("rg_silu")
        r_s, r_d, r_o, r_sq, r_ms, r_sd, r_y, r_t, r_ta, r_tv, rout_mm = (
            sem("r_" + n) for n in ("scores", "decayed", "o", "squares", "means", "roots", "y", "turned",
                                    "yT_a", "yT_v", "out_mm"))
        free_by("ret_qk", rqk_mm, 2)
        free_by("ret_vg", rvg_mm, 2)
        free_by("ret_out", rout_mm, 1)

        hff = carve(0, FP, T)
        cv = carve(5632, 2, C)
        ada_w = [carve(6656, 4, C), gates[:, :, :].rearrange("p a (b n) -> p (a b) n", n=C)]
        ada_acc = carve(8704, 12 * C)
        up_mm, up_id, up_cv, up_free, up_si, up_h, down_mm = (
            sem("up_" + n) for n in ("mm", "identity", "convolved", "free", "silu", "h", "down_mm"))
        for l in range(2):
            free_by(f"up{l}", up_mm, 2, FP * l)
            free_by(f"down{l}", down_mm, 1, 6 * l)
        ada_in = [sem("ada_in0"), sem("ada_in1")]
        ada_used, ada_sum, ada_mods, ada_gate, ada_c, bias_in = (
            sem("ada_" + n) for n in ("used", "sum", "mods", "gate", "c", "bias_in"))

        sqk = carve(0, 8, C)
        sqk_t = sqk.rearrange("p a (b t) -> p (a b) t", b=2)
        sv = carve(4096, NT, D)
        z_b = [carve(6144 + 768 * i, 2, TRI) for i in range(2)]
        l_b = [carve(7680 + 768 * i, 2, TRI) for i in range(2)]
        sp_b = [carve(9216 + 768 * i, 2, TRI) for i in range(2)]
        a_b = [carve(10752 + 768 * i, 2, TRI) for i in range(2)]
        soT = carve(12288, KD, T)
        sqk_mm, sqk_fa, sqk_fv, sv_mm, sv_a, sv_v = (
            sem("s_" + n) for n in ("qk_mm", "qk_fa", "qk_fv", "v_mm", "v_a", "v_v"))
        s_z, s_zc, s_l, s_sp, s_m1, s_ex, s_la, s_a, s_m2, s_o, s_ot, sout_mm = (
            sem("s_" + n) for n in ("z", "zcopy", "log", "softplus", "masked", "excl", "log_a", "a", "a_masked",
                                    "o", "oT", "out_mm"))
        free_by("sb_qk", sqk_mm, 2)
        free_by("sb_v", sv_mm, 2)
        free_by("sb_out", sout_mm, 1)

        qkm = carve(0, 2 * LH, T)
        qka = carve(2048, 2 * MH // 2, T)
        vm = carve(4096, NT, LH * (LDH + 1))
        om = carve(5128, NT, C)
        va = carve(6152, NT, C)
        hm = carve(7176, NT, C)
        mixT = xn[:, :, :].rearrange("p a (b t) -> p (a b) t", t=T)
        cvm = carve(8200, 2, T)
        w8 = carve(8712, KD, 8)
        bg = carve(8776, 4)
        ghead = carve(8780, C)
        rows4 = carve(9292, 9, T)
        acol = carve(11596, NT, 4)
        fcol = carve(11604, NT, 4)
        sel4 = carve(11612, 4, P)
        wt = carve(12124, 2, TRI)
        pt = carve(12892, 2, TRI)
        m_sc = carve(13660, 2, TRI)
        mst = carve(14428, 128)
        mi_mm, mi_id, mi_cv, mi_si, mi_ev_a, mi_ev_v, mi_g = (
            sem("mi_" + n) for n in ("mm", "identity", "convolved", "silu", "ev_a", "ev_v", "gates"))
        mix_small = sem("mix_small")
        l_f, l_floor, l_ln, l_rows, l_tr, l_cols, l_sig = (
            sem("l_" + n) for n in ("forget", "floor", "ln", "rows", "turned", "cols", "sigmoid"))
        l_s, l_w, l_e, l_p, l_o, l_h, l_sq, l_ms, l_sd, l_hn, l_t, l_mt = (
            sem("l_" + n) for n in ("scores", "w", "expw", "p", "o", "h", "squares", "means", "roots", "hn",
                                    "hT", "mixT"))
        b_s, b_mx, b_e, b_p, b_t, b_tc, b_o, b_oc, mo_mm = (
            sem("b_" + n) for n in ("scores", "max", "exp", "p", "pT", "pT_copy", "o", "oT", "mo_mm"))
        free_by("mix_in", mi_mm, 2)
        free_by("mix_out", mo_mm, 1)

        EP = NE + 4
        wr = carve(0, KD, NG + NE)
        br = carve(288, NG + NE)
        lg = carve(324, NT, NG + NE)
        g8 = carve(396, NT, 8)
        m8 = carve(412, NT, 8)
        i8 = carve(428, NT, 8).bitcast(U32)
        f8 = carve(444, NT, 8)
        oh = carve(460, NT, NG)
        em = carve(476, NT, NE)
        oh1 = carve(540, NT, NE)
        oh2 = carve(604, NT, NE)
        asg = carve(668, NT, NE)
        wgt = carve(732, NT, EP)
        pos = carve(804, NT, EP)
        rst = carve(876, 64)
        flag = carve(940, 1).bitcast(I32)
        sel = carve(1024, NT, P)
        selw = carve(1280, NT, P)
        selT = carve(1536, T)
        gtmp = carve(4864, NT, D)
        xg = carve(1792, KD, P)
        hs = carve(2816, DE)
        hg = carve(3328, DE)
        hgT = carve(6912, KE, P)
        ye = carve(3840, D)
        r_in, t_lg, t_rank, t_flag, t_top, t_exp = (sem("t_" + n) for n in ("router_in", "logits", "rank", "flag", "top", "exp"))
        m_zero, m_start, m_s, m_sw, m_ga, m_xa, m_xv, m_gu, m_si, m_h, m_ht, m_hc, m_tr, m_sct, m_swt, m_dn, m_ya, m_yv = (
            sem("m_" + n) for n in ("zeroed", "started", "select", "select_w", "gathered", "xg_a", "xg_v", "gate_up",
                                    "silu", "h", "h_turned", "hT", "turned", "scattered", "selT", "down", "y_a", "y_v"))

        @block.sync
        def _(sp):
            sp.dma_start(x[:, :, :], A["x"][0].rearrange("(t p) d -> p t d", p=P)).then_inc(x_in, 16)
            sp.dma_start(const[:, 0:P], A["const"][:, 0:P]).then_inc(ident_in, 16)
            sp.dma_start(small[:, :], A["small"]).then_inc(small_in, 16)

            def fill(n):
                _, slot, parts = units[n]
                return [sp.dma_start(wide[slot][:, :, part[1][0]:part[1][1]] if part[0] is not None
                                     else tall[slot][:, 0:part[1], :], part[2]) for part in parts]

            for n in range(len(units)):
                if before[n] is not None:
                    sp.wait_ge(*freed[before[n]])
                if n == 1:
                    sp.dma_start(const[:, P:], A["const"][:, P:]).then_inc(const_in, 16)
                _, slot, parts = units[n]
                if len(parts) == 1:
                    fill(n)[0].then_inc(ring_in[slot], 16)
                else:
                    for half, d in enumerate(fill(n)):
                        d.then_inc(ring_in[slot], 16)

            def expert_unit(slot, e):
                name, shape = (("w_expert_gate_2", 0), ("w_expert_up_2", 0), ("w_expert_down_2", 1))[slot % 3]
                w = A[name][0]
                if shape:
                    src = w[bass.ds(e, 1)].rearrange("a (k p) n -> p (a k) n", p=P)
                    sp.dma_start(tall[slot][:, :, :], src).then_inc(ring_in[slot], 16)
                else:
                    src = w[bass.ds(e, 1)].rearrange("a (k p) n -> p (a k) n", p=P)
                    sp.dma_start(wide[slot][:, :, :], src).then_inc(ring_in[slot], 16)

            LOADS = (0, 3, 1, 4, 2, 5)

            def expert_pairs(r):
                def one(i, first):
                    for slot in LOADS:
                        if first:
                            sp.wait_ge(*freed[holder[slot]])
                        elif slot % 3 < 2:
                            sp.wait_ge(m_gu, i * 2 + (PAIRS * 2 * r - 1 + slot % 3))
                        else:
                            sp.wait_ge(m_dn, i + PAIRS * r)
                        expert_unit(slot, i * 2 + slot // 3)
                if r == 0:
                    one(0, True)
                with sp.Fori(1 if r == 0 else 0, PAIRS) as i:
                    one(i, False)

            expert_pairs(0)
            sp.wait_ge(t_flag, 1)
            most = sp.value_load(flag[0:1, 0:1])
            with sp.If(most > R):
                for r in range(1, PASSES):
                    expert_pairs(r)
            sp.wait_ge(x_new, update(5) + 4)
            sp.dma_start(out[0].rearrange("(t p) d -> p t d", p=P), x[:, :, :]).then_inc(out_done, 16)
            sp.wait_ge(out_done, 16)

        @block.gpsimd
        def _(pool):
            pool.dma_start(rowv[:, :], A["final_norm"].rearrange("(a d) -> a d", a=1).broadcast_to([P, D]))\
                .then_inc(row_in, 16)
            w_ada = A["w_ada_2"][0].rearrange("(p c) n -> p c n", p=P)
            with pool.Fori(0, 12) as nb:
                for kh in range(2):
                    pool.wait_ge(ada_used, nb * 2 + (kh + 1))
                    pool.dma_start(ada_w[kh], w_ada[:, 4 * kh:4 * kh + 4, bass.ds(nb * C, C)])\
                        .then_inc(ada_in[kh], 16)
            pool.wait_ge(ada_used, 2 + 24)
            for g, m in enumerate((2, 5)):
                pool.dma_start(gates[:, g, :], A["b_ada_2"][0:1, m * D:(m + 1) * D].broadcast_to([P, D]))\
                    .then_inc(bias_in, 16)

            def mask(buf, g, ready, done):
                pool.wait_ge(ready, g + 1)
                diag = buf[:, :, :].rearrange("p h (b t) -> p h b t", b=3)[:, :, 0:3:2, :]
                m = before_m.unsqueeze(1).unsqueeze(1).broadcast_to([P, 2, 2, P])
                nc.gpsimd.tensor_tensor(diag, diag, m, ALU.mult).then_inc(done, 1)

            pool.wait_ge(const_in, 16)
            for g in range(SH // 2):
                if g == 0:
                    mask(sp_b[0], 0, s_sp, s_m1)
                    mask(sp_b[1], 1, s_sp, s_m1)
                mask(a_b[g % 2], g, s_a, s_m2)
                if g + 2 < SH // 2:
                    mask(sp_b[g % 2], g + 2, s_sp, s_m1)

            pool.wait_ge(x_new, update(3))
            pool.dma_start(w8, A["w_in_2"][0].rearrange("(k p) n -> p k n", p=P)[:, :, 4 * LH * LDH:4 * LH * LDH + 8])\
                .then_inc(mix_small, 16)
            pool.dma_start(bg[0:LH, 0:1], A["b_gates_2"][0:1, 0:LH].rearrange("a h -> h a")).then_inc(mix_small, 16)
            pool.dma_start(bg[0:LH, 1:2], A["b_gates_2"][0:1, LH:2 * LH].rearrange("a h -> h a")).then_inc(mix_small, 16)
            pool.dma_start(ghead, A["g_mlstm_head_2"][0:1, :].broadcast_to([P, C])).then_inc(mix_small, 16)
            pool.dma_start(sel4[0:LH, :, :].rearrange("p a b -> p (a b)"), A["sel4"]).then_inc(mix_small, 16)
            pool.wait_ge(x_new, update(4) + 2)
            pool.dma_start(wr[:, :, 0:NG], A["w_router_group_2"][0].rearrange("(k p) n -> p k n", p=P)).then_inc(r_in, 16)
            pool.dma_start(wr[:, :, NG:], A["w_router_expert_2"][0].rearrange("(k p) n -> p k n", p=P)).then_inc(r_in, 16)
            pool.dma_start(br[:, 0:NG], A["b_router_group_2"][0:1, :].broadcast_to([P, NG])).then_inc(r_in, 16)
            pool.dma_start(br[:, NG:], A["b_router_expert_2"][0:1, :].broadcast_to([P, NE])).then_inc(r_in, 16)
            pool.dma_start(rowv[:, :], A["g_final_2"].rearrange("(a d) -> a d", a=1).broadcast_to([P, D]))\
                .then_inc(row_in, 16)

        @block.tensor
        def _(pe):
            pe.wait_ge(ident_in, 16)
            norm_pe(pe, 0)
            normed(pe, 0)

            with pe.Fori(0, 2) as i:
                for b in range(2):
                    arrived_pair(pe, "ret_qk", b, i)
                    for j in range(2):
                        pe.wait_ge(rqk_free, i * 4 + (2 * b + j + 1))
                        by_feature(2 * b + j, b, (2 * j * P, (2 * j + 1) * P)).then_inc(rqk_mm, 1)
            with pe.Fori(0, 4) as i:
                for b in range(2):
                    arrived_pair(pe, "ret_vg", b, i)
                    for t in range(NT):
                        pe.wait_ge(rvg_fv if t else rvg_fa, i * 2 + (b + 1))
                        by_token(2 * b + t + 4, 2 + b, t).then_inc(rvg_mm, 1)

            def ret_scores(h):
                if h >= 2:
                    pe.wait_ge(r_d, h - 1)
                for f in range(2):
                    nc.tensor.matmul(ps[:, h % 2, 0:T], qk[:, RH + h, f * T:f * T + P], qk[:, h, f * T:(f + 1) * T],
                                     start=(f == 0), stop=(f == 1))
                for f in range(2):
                    last = nc.tensor.matmul(ps[:, h % 2, T:TRI], qk[:, RH + h, f * T + P:(f + 1) * T],
                                            qk[:, h, f * T + P:(f + 1) * T], start=(f == 0), stop=(f == 1))
                last.then_inc(r_s, 1)

            def ret_out(h):
                pe.wait_ge(r_d, h + 1)
                if h >= 2:
                    pe.wait_ge(r_y, 2 * (h - 1))
                sc, v = r_sc[:, h % 2, :], vg[:, :, h * RDV:(h + 1) * RDV]
                ob = 2 + 2 * (h % 2)
                nc.tensor.matmul(ps[:, ob, :], sc[:, 0:P], v[:, 0, :], start=True, stop=True).then_inc(r_o, 1)
                nc.tensor.matmul(ps[:, ob + 1, :], sc[:, P:T], v[:, 0, :], start=True, stop=False)
                nc.tensor.matmul(ps[:, ob + 1, :], sc[:, T:TRI], v[:, 1, :], start=False, stop=True).then_inc(r_o, 1)

            def ret_turn(h):
                pe.wait_ge(r_y, 2 * (h + 1))
                for j in range(2):
                    if h >= 1:
                        pe.wait_ge(r_tv if j else r_ta, h)
                    for f in range(2):
                        for t in range(NT):
                            last = nc.tensor.transpose(
                                ps[:, 6 + j, f * T + t * P:f * T + (t + 1) * P],
                                vg[:, t, RV + h * RDV + (2 * j + f) * P:RV + h * RDV + (2 * j + f + 1) * P], ident)
                    last.then_inc(r_t, 1)

            pe.wait_ge(rqk_out, 8)
            ret_scores(0)
            ret_scores(1)
            pe.wait_ge(rvg_fa, 2 + 8)
            pe.wait_ge(rvg_fv, 2 + 8)
            for h in range(RH):
                ret_out(h)
                if h + 2 < RH:
                    ret_scores(h + 2)
                if h >= 1:
                    ret_turn(h - 1)
            ret_turn(RH - 1)
            pe.wait_ge(r_ta, RH)
            pe.wait_ge(r_tv, RH)
            project(pe, "ret_out", yT, 2 * KD, rout_mm)

            def ffn(l):
                normed(pe, 2 * l + 1)

                def unit(b, off):
                    for j in range(2):
                        pe.wait_ge(up_free, off + ((FP + 4) * l + 2 * b + j + 1))
                        slot = units[phases[f"up{l}"][b]][1]
                        by_feature(2 * b + j, slot, (j * P, T + j * P)).then_inc(up_mm, 1)

                with pe.Fori(0, 5) as i:
                    for b in range(2):
                        arrived_pair(pe, f"up{l}", b, i)
                        unit(b, i * 4)
                arrived(pe, phases[f"up{l}"][10])
                unit(0, 20)
                pe.wait_ge(up_h, FP * (l + 1))
                project(pe, f"down{l}", hff, FP, down_mm)

            norm_pe(pe, 1)
            ffn(0)

            pe.wait_ge(const_in, 16)
            pe.wait_ge(ada_sum, 1)
            pe.wait_ge(x_new, update(1))
            for m, q in enumerate((0, 1, 3, 4)):
                for k in range(KD):
                    last = nc.tensor.matmul(ps[:, 3, m * KD + k:m * KD + k + 1],
                                            ada_acc[:, q * D + k * P:q * D + (k + 1) * P], ones[:, 0:1],
                                            start=True, stop=True)
            last.then_inc(ada_mods, 1)
            for g, q in enumerate((2, 5)):
                for half in range(2):
                    last = nc.tensor.matmul(ps[:, 4 + 2 * g + half, :], ones,
                                            ada_acc[:, q * D + half * C:q * D + (half + 1) * C],
                                            start=True, stop=True)
            last.then_inc(ada_mods, 1)
            pe.wait_ge(ada_gate, 1)
            norm_pe(pe, 2)
            normed(pe, 2)

            with pe.Fori(0, 2) as i:
                for b in range(2):
                    arrived_pair(pe, "sb_qk", b, i)
                    for j in range(2):
                        pe.wait_ge(sqk_fv if j else sqk_fa, i * 2 + (b + 1))
                        by_feature(2 * b + j, 4 + b, (2 * j * P, (2 * j + 1) * P)).then_inc(sqk_mm, 1)
            for u, n in enumerate(phases["sb_v"]):
                arrived(pe, n)
                for t in range(NT):
                    if u == 0:
                        pe.wait_ge(ada_gate, 1 + 2 * (t + 1))
                    by_token(4 + 2 * u + t, units[n][1], t).then_inc(sv_mm, 1)

            def sb_z(g):
                if g == 0:
                    pe.wait_ge(sqk_fa, 2 + 4)
                    pe.wait_ge(sqk_fv, 2 + 4)
                if g >= 2:
                    pe.wait_ge(s_zc, g - 1)
                for hh in range(2):
                    rows = slice(hh * SDH, (hh + 1) * SDH)
                    q, k = sqk_t[rows, g, :], sqk_t[rows, KD + g, :]
                    bank = 2 * (g % 2) + hh
                    nc.tensor.matmul(ps[:, bank, 0:T], k[:, 0:P], q, start=True, stop=True)
                    last = nc.tensor.matmul(ps[:, bank, T:TRI], k[:, P:T], q[:, P:T], start=True, stop=True)
                last.then_inc(s_z, 1)

            def sb_excl(g):
                pe.wait_ge(s_m1, g + 1)
                if g == 0:
                    pe.wait_ge(sv_a, 2)
                    pe.wait_ge(sv_v, 2)
                else:
                    pe.wait_ge(s_la, g)
                for hh in range(2):
                    sp = sp_b[g % 2][:, hh, :]
                    nc.tensor.matmul(ps[:, 4 + hh, 0:T], after, sp[:, 0:T], start=True, stop=False)
                    nc.tensor.matmul(ps[:, 4 + hh, P:T], ones, sp[:, T:TRI], start=False, stop=True)
                    last = nc.tensor.matmul(ps[:, 4 + hh, T:TRI], after, sp[:, T:TRI], start=True, stop=True)
                last.then_inc(s_ex, 1)

            def sb_o(g):
                pe.wait_ge(s_m2, g + 1)
                if g >= 2:
                    pe.wait_ge(s_ot, g - 1)
                for hh in range(2):
                    h = 2 * g + hh
                    a = a_b[g % 2][:, hh, :]
                    o = ps[hh * SDH:(hh + 1) * SDH, 6 + g % 2, :]
                    nc.tensor.matmul(o[:, 0:T], sv[:, 0, h * SDH:(h + 1) * SDH], a[:, 0:T], start=True, stop=False)
                    last = nc.tensor.matmul(o[:, P:T], sv[:, 1, h * SDH:(h + 1) * SDH], a[:, T:TRI],
                                            start=False, stop=True)
                last.then_inc(s_o, 1)

            sb_z(0)
            sb_z(1)
            for g in range(SH // 2):
                sb_excl(g)
                if g >= 1:
                    sb_o(g - 1)
                if g + 2 < SH // 2:
                    sb_z(g + 2)
            sb_o(SH // 2 - 1)
            pe.wait_ge(s_ot, SH // 2)
            project(pe, "sb_out", soT, KD, sout_mm)

            norm_pe(pe, 3)
            ffn(1)

            norm_pe(pe, 5)
            normed(pe, 5)
            pe.wait_ge(mix_small, 80)
            for g in range(2):
                for k in range(KD):
                    last = nc.tensor.matmul(ps[0:LH, 4 + g, 0:T], w8[:, k, g * LH:(g + 1) * LH], hT[:, k, :],
                                            start=(k == 0), stop=(k == KD - 1))
            last.then_inc(mi_g, 1)
            for u, n in enumerate(phases["mix_in"]):
                arrived(pe, n)
                for j in range(2):
                    q = 2 * u + j
                    if 4 <= q < 8:
                        pe.wait_ge(mi_cv, q - 3)
                    if q >= 8:
                        pe.wait_ge(mi_ev_v if q % 2 else mi_ev_a, (q - 8) // 2 + 1)
                    if u < 4:
                        by_feature(q % 4, units[n][1], (2 * j * P, (2 * j + 1) * P)).then_inc(mi_mm, 1)
                    else:
                        by_token(q % 4, units[n][1], j).then_inc(mi_mm, 1)

            pe.wait_ge(l_rows, 1)
            for n, row in enumerate((4, 7)):
                for t in range(NT):
                    last = nc.tensor.transpose(ps[:, 6, (2 * n + t) * 4:(2 * n + t) * 4 + 4],
                                               rows4[0:LH, row, t * P:(t + 1) * P], ident[0:LH, 0:LH])
            last.then_inc(l_tr, 1)
            pe.wait_ge(mi_ev_a, 5)
            pe.wait_ge(mi_ev_v, 5)
            pe.wait_ge(mi_si, 4)

            def ls_scores(h):
                b = 3 * (h % 2)
                if h >= 2:
                    pe.wait_ge(l_p, h - 1)
                nc.tensor.matmul(ps[:, b, 0:T], sel4[0:LH, h, :], rows4[0:LH, 6, :], start=True, stop=True)
                nc.tensor.matmul(ps[:, b + 1, 0:T], qkm[:, LH + h, 0:P], qkm[:, h, :], start=True, stop=True)
                nc.tensor.matmul(ps[:, b + 1, T:TRI], qkm[:, LH + h, P:T], qkm[:, h, P:T], start=True, stop=True)\
                    .then_inc(l_s, 1)

            def ls_out(h):
                b = 3 * (h % 2) + 2
                pe.wait_ge(l_p, h + 1)
                if h >= 2:
                    pe.wait_ge(l_h, h - 1)
                v = vm.rearrange("p t (h e) -> p t h e", h=LH)
                E1 = LDH + 1
                nc.tensor.matmul(ps[:, b, 0:E1], pt[:, h % 2, 0:P], v[:, 0, h, :], start=True, stop=True)
                nc.tensor.matmul(ps[:, b, T:T + E1], pt[:, h % 2, P:T], v[:, 0, h, :], start=True, stop=False)
                nc.tensor.matmul(ps[:, b, T:T + E1], pt[:, h % 2, T:TRI], v[:, 1, h, :], start=False, stop=True)\
                    .then_inc(l_o, 1)

            ls_scores(0)
            ls_scores(1)
            for h in range(LH):
                ls_out(h)
                if h + 2 < LH:
                    ls_scores(h + 2)

            def mb_scores(h):
                if h == 0:
                    pe.wait_ge(l_cols, 1)
                if h >= 2:
                    pe.wait_ge(b_mx, h - 1)
                rows = slice((h % 2) * MDH, (h % 2 + 1) * MDH)
                q, k = qka[rows, h // 2, :], qka[rows, MH // 2 + h // 2, :]
                bank = 6 + h % 2
                nc.tensor.matmul(ps[:, bank, 0:P], q[:, 0:P], k[:, 0:P], start=True, stop=True)
                nc.tensor.matmul(ps[:, bank, P:TRI], q[:, P:T], k, start=True, stop=True).then_inc(b_s, 1)

            def mb_turn(h):
                pe.wait_ge(b_p, h + 1)
                if h >= 2:
                    pe.wait_ge(b_tc, h - 1)
                if h == 0:
                    pe.wait_ge(l_h, LH)
                sc = m_sc[:, h % 2, :]
                for blk in range(3):
                    last = nc.tensor.transpose(ps[:, h % 2, blk * P:(blk + 1) * P], sc[:, blk * P:(blk + 1) * P], ident)
                last.then_inc(b_t, 1)

            def mb_out(h):
                pe.wait_ge(b_tc, h + 1)
                if h >= 4 and h % 2 == 0:
                    pe.wait_ge(b_oc, h // 2 - 1)
                o = ps[(h % 2) * MDH:(h % 2 + 1) * MDH, 3 + (h // 2) % 2, :]
                p_ = wt[:, h % 2, :]
                cols = slice(h * MDH, (h + 1) * MDH)
                nc.tensor.matmul(o[:, 0:T], va[:, 0, cols], p_[:, 0:T], start=True, stop=False)
                nc.tensor.matmul(o[:, P:T], va[:, 1, cols], p_[:, T:TRI], start=False, stop=True).then_inc(b_o, 1)

            mb_scores(0)
            mb_scores(1)
            for h in range(MH):
                mb_turn(h)
                if h >= 1:
                    mb_out(h - 1)
                if h + 2 < MH:
                    mb_scores(h + 2)
            mb_out(MH - 1)

            pe.wait_ge(l_hn, 2 * LH)
            pe.wait_ge(b_tc, MH)
            for j in range(2):
                for f in range(2):
                    for t in range(NT):
                        last = nc.tensor.transpose(ps[:, j, f * T + t * P:f * T + (t + 1) * P],
                                                   hm[:, t, (2 * j + f) * P:(2 * j + f + 1) * P], ident)
                last.then_inc(l_t, 1)
            pe.wait_ge(l_mt, 2)
            pe.wait_ge(b_oc, MH // 2)
            project(pe, "mix_out", mixT, KD, mo_mm)

            norm_pe(pe, 6)
            normed(pe, 6)
            pe.wait_ge(r_in, 64)
            for t in range(NT):
                for k in range(KD):
                    last = nc.tensor.matmul(ps[:, 4, t * 64:t * 64 + NG + NE], hT[:, k, t * P:(t + 1) * P],
                                            wr[:, k, :], start=(k == 0), stop=(k == KD - 1))
            last.then_inc(t_lg, 1)
            pe.wait_ge(t_rank, 1)
            nc.tensor.matmul(ps[:, 5, 0:NE], before_m, asg[:, 0, :], start=True, stop=True)
            nc.tensor.matmul(ps[:, 5, 64:64 + NE], ones, asg[:, 0, :], start=True, stop=False)
            nc.tensor.matmul(ps[:, 5, 64:64 + NE], before_m, asg[:, 1, :], start=False, stop=True)
            nc.tensor.matmul(ps[:, 5, 128:128 + NE], ones, asg[:, 0, :], start=True, stop=False)
            nc.tensor.matmul(ps[:, 5, 128:128 + NE], ones, asg[:, 1, :], start=False, stop=True).then_inc(t_lg, 1)

            def gather(value, hgt):
                pe.wait_ge(m_s, value)
                for half in (1, 0):
                    if half == 0 and hgt is not None:
                        pe.wait_ge(m_hc, hgt)
                    for k in range(4 * half, 4 * half + 4):
                        for t in range(NT):
                            last = nc.tensor.matmul(ps[:, 4 + half, (k % 4) * P:(k % 4 + 1) * P],
                                                    xn[:, t, k * P:(k + 1) * P], sel[:, t, :],
                                                    start=(t == 0), stop=(t == NT - 1))
                    last.then_inc(m_ga, 1)

            def scatter(stop):
                for t in range(NT):
                    for half in range(2):
                        last = nc.tensor.matmul(ps[:, 2 * t + half, :], selT[:, t * P:(t + 1) * P],
                                                ye[:, half * C:(half + 1) * C], start=False, stop=stop,
                                                skip_group_check=True)
                last.then_inc(m_sct, 1)

            def expert_pass(r):
                pe.wait_ge(m_zero, 3 * (r + 1))
                for b in range(4):
                    last = nc.tensor.matmul(ps[:, b, :], selT[:, 0:P], ye[:, 0:C], start=True, stop=False,
                                            skip_group_check=True)
                last.then_inc(m_start, 1)
                gather((PAIRS + 2) * r + 1, None)
                with pe.Fori(0, PAIRS) as i:
                    pe.wait_ge(m_xa, i + ((PAIRS + 1) * r + 1))
                    pe.wait_ge(m_xv, i + ((PAIRS + 1) * r + 1))
                    for g in range(2):
                        for s in (g, 3 + g):
                            pe.wait_ge(ring_in[s], i * 16 + (last_fill[s] + 16 * (PAIRS * r + 1)))
                        for k in range(KD):
                            for e in range(2):
                                last = nc.tensor.matmul(ps[e * R:(e + 1) * R, 4 + g, :], xg[:, k, e * R:(e + 1) * R],
                                                        wide[3 * e + g][:, k, :], start=(k == 0), stop=(k == KD - 1))
                        last.then_inc(m_gu, 1)
                    pe.wait_ge(m_sw, i + ((PAIRS + 1) * r + 1))
                    pe.wait_ge(m_ya, i + ((PAIRS + 1) * r + 1))
                    for t in range(NT):
                        last = nc.tensor.transpose(ps[:, 6, t * P:(t + 1) * P], selw[:, t, :], ident)
                    last.then_inc(m_tr, 1)
                    pe.wait_ge(m_yv, i + ((PAIRS + 1) * r + 1))
                    scatter(False)
                    pe.wait_ge(m_h, i + (PAIRS * r + 1))
                    for k in range(KE):
                        last = nc.tensor.transpose(ps[:, 4, k * P:(k + 1) * P], hg[:, k * P:(k + 1) * P], ident)
                    last.then_inc(m_ht, 1)
                    gather(i + ((PAIRS + 2) * r + 2), i + (PAIRS * r + 1))
                    pe.wait_ge(m_swt, i + (PAIRS * r + 1))
                    for s in (2, 5):
                        pe.wait_ge(ring_in[s], i * 16 + (last_fill[s] + 16 * (PAIRS * r + 1)))
                    for half in range(2):
                        for k in range(KE):
                            for e in range(2):
                                last = nc.tensor.matmul(ps[e * R:(e + 1) * R, 6 + half, :],
                                                        hgT[:, k, e * R:(e + 1) * R],
                                                        tall[3 * e + 2][:, k, half * C:(half + 1) * C],
                                                        start=(k == 0), stop=(k == KE - 1))
                    last.then_inc(m_dn, 1)
                pe.wait_ge(m_ya, (PAIRS + 1) * (r + 1))
                pe.wait_ge(m_yv, (PAIRS + 1) * (r + 1))
                scatter(True)

            expert_pass(0)
            pe.wait_ge(t_flag, 1)
            most = pe.value_load(flag[0:1, 0:1])
            with pe.If(most > R):
                for r in range(1, PASSES):
                    expert_pass(r)

        @block.scalar
        def _(act):
            link = Link(act, act_chain)
            act.wait_ge(small_in, 16)
            norm_act(act, 0)
            norm_evict(act, 0, 0)
            nc.scalar.activation(credit[:, 3:4], small[:, 0:1], ACT.Copy).then_inc(rvg_fa, 2)
            with act.Fori(0, 4) as i:
                for b in range(2):
                    act.wait_ge(rvg_mm, i * 4 + (2 * b + 1))
                    nc.scalar.activation(vg[:, 0, bass.ds(i * 2 * C + b * C, C)], ps[:, 4 + 2 * b, :], ACT.Copy)\
                        .then_inc(rvg_fa, 1)
            act.wait_ge(rvg_fv, 2 + 8)
            act.wait_ge(rvg_fa, 2 + 8)
            for t in range(NT):
                nc.scalar.activation(vg[:, t, RV:2 * RV], vg[:, t, RV:2 * RV], ACT.Silu).then_inc(rg_silu, 1)
            nc.scalar.activation(stat[:, 16:24], s_("c"), ACT.Silu).then_inc(ada_c, 1)

            def ret_squares(h):
                for t in range(NT):
                    act.wait_ge(r_o, 2 * h + t + 1)
                    nc.scalar.activation(xn[:, 1, 0:C], ps[:, 2 + 2 * (h % 2) + t, :], ACT.Square,
                                         accum_out=stat[:, 8 + t:9 + t]).then_inc(r_sq, 1)
                    act.wait_ge(r_sq, 2 * h + t + 1)
                act.wait_ge(r_ms, h + 1)
                nc.scalar.activation(stat[:, 12:14], stat[:, 10:12], ACT.Sqrt).then_inc(r_sd, 1)

            def ret_copy(h):
                act.wait_ge(r_t, 2 * h + 1)
                nc.scalar.activation(yT[:, 4 * h:4 * h + 2, :].rearrange("p a b -> p (a b)"), ps[:, 6, :], ACT.Copy)\
                    .then_inc(r_ta, 1)

            for h in range(RH):
                ret_squares(h)
                if h >= 1:
                    ret_copy(h - 1)
            ret_copy(RH - 1)

            def ffn(l):
                def pair(b, j, off):
                    n = off + (2 * b + j)
                    w0, b0 = SMALL["conv_w"][0], SMALL["conv_b"][0]
                    act.wait_ge(up_mm, off + (FP * l + 2 * b + j + 1))
                    for gv in range(2):
                        at = (l * 2 + gv) * FP
                        last = nc.scalar.activation(
                            cv[:, j, gv * T:(gv + 1) * T], ps[:, 2 * b + j, gv * T:(gv + 1) * T], ACT.Identity,
                            scale=small[:, bass.ds(n * 3 + (w0 + at * 3 + 2), 1)],
                            bias=small[:, bass.ds(n + (b0 + at), 1)])
                    last.then_inc(up_id, 1)
                    act.wait_ge(up_cv, off + (FP * l + 2 * b + j + 1))
                    nc.scalar.activation(cv[:, j, 0:T], cv[:, j, 0:T], ACT.Silu).then_inc(up_si, 1)

                with act.Fori(0, 5) as i:
                    for b in range(2):
                        for j in range(2):
                            pair(b, j, i * 4)
                for j in range(2):
                    pair(0, j, 20)

            norm_act(act, 1)
            norm_evict(act, 1, 0)
            ffn(0)
            norm_act(act, 2)
            norm_evict(act, 2, 0)

            nc.scalar.activation(credit[:, 4:5], small[:, 0:1], ACT.Copy).then_inc(sqk_fa, 2)
            with act.Fori(0, 2) as i:
                for b in range(2):
                    act.wait_ge(sqk_mm, i * 4 + (2 * b + 1))
                    nc.scalar.activation(sqk[:, i * 4 + 2 * b, :], ps[:, 2 * b, :], ACT.Copy).then_inc(sqk_fa, 1)
            for u in range(2):
                act.wait_ge(sv_mm, 2 * u + 1)
                nc.scalar.activation(sv[:, 0, u * C:(u + 1) * C], ps[:, 4 + 2 * u, :], ACT.Copy).then_inc(sv_a, 1)

            def sb_log(g):
                z = ps[:, 2 * (g % 2):2 * (g % 2) + 2, 0:TRI]
                act.wait_ge(s_z, g + 1)
                if g >= 2:
                    act.wait_ge(s_la, g - 1)
                link(nc.scalar.activation(l_b[g % 2], z, ACT.Abs, scale=SDH ** -0.5))
                nc.scalar.activation(z_b[g % 2], z, ACT.Copy, scale=SDH ** -0.5).then_inc(s_zc, 1)
                link(nc.scalar.activation(l_b[g % 2], l_b[g % 2], ACT.Exp, scale=-1.0))
                nc.scalar.activation(l_b[g % 2], l_b[g % 2], ACT.Ln, bias=1.0).then_inc(s_l, 1)

            def sb_exp(g):
                act.wait_ge(s_la, g + 1)
                nc.scalar.activation(a_b[g % 2], a_b[g % 2], ACT.Exp).then_inc(s_a, 1)

            sb_log(0)
            sb_log(1)
            for g in range(SH // 2):
                sb_exp(g)
                if g + 2 < SH // 2:
                    sb_log(g + 2)

            norm_act(act, 3)
            norm_evict(act, 3, 0)
            ffn(1)
            norm_act(act, 4)
            norm_act(act, 5)
            norm_evict(act, 5, 0)

            act.wait_ge(l_f, 1)
            link(nc.scalar.activation(rows4[0:LH, 2, :], rows4[0:LH, 1, :], ACT.Abs))
            link(nc.scalar.activation(rows4[0:LH, 2, :], rows4[0:LH, 2, :], ACT.Exp, scale=-1.0))
            nc.scalar.activation(rows4[0:LH, 2, :], rows4[0:LH, 2, :], ACT.Ln, bias=1.0).then_inc(l_ln, 1)
            w0, b0 = SMALL["conv2_w"][0], SMALL["conv2_b"][0]
            for q in range(4):
                act.wait_ge(mi_mm, q + 1)
                if q:
                    act.wait_ge(mi_si, q)
                for f in range(2):
                    n = 2 * q + f
                    last = nc.scalar.activation(cvm[:, f, :], ps[:, q, f * T:(f + 1) * T], ACT.Identity,
                                                scale=small[:, w0 + 4 * n + 3:w0 + 4 * n + 4],
                                                bias=small[:, b0 + n:b0 + n + 1])
                last.then_inc(mi_id, 1)
                act.wait_ge(mi_cv, q + 1)
                nc.scalar.activation(qkm[:, 2 * q:2 * q + 2, :], cvm[:, :, :], ACT.Silu).then_inc(mi_si, 1)
            for n, q in enumerate((4, 6)):
                act.wait_ge(mi_mm, q + 1)
                nc.scalar.activation(qka[:, 2 * (q - 4):2 * (q - 4) + 2, :].rearrange("p a b -> p (a b)"),
                                     ps[:, q % 4, :], ACT.Copy).then_inc(mi_ev_a, 1)
            act.wait_ge(mi_mm, 9)
            nc.scalar.activation(vm[:, 0, :].rearrange("p (h e) -> p h e", h=LH)[:, :, 0:LDH],
                                 ps[:, 0, :].rearrange("p (h e) -> p h e", h=LH), ACT.Copy).then_inc(mi_ev_a, 1)
            act.wait_ge(mi_mm, 11)
            nc.scalar.activation(om[:, 0, :], ps[:, 2, :], ACT.Copy).then_inc(mi_ev_a, 1)
            act.wait_ge(mi_mm, 13)
            nc.scalar.activation(va[:, 0, :], ps[:, 0, :], ACT.Copy).then_inc(mi_ev_a, 1)
            act.wait_ge(mi_ev_a, 5)
            act.wait_ge(mi_ev_v, 5)
            nc.scalar.activation(om[:, :, :], om[:, :, :], ACT.Sigmoid).then_inc(l_sig, 1)
            act.wait_ge(l_rows, 1)
            act.wait_ge(l_cols, 1)
            nc.scalar.activation(fcol[:, :, :], fcol[:, :, :], ACT.Exp).then_inc(l_floor, 1)
            for h in range(LH):
                act.wait_ge(l_w, h + 1)
                nc.scalar.activation(wt[:, h % 2, :], wt[:, h % 2, :], ACT.Exp).then_inc(l_e, 1)
            for h in range(MH):
                act.wait_ge(b_mx, h + 1)
                for blk, (c0, c1) in enumerate(((0, P), (P, TRI))):
                    last = nc.scalar.activation(m_sc[:, h % 2, c0:c1], m_sc[:, h % 2, c0:c1], ACT.Exp,
                                                bias=mst[:, 4 * h + blk:4 * h + blk + 1],
                                                accum_out=mst[:, 4 * h + 2 + blk:4 * h + 3 + blk])
                last.then_inc(b_e, 1)
            act.wait_ge(l_h, LH)
            for h in range(LH):
                for t in range(NT):
                    link(nc.scalar.activation(pt[:, 0, 0:LDH], hm[:, t, h * LDH:(h + 1) * LDH], ACT.Square,
                                              accum_out=mst[:, 64 + 2 * h + t:65 + 2 * h + t]))
            nc.scalar.activation(credit[:, 5:6], small[:, 0:1], ACT.Copy).then_inc(l_sq, 1)
            act.wait_ge(l_ms, 1)
            nc.scalar.activation(mst[:, 72:80], mst[:, 64:72], ACT.Sqrt).then_inc(l_sd, 1)

            norm_act(act, 6)
            norm_evict(act, 6, 0)
            act.wait_ge(t_top, 1)
            for t in range(NT):
                last = nc.scalar.activation(g8[:, t, 0:NG], g8[:, t, 0:NG], ACT.Exp, accum_out=rst[:, 4 + t:5 + t])
            link(last)
            nc.scalar.activation(rst[:, 8:10], rst[:, 6:8], ACT.Exp).then_inc(t_exp, 1)

            def expert_pass(r):
                def xg_evict(value):
                    act.wait_ge(m_ga, value)
                    for k in range(4):
                        last = nc.scalar.activation(xg[:, k, :], ps[:, 4, k * P:(k + 1) * P], ACT.Identity,
                                                    scale=mods[:, 2, k:k + 1], bias=mods[:, 3, k:k + 1])
                    last.then_inc(m_xa, 1)

                act.wait_ge(m_zero, 3 * (r + 1))
                nc.scalar.activation(credit[:, 6:7], small[:, 0:1], ACT.Copy).then_inc(m_ya, 1)
                xg_evict((PAIRS + 1) * 2 * r + 2)
                with act.Fori(0, PAIRS) as i:
                    act.wait_ge(m_gu, i * 2 + (PAIRS * 2 * r + 1))
                    nc.scalar.activation(hs, ps[:, 4, :], ACT.Silu).then_inc(m_si, 1)
                    act.wait_ge(m_ht, i + (PAIRS * r + 1))
                    nc.scalar.activation(hgT[:, :, :].rearrange("p k n -> p (k n)"), ps[:, 4, :], ACT.Copy)\
                        .then_inc(m_hc, 1)
                    xg_evict(i * 2 + ((PAIRS + 1) * 2 * r + 4))
                    act.wait_ge(m_dn, i + (PAIRS * r + 1))
                    nc.scalar.activation(ye[:, 0:C], ps[:, 6, :], ACT.Copy).then_inc(m_ya, 1)

            expert_pass(0)
            act.wait_ge(t_flag, 1)
            most = act.value_load(flag[0:1, 0:1])
            with act.If(most > R):
                for r in range(1, PASSES):
                    expert_pass(r)
            norm_act(act, 7)

        @block.vector
        def _(dve):
            link = Link(dve, dve_chain)
            norm_dve(dve, link, 0)
            dve.wait_ge(small_in, 16)
            norm_evict(dve, 0, 1)
            dve.wait_ge(norm_ha, 2)
            nc.vector.memset(credit[:, 0:1], 0.0).then_inc(rqk_free, 4)
            cos, sin = k_("cos"), k_("sin")
            dve.wait_ge(const_in, 16)
            with dve.Fori(0, 2) as i:
                link.enter(i, 4)
                for b in range(2):
                    for j in range(2):
                        q = i * 4 + (2 * b + j)
                        u = ps[:, 2 * b + j, :]
                        dve.wait_ge(rqk_mm, i * 4 + (2 * b + j + 1))
                        nc.vector.tensor_tensor(rot_a, u, cos, ALU.mult)
                        nc.vector.tensor_tensor(rot_b[:, 0:T], u[:, T:C], sin[:, 0:T], ALU.mult)
                        nc.vector.tensor_tensor(rot_b[:, T:C], u[:, 0:T], sin[:, T:C], ALU.mult)\
                            .then_inc(rqk_free, 1)
                        dve.wait_ge(rqk_free, i * 4 + (4 + 2 * b + j + 1))
                        link(nc.vector.tensor_tensor(qk[:, q, :], rot_a, rot_b, ALU.add))
            link.leave(2)
            nc.vector.memset(credit[:, 0:1], 0.0).then_inc(rqk_out, 8)
            nc.vector.memset(credit[:, 2:3], 0.0).then_inc(rvg_fv, 2)
            with dve.Fori(0, 4) as i:
                for b in range(2):
                    dve.wait_ge(rvg_mm, i * 4 + (2 * b + 2))
                    nc.vector.tensor_copy(vg[:, 1, bass.ds(i * 2 * C + b * C, C)], ps[:, 5 + 2 * b, :])\
                        .then_inc(rvg_fv, 1)

            decay = k_("decay").rearrange("p (h t) -> p h t", h=RH)

            def ret_decay(h):
                dve.wait_ge(r_s, h + 1)
                if h >= 2:
                    dve.wait_ge(r_o, 2 * (h - 1))
                nc.vector.tensor_tensor(r_sc[:, h % 2, :], ps[:, h % 2, 0:TRI], decay[:, h, :], ALU.mult)\
                    .then_inc(r_d, 1)

            def ret_y(h):
                dve.wait_ge(r_sq, 2 * (h + 1))
                nc.vector.tensor_scalar(stat[:, 10:12], stat[:, 8:10], 1.0 / RDV, EPS, ALU.mult, ALU.add)\
                    .then_inc(r_ms, 1)
                dve.wait_ge(r_sd, h + 1)
                link(nc.vector.reciprocal(stat[:, 14:16], stat[:, 12:14]))
                if h == 0:
                    dve.wait_ge(rg_silu, 2)
                for t in range(NT):
                    g = vg[:, t, RV + h * RDV:RV + (h + 1) * RDV]
                    nc.vector.scalar_tensor_tensor(out=g, in0=ps[:, 2 + 2 * (h % 2) + t, :], scalar=stat[:, 14 + t:15 + t],
                                                   in1=g, op0=ALU.mult, op1=ALU.mult).then_inc(r_y, 1)

            def ret_copy(h):
                dve.wait_ge(r_t, 2 * h + 2)
                nc.vector.tensor_copy(yT[:, 4 * h + 2:4 * h + 4, :].rearrange("p a b -> p (a b)"), ps[:, 7, :])\
                    .then_inc(r_tv, 1)

            ret_decay(0)
            ret_decay(1)
            for h in range(RH):
                ret_y(h)
                if h + 2 < RH:
                    ret_decay(h + 2)
                if h >= 1:
                    ret_copy(h - 1)
            ret_copy(RH - 1)
            residual(dve, rout_mm, 4)
            norm_dve(dve, link, 1)
            norm_evict(dve, 1, 1)

            def ffn(l, ada):
                base = (FP + 4) * l
                dve.wait_ge(norm_ha, 2 * (N_TR[2 * l + 1] + 1))
                nc.vector.memset(credit[:, 0:1], 0.0).then_inc(up_free, 4)
                if ada:
                    dve.wait_ge(ada_c, 1)
                    nc.vector.memset(credit[:, 1:2], 0.0).then_inc(ada_used, 2)

                def pair(b, j, off):
                    n = off + (2 * b + j)
                    w0 = SMALL["conv_w"][0]
                    tap = lambda gv, k: small[:, bass.ds(n * 3 + (w0 + (l * 2 + gv) * FP * 3 + k), 1)]
                    c, u = cv[:, j, :], ps[:, 2 * b + j, :]
                    dve.wait_ge(up_id, off + (FP * l + 2 * b + j + 1))
                    for gv in range(2):
                        o = gv * T
                        last = nc.vector.scalar_tensor_tensor(
                            out=c[:, o + 1:o + T], in0=u[:, o:o + T - 1], scalar=tap(gv, 1), in1=c[:, o + 1:o + T],
                            op0=ALU.mult, op1=ALU.add)
                    link(last)
                    for gv in range(2):
                        o = gv * T
                        last = nc.vector.scalar_tensor_tensor(
                            out=c[:, o + 2:o + T], in0=u[:, o:o + T - 2], scalar=tap(gv, 0), in1=c[:, o + 2:o + T],
                            op0=ALU.mult, op1=ALU.add)
                        if gv == 0:
                            last.then_inc(up_cv, 1)
                    last.then_inc(up_free, 1)
                    dve.wait_ge(up_free, off + (base + 4 + 2 * b + j + 1))
                    dve.wait_ge(up_si, off + (FP * l + 2 * b + j + 1))
                    nc.vector.tensor_tensor(hff[:, n, :], c[:, 0:T], c[:, T:C], ALU.mult).then_inc(up_h, 1)

                def ada_half(nb, kh):
                    acc = ada_acc[:, bass.ds(nb * C, C)]
                    dve.wait_ge(ada_in[kh], nb * 16 + 16)
                    for k in range(4):
                        w, s = ada_w[kh][:, k, :], stat[:, 16 + 4 * kh + k:17 + 4 * kh + k]
                        if kh == 0 and k == 0:
                            ins = nc.vector.tensor_scalar(acc, w, s, None, ALU.mult)
                        else:
                            ins = nc.vector.scalar_tensor_tensor(out=acc, in0=w, scalar=s, in1=acc,
                                                                 op0=ALU.mult, op1=ALU.add)
                        if k < 3:
                            link(ins)
                    ins.then_inc(ada_used, 1)
                    dve.wait_ge(ada_used, nb * 2 + (2 + kh + 1))

                with dve.Fori(0, 5) as i:
                    link.enter(i, 4 + (6 if ada else 0))
                    for b in range(2):
                        for j in range(2):
                            pair(b, j, i * 4)
                        if ada:
                            ada_half(i, b)
                link.leave(5)
                for j in range(2):
                    pair(0, j, 20)
                if ada:
                    with dve.Fori(5, 12) as nb:
                        link.enter(nb - 5, 6)
                        for j in range(2):
                            ada_half(nb, j)
                    link.leave(7)
                    nc.vector.memset(credit[:, 1:2], 0.0).then_inc(ada_sum, 1)
                residual(dve, down_mm, 6 * (l + 1))

            ffn(0, True)

            def modulations():
                mr = modr[:, :].rearrange("p (m k) -> p m k", m=4)
                dve.wait_ge(ada_mods, 1)
                ba = b_ada.rearrange("p (m k) -> p m k", m=6)
                for m, q in enumerate((0, 1, 3, 4)):
                    last = nc.vector.tensor_tensor(mr[:, m, :], ps[:, 3, m * KD:(m + 1) * KD], ba[:, q, :], ALU.add)
                last.then_inc(ada_gate, 1)
                dve.wait_ge(ada_gate, 1)
                for n, (sh, scl, g) in enumerate(((0, 1, "g1"), (2, 3, "g2"))):
                    nc.vector.tensor_copy(mods[:, 2 * n + 1, :], mr[:, sh, :])
                    link(nc.vector.scalar_tensor_tensor(out=mods[:, 2 * n, :], in0=mr[:, scl, :], scalar=1.0,
                                                        in1=s_(g), op0=ALU.add, op1=ALU.mult))

            modulations()
            norm_dve(dve, link, 2)
            norm_evict(dve, 2, 1)
            dve.wait_ge(ada_mods, 2)
            dve.wait_ge(bias_in, 32)
            for half in range(4):
                gt = gates[:, half // 2, (half % 2) * C:(half % 2 + 1) * C]
                nc.vector.tensor_tensor(gt, ps[:, 4 + half, :], gt, ALU.add).then_inc(ada_gate, 1)

            dve.wait_ge(norm_ha, 6)
            nc.vector.memset(credit[:, 0:1], 0.0).then_inc(sqk_fv, 2)
            with dve.Fori(0, 2) as i:
                for b in range(2):
                    dve.wait_ge(sqk_mm, i * 4 + (2 * b + 2))
                    nc.vector.tensor_copy(sqk[:, i * 4 + (2 * b + 1), :], ps[:, 2 * b + 1, :])\
                        .then_inc(sqk_fv, 1)
            for u in range(2):
                dve.wait_ge(sv_mm, 2 * u + 2)
                nc.vector.tensor_copy(sv[:, 1, u * C:(u + 1) * C], ps[:, 5 + 2 * u, :]).then_inc(sv_v, 1)

            def sb_softplus(g):
                dve.wait_ge(s_zc, g + 1)
                dve.wait_ge(s_l, g + 1)
                if g >= 2:
                    dve.wait_ge(s_ex, g - 1)
                nc.vector.scalar_tensor_tensor(out=sp_b[g % 2], in0=z_b[g % 2], scalar=0.0, in1=l_b[g % 2],
                                               op0=ALU.max, op1=ALU.add).then_inc(s_sp, 1)

            def sb_log_a(g):
                link(nc.vector.scalar_tensor_tensor(out=z_b[g % 2], in0=z_b[g % 2], scalar=0.0, in1=l_b[g % 2],
                                                    op0=ALU.min, op1=ALU.subtract))
                dve.wait_ge(s_ex, g + 1)
                if g >= 2:
                    dve.wait_ge(s_o, g - 1)
                nc.vector.tensor_tensor(a_b[g % 2], z_b[g % 2], ps[:, 4:6, 0:TRI], ALU.subtract).then_inc(s_la, 1)

            def sb_copy(g):
                dve.wait_ge(s_o, g + 1)
                nc.vector.tensor_copy(soT[:, g, :], ps[:, 6 + g % 2, 0:T]).then_inc(s_ot, 1)

            sb_softplus(0)
            sb_softplus(1)
            for g in range(SH // 2):
                dve.wait_ge(s_sp, g + 1)
                sb_log_a(g)
                if g + 2 < SH // 2:
                    sb_softplus(g + 2)
                if g >= 1:
                    sb_copy(g - 1)
            sb_copy(SH // 2 - 1)
            residual(dve, sout_mm, 2)
            norm_dve(dve, link, 3)
            norm_evict(dve, 3, 1)
            ffn(1, False)

            def scale_rows():
                for t in range(NT):
                    nc.vector.scalar_tensor_tensor(out=x[:, t, :], in0=x[:, t, :], scalar=stat[:, 6 + t:7 + t],
                                                   in1=rowv[:, :], op0=ALU.mult, op1=ALU.mult).then_inc(x_new, 1)

            norm_dve(dve, link, 4)
            dve.wait_ge(row_in, 16)
            dve.wait_ge(x_new, update(3))
            scale_rows()
            norm_dve(dve, link, 5)
            norm_evict(dve, 5, 1)

            row = lambda n: rows4[0:LH, n, :]
            dve.wait_ge(mix_small, 80)
            nc.vector.memset(vm[:, :, :], 1.0)
            nc.vector.memset(row(8), 1.0)
            dve.wait_ge(mi_g, 1)
            link(nc.vector.tensor_scalar(row(0), ps[0:LH, 4, 0:T], bg[0:LH, 0:1], None, ALU.add))
            nc.vector.tensor_scalar(row(1), ps[0:LH, 5, 0:T], bg[0:LH, 1:2], None, ALU.add).then_inc(l_f, 1)
            dve.wait_ge(l_ln, 1)
            dve.wait_ge(l_f, 1)
            link(nc.vector.scalar_tensor_tensor(out=row(1), in0=row(1), scalar=0.0, in1=row(2), op0=ALU.min,
                                                op1=ALU.subtract))
            link(nc.vector.tensor_tensor_scan(row(3), row(8), row(1), 0.0, ALU.mult, ALU.add))
            link(nc.vector.tensor_tensor(row(4), row(0), row(3), ALU.subtract))
            link(nc.vector.tensor_tensor_scan(row(5), row(8), row(4), 0.0, ALU.mult, ALU.max))
            nc.vector.tensor_scalar(row(6), row(5), -1.0, None, ALU.mult)
            nc.vector.scalar_tensor_tensor(out=row(7), in0=row(3), scalar=-1.0, in1=row(5), op0=ALU.mult,
                                           op1=ALU.subtract).then_inc(l_rows, 1)

            w0 = SMALL["conv2_w"][0]
            for q in range(4):
                dve.wait_ge(mi_id, q + 1)
                for k in (2, 1, 0):
                    for f in range(2):
                        n, d = 2 * q + f, 3 - k
                        ins = nc.vector.scalar_tensor_tensor(
                            out=cvm[:, f, d:T], in0=ps[:, q, f * T:(f + 1) * T - d],
                            scalar=small[:, w0 + 4 * n + k:w0 + 4 * n + k + 1], in1=cvm[:, f, d:T],
                            op0=ALU.mult, op1=ALU.add)
                    if k:
                        link(ins)
                ins.then_inc(mi_cv, 1)
            for q in (5, 7):
                dve.wait_ge(mi_mm, q + 1)
                nc.vector.tensor_copy(qka[:, 2 * (q - 4):2 * (q - 4) + 2, :].rearrange("p a b -> p (a b)"),
                                      ps[:, q % 4, :]).then_inc(mi_ev_v, 1)
            dve.wait_ge(mi_mm, 10)
            nc.vector.tensor_copy(vm[:, 1, :].rearrange("p (h e) -> p h e", h=LH)[:, :, 0:LDH],
                                  ps[:, 1, :].rearrange("p (h e) -> p h e", h=LH)).then_inc(mi_ev_v, 1)
            dve.wait_ge(mi_mm, 12)
            nc.vector.tensor_copy(om[:, 1, :], ps[:, 3, :]).then_inc(mi_ev_v, 1)
            dve.wait_ge(l_tr, 1)
            nc.vector.tensor_copy(acol[:, :, :].rearrange("p a b -> p (a b)"), ps[:, 6, 0:8])
            nc.vector.tensor_copy(fcol[:, :, :].rearrange("p a b -> p (a b)"), ps[:, 6, 8:16]).then_inc(l_cols, 1)
            dve.wait_ge(mi_mm, 14)
            nc.vector.tensor_copy(va[:, 1, :], ps[:, 1, :]).then_inc(mi_ev_v, 1)
            dve.wait_ge(l_sig, 1)
            gh = ghead.unsqueeze(1).broadcast_to([P, NT, C])
            link(nc.vector.tensor_tensor(om[:, :, :], om[:, :, :], gh, ALU.mult))
            dve.wait_ge(l_cols, 1)

            def ls_w(h):
                b = 3 * (h % 2)
                dve.wait_ge(l_s, h + 1)
                if h >= 2:
                    dve.wait_ge(l_p, h - 1)
                nc.vector.tensor_scalar(wt[:, h % 2, 0:T], ps[:, b, 0:T], acol[:, 0, h:h + 1], 0.0, ALU.add, ALU.min)
                nc.vector.tensor_scalar(wt[:, h % 2, T:TRI], ps[:, b, P:T], acol[:, 1, h:h + 1], 0.0, ALU.add, ALU.min)\
                    .then_inc(l_w, 1)

            def ls_p(h):
                b = 3 * (h % 2) + 1
                dve.wait_ge(l_e, h + 1)
                diag = wt[:, h % 2, :].rearrange("p (b t) -> p b t", b=3)[:, 0:3:2, :]
                link(nc.vector.tensor_tensor(diag, diag, upto.unsqueeze(1).broadcast_to([P, 2, P]), ALU.mult))
                if h >= 2:
                    dve.wait_ge(l_o, h - 1)
                nc.vector.scalar_tensor_tensor(out=pt[:, h % 2, :], in0=ps[:, b, 0:TRI], scalar=LDH ** -0.5,
                                               in1=wt[:, h % 2, :], op0=ALU.mult, op1=ALU.mult).then_inc(l_p, 1)

            def ls_h(h):
                b = 3 * (h % 2) + 2
                dve.wait_ge(l_o, h + 1)
                if h == 0:
                    dve.wait_ge(l_floor, 1)
                den = lambda t: mst[:, 80 + 2 * h + t:81 + 2 * h + t]
                for t in range(NT):
                    last = nc.vector.tensor_scalar(den(t), ps[:, b, t * T + LDH:t * T + LDH + 1], -1.0,
                                                   fcol[:, t, h:h + 1], ALU.mult, ALU.max)
                link(last)
                for t in range(NT):
                    last = nc.vector.tensor_tensor(den(t), ps[:, b, t * T + LDH:t * T + LDH + 1], den(t), ALU.max)
                link(last)
                link(nc.vector.reciprocal(mst[:, 88 + 2 * h:90 + 2 * h], mst[:, 80 + 2 * h:82 + 2 * h]))
                for t in range(NT):
                    last = nc.vector.tensor_scalar(hm[:, t, h * LDH:(h + 1) * LDH], ps[:, b, t * T:t * T + LDH],
                                                   mst[:, 88 + 2 * h + t:89 + 2 * h + t], None, ALU.mult)
                last.then_inc(l_h, 1)

            ls_w(0)
            ls_w(1)
            for h in range(LH):
                ls_p(h)
                if h + 2 < LH:
                    dve.wait_ge(l_p, h + 1)
                    ls_w(h + 2)
                ls_h(h)

            future = k_("future")

            def mb_max(h):
                dve.wait_ge(b_s, h + 1)
                if h >= 2:
                    dve.wait_ge(b_t, h - 1)
                sc = m_sc[:, h % 2, :]
                link(nc.vector.scalar_tensor_tensor(out=sc, in0=ps[:, 6 + h % 2, 0:TRI], scalar=MDH ** -0.5, in1=future,
                                                    op0=ALU.mult, op1=ALU.add))
                nc.vector.tensor_reduce(mst[:, 4 * h:4 * h + 1], sc[:, 0:P], AX, ALU.max, negate=True)
                nc.vector.tensor_reduce(mst[:, 4 * h + 1:4 * h + 2], sc[:, P:TRI], AX, ALU.max, negate=True)\
                    .then_inc(b_mx, 1)

            def mb_p(h):
                dve.wait_ge(b_e, h + 1)
                link(nc.vector.reciprocal(mst[:, 4 * h + 2:4 * h + 4], mst[:, 4 * h + 2:4 * h + 4]))
                for blk, (c0, c1) in enumerate(((0, P), (P, TRI))):
                    last = nc.vector.tensor_scalar(m_sc[:, h % 2, c0:c1], m_sc[:, h % 2, c0:c1],
                                                   mst[:, 4 * h + 2 + blk:4 * h + 3 + blk], None, ALU.mult)
                last.then_inc(b_p, 1)

            def mb_copy(h):
                dve.wait_ge(b_t, h + 1)
                if h >= 2:
                    dve.wait_ge(b_o, h - 1)
                nc.vector.tensor_copy(wt[:, h % 2, :], ps[:, h % 2, 0:TRI]).then_inc(b_tc, 1)

            def mb_o(g):
                dve.wait_ge(b_o, 2 * (g + 1))
                nc.vector.tensor_copy(mixT[:, 4 + g, :], ps[:, 3 + g % 2, 0:T]).then_inc(b_oc, 1)

            mb_max(0)
            mb_max(1)
            for h in range(MH):
                mb_p(h)
                mb_copy(h)
                if h + 2 < MH:
                    mb_max(h + 2)
                if h >= 1 and h % 2 == 0:
                    mb_o(h // 2 - 1)
            mb_o(MH // 2 - 1)

            dve.wait_ge(l_sq, 1)
            nc.vector.tensor_scalar(mst[:, 64:72], mst[:, 64:72], 1.0 / LDH, EPS, ALU.mult, ALU.add).then_inc(l_ms, 1)
            dve.wait_ge(l_sd, 1)
            link(nc.vector.reciprocal(mst[:, 96:104], mst[:, 72:80]))
            for h in range(LH):
                for t in range(NT):
                    cols = slice(h * LDH, (h + 1) * LDH)
                    nc.vector.scalar_tensor_tensor(out=hm[:, t, cols], in0=hm[:, t, cols],
                                                   scalar=mst[:, 96 + 2 * h + t:97 + 2 * h + t], in1=om[:, t, cols],
                                                   op0=ALU.mult, op1=ALU.mult).then_inc(l_hn, 1)
            for j in range(2):
                dve.wait_ge(l_t, j + 1)
                nc.vector.tensor_copy(mixT[:, 2 * j:2 * j + 2, :].rearrange("p a b -> p (a b)"), ps[:, j, :])\
                    .then_inc(l_mt, 1)

            dve.wait_ge(mo_mm, 2)
            gated_residual(link, 0, 4, xn, True)

            norm_dve(dve, link, 6)
            norm_evict(dve, 6, 1)

            dve.wait_ge(t_lg, 1)
            dve.wait_ge(r_in, 64)
            lgp = ps[:, 4, 0:P].rearrange("p (t n) -> p t n", t=NT)[:, :, 0:NG + NE]
            nc.vector.memset(g8[:, :, :], NEG)
            nc.vector.memset(pos[:, :, :], -1.0)
            nc.vector.memset(wgt[:, :, :], 0.0)
            link(nc.vector.tensor_tensor(lg[:, :, :], lgp, br.unsqueeze(1).broadcast_to([P, NT, NG + NE]), ALU.add))
            link(nc.vector.tensor_copy(g8[:, :, 0:NG], lg[:, :, 0:NG]))
            for t in range(NT):
                link(nc.vector.max(m8[:, t, :], g8[:, t, :]))
                link(nc.vector.max_index(i8[:, t, :], m8[:, t, :], g8[:, t, :]))
            link(nc.vector.tensor_copy(f8[:, :, :], i8[:, :, :]))
            for t in range(NT):
                nc.vector.tensor_scalar(oh[:, t, :], iota[:, 0:NG], f8[:, t, 0:1], None, ALU.is_equal)
                link(nc.vector.tensor_scalar(g8[:, t, 0:NG], g8[:, t, 0:NG], m8[:, t, 0:1], None, ALU.subtract))
            link(nc.vector.tensor_scalar(oh[:, :, :], oh[:, :, :], -1.0, -NEG, ALU.add, ALU.mult))
            for t in range(NT):
                pen = oh[:, t, :].unsqueeze(2).broadcast_to([P, NG, EPG])
                link(nc.vector.tensor_tensor(em[:, t, :].rearrange("p (g e) -> p g e", g=NG),
                                             lg[:, t, NG:].rearrange("p (g e) -> p g e", g=NG), pen, ALU.add))
                link(nc.vector.max(m8[:, t, :], em[:, t, :]))
                link(nc.vector.max_index(i8[:, t, :], m8[:, t, :], em[:, t, :]))
            link(nc.vector.tensor_copy(f8[:, :, :], i8[:, :, :]))
            for t in range(NT):
                last = nc.vector.tensor_tensor(rst[:, 6 + t:7 + t], m8[:, t, 1:2], m8[:, t, 0:1], ALU.subtract)
                link(nc.vector.tensor_scalar(oh1[:, t, :], iota[:, 0:NE], f8[:, t, 0:1], None, ALU.is_equal))
                link(nc.vector.tensor_scalar(oh2[:, t, :], iota[:, 0:NE], f8[:, t, 1:2], None, ALU.is_equal))
            nc.vector.memset(credit[:, 0:1], 0.0).then_inc(t_top, 1)
            nc.vector.tensor_tensor(asg[:, :, :], oh1[:, :, :], oh2[:, :, :], ALU.add).then_inc(t_rank, 1)
            dve.wait_ge(t_exp, 1)
            link(nc.vector.tensor_scalar(rst[:, 10:12], rst[:, 8:10], 1.0, None, ALU.add))
            link(nc.vector.tensor_tensor(rst[:, 10:12], rst[:, 10:12], rst[:, 4:6], ALU.mult))
            link(nc.vector.reciprocal(rst[:, 12:14], rst[:, 10:12]))
            link(nc.vector.tensor_tensor(rst[:, 14:16], rst[:, 12:14], rst[:, 8:10], ALU.mult))
            for t in range(NT):
                link(nc.vector.tensor_scalar(oh2[:, t, :], oh2[:, t, :], rst[:, 14 + t:15 + t], None, ALU.mult))
                link(nc.vector.scalar_tensor_tensor(out=wgt[:, t, 0:NE], in0=oh1[:, t, :], scalar=rst[:, 12 + t:13 + t],
                                                    in1=oh2[:, t, :], op0=ALU.mult, op1=ALU.add))
            dve.wait_ge(t_lg, 2)
            dve.wait_ge(t_rank, 1)
            rank = ps[:, 5, 0:P].rearrange("p (t n) -> p t n", t=NT)[:, :, 0:NE]
            link(nc.vector.scalar_tensor_tensor(out=em[:, :, :], in0=rank, scalar=1.0, in1=asg[:, :, :],
                                                op0=ALU.add, op1=ALU.mult))
            link(nc.vector.tensor_scalar(pos[:, :, 0:NE], em[:, :, :], -1.0, None, ALU.add))
            link(nc.vector.tensor_reduce(rst[:, 20:21], ps[:, 5, 128:128 + NE], AX, ALU.max))
            nc.vector.tensor_copy(flag, rst[:, 20:21]).then_inc(t_flag, 1)
            dve.wait_ge(norm_ha, 12)

            def expert_pass(r, link):
                slots = iota[:, r * R:(r + 1) * R]

                def select(buf, i, weigh, done):
                    for t in range(NT):
                        for e in range(2):
                            col = i * 2 + e
                            if weigh:
                                ins = nc.vector.tensor_scalar(buf[:, t, e * R:(e + 1) * R], slots,
                                                              pos[:, t, bass.ds(col, 1)], wgt[:, t, bass.ds(col, 1)],
                                                              ALU.is_equal, ALU.mult)
                            else:
                                ins = nc.vector.tensor_scalar(buf[:, t, e * R:(e + 1) * R], slots,
                                                              pos[:, t, bass.ds(col, 1)], None, ALU.is_equal)
                    ins.then_inc(done, 1)

                def xg_evict(value):
                    dve.wait_ge(m_ga, value)
                    for k in range(4, 8):
                        last = nc.vector.tensor_scalar(xg[:, k, :], ps[:, 5, (k - 4) * P:(k - 3) * P],
                                                       mods[:, 2, k:k + 1], mods[:, 3, k:k + 1], ALU.mult, ALU.add)
                    last.then_inc(m_xv, 1)

                nc.vector.memset(selT[:, :], 0.0).then_inc(m_zero, 1)
                nc.vector.memset(ye[:, :], 0.0).then_inc(m_zero, 1)
                nc.vector.memset(credit[:, 0:1], 0.0).then_inc(m_zero, 1)
                dve.wait_ge(m_zero, 3 * (r + 1))
                nc.vector.memset(credit[:, 1:2], 0.0).then_inc(m_yv, 1)
                dve.wait_ge(m_start, r + 1)
                select(sel, 0, False, m_s)
                select(selw, 0, True, m_sw)
                xg_evict((PAIRS + 1) * 2 * r + 1)
                dve.wait_ge(m_ga, (PAIRS + 1) * 2 * r + 2)
                select(sel, 1, False, m_s)
                with dve.Fori(0, PAIRS) as i:
                    dve.wait_ge(m_si, i + (PAIRS * r + 1))
                    dve.wait_ge(m_gu, i * 2 + (PAIRS * 2 * r + 2))
                    nc.vector.tensor_tensor(hg, hs, ps[:, 5, :], ALU.mult).then_inc(m_h, 1)
                    dve.wait_ge(m_sct, i + ((PAIRS + 1) * r + 1))
                    nc.vector.tensor_copy(selT[:, :], ps[:, 6, 0:T]).then_inc(m_swt, 1)
                    xg_evict(i * 2 + ((PAIRS + 1) * 2 * r + 3))
                    dve.wait_ge(m_ga, i * 2 + ((PAIRS + 1) * 2 * r + 4))
                    select(sel, i + 2, False, m_s)
                    select(selw, i + 1, True, m_sw)
                    dve.wait_ge(m_dn, i + (PAIRS * r + 1))
                    nc.vector.tensor_copy(ye[:, C:2 * C], ps[:, 7, :]).then_inc(m_yv, 1)
                dve.wait_ge(m_sct, (PAIRS + 1) * (r + 1))
                gated_residual(link, 1, 0, gtmp, False)

            expert_pass(0, link)
            most = dve.value_load(flag[0:1, 0:1])
            with dve.If(most > R):
                more = Link(dve, over_chain)
                for r in range(1, PASSES):
                    expert_pass(r, more)
            nc.vector.memset(credit[:, 0:1], 0.0).then_inc(x_new, 4)
            norm_dve(dve, link, 7)
            dve.wait_ge(row_in, 32)
            scale_rows()


_DIRECT = ["x", "ret_w_in", "ret_w_out", "sb_w_in", "sb_w_out", "ffn_w_up", "ffn_w_down", "final_norm", "w_ada_2",
           "b_ada_2", "w_in_2", "w_out_2", "b_gates_2", "g_mlstm_head_2", "w_router_group_2", "b_router_group_2",
           "w_router_expert_2", "b_router_expert_2", "w_expert_gate_2", "w_expert_up_2", "w_expert_down_2",
           "g_final_2"]


def small_weights(inputs):
    get = lambda n: np.asarray(inputs[n])
    feat = lambda a: a.reshape(-1, P).T
    tiles = lambda a: a.reshape(-1, P).T
    cw = get("ffn_conv_w").reshape(2, 3, 2, FP, P).transpose(4, 0, 2, 3, 1).reshape(P, -1)
    parts = {
        "ret_norm": feat(get("ret_norm")[0]), "sb_norm": feat(get("sb_norm")[0]), "ffn_norm": feat(get("ffn_norm")),
        "g1": feat(get("g_norm1_2")[0]), "g2": feat(get("g_norm2_2")[0]), "c": get("c_2").reshape(P, KD),
        "b_ada": feat(get("b_ada_2")[0]), "conv_w": cw, "conv_b": tiles(get("ffn_conv_b")),
        "conv2_w": get("w_conv_2")[0].reshape(4, 2 * LH, P).transpose(2, 1, 0).reshape(P, -1),
        "conv2_b": feat(get("b_conv_2")[0]),
    }
    return np.ascontiguousarray(np.concatenate([parts[n] for n in SMALL], axis=1))


def kernel(**inputs):
    import concourse.bacc as _bacc
    from concourse.bass_utils import run_bass_kernel_spmd as _run

    nc = _bacc.Bacc("TRN2", target_bir_lowering=False, num_devices=1)
    arrays = {f"in_{n}_dram": np.ascontiguousarray(inputs[n]) for n in _DIRECT}
    arrays["in_small_dram"] = small_weights(inputs)
    arrays["in_const_dram"] = shape_constants()
    arrays["in_sel4_dram"] = np.repeat(np.eye(LH, dtype=np.float32), P, axis=1)
    A = {n[3:-5]: nc.dram_tensor(n, a.shape, mybir.dt.from_np(a.dtype), kind="ExternalInput").ap()
         for n, a in arrays.items()}
    out = nc.dram_tensor("out_0_dram", (1, T, D), F32, kind="ExternalOutput").ap()
    build(nc, A, out)
    r = _run(nc, [arrays], core_ids=[0])
    return r.results[0]["out_0_dram"]
```

```python
from contextlib import ExitStack

import numpy as np

import concourse.bass as bass
from concourse import mybir

P = 128
D = 1024
T = 256
NT = T // P
KD = D // P
C = 512
EPS = 1e-6
RH, RDK, RDV = 4, 256, 512
RV = RH * RDV
SH, SDH = 16, 64
FF = 2816
FP = FF // P
LH, LDH = 4, 128
MH, MDH = 8, 64
NE, NG, EPG = 32, 4, 8
DE = 512
KE = DE // P
R = 64
PASSES = T // R
PAIRS = NE // 2
TRI = 3 * P
NEG = -1e30

F32 = mybir.dt.float32
F32R = mybir.dt.float32r
I32 = mybir.dt.int32
U32 = mybir.dt.uint32
ALU = mybir.AluOpType
ACT = mybir.ActivationFunctionType
AX = mybir.AxisListType.X

CONST = {}
_at = 0
for _name, _n in (("ident", P), ("ones", P), ("after", P), ("before", P), ("upto", P), ("future", TRI),
                  ("decay", RH * TRI), ("cos", 2 * T), ("sin", 2 * T), ("iota", T)):
    CONST[_name] = (_at, _at + _n)
    _at += _n
NCONST = _at

SMALL = {}
_at = 0
for _name, _n in (("ret_norm", KD), ("sb_norm", KD), ("ffn_norm", 2 * KD), ("g1", KD), ("g2", KD), ("c", KD),
                  ("b_ada", 6 * KD), ("conv_w", 2 * 2 * FP * 3), ("conv_b", 2 * 2 * FP),
                  ("conv2_w", 2 * LH * 4), ("conv2_b", 2 * LH)):
    SMALL[_name] = (_at, _at + _n)
    _at += _n
NSMALL = _at


def shape_constants():
    i = np.arange(P)
    s, t = i[:, None], i[None, :]
    out = np.zeros((P, NCONST), np.float32)

    def put(name, value):
        a, b = CONST[name]
        out[:, a:b] = value.reshape(P, b - a)

    put("ident", np.eye(P))
    put("ones", np.ones((P, P)))
    put("after", (s > t))
    put("before", (s < t))
    put("upto", (s <= t))
    put("future", np.concatenate([np.where(t > s, NEG, 0.0), np.zeros((P, P)), np.where(t > s, NEG, 0.0)], 1))
    decay = np.zeros((P, RH, TRI))
    for h in range(RH):
        log_g = np.log(1.0 - 2.0 ** (-5.0 - h))
        diag = np.where(s <= t, np.exp((t - s) * log_g), 0.0)
        decay[:, h] = np.concatenate([diag, np.exp((t - s + P) * log_g), diag], 1) * RDK ** -0.5
    put("decay", decay)
    freq = np.float32(10000.0) ** (-np.arange(0, RDK, 2, dtype=np.float32) / np.float32(RDK))
    ang = (freq.astype(np.float32)[:, None] * np.arange(T, dtype=np.float32)[None, :]).astype(np.float64)
    put("cos", np.concatenate([np.cos(ang), np.cos(ang)], 1))
    put("sin", np.concatenate([-np.sin(ang), np.sin(ang)], 1))
    put("iota", np.broadcast_to(np.arange(T), (P, T)))
    return out


def weight_plan(A):
    rows = lambda w: w.rearrange("(k p) n -> p k n", p=P)
    units = []

    def wide(phase, slot, w, c0):
        units.append((phase, slot, [((0, KD), (0, C), rows(w)[:, :, c0:c0 + C])]))

    def down(phase, slot, w, k0, n):
        units.append((phase, slot, [(None, n, rows(w)[:, k0:k0 + n, :])]))

    def ffn_up(l, slots):
        w = rows(A["ffn_w_up"][l])
        for u in range(FP // 2):
            s = slots[u % 2]
            units.append((f"up{l}", s, [((0, KD), (0, T), w[:, :, u * T:(u + 1) * T]),
                                        ((0, KD), (T, C), w[:, :, FF + u * T:FF + (u + 1) * T])]))

    def ffn_down(l, slots):
        for u, s in enumerate(slots):
            down(f"down{l}", s, A["ffn_w_down"][l], 4 * u, min(4, FP - 4 * u))

    for u in range(4):
        wide("ret_qk", u % 2, A["ret_w_in"][0], u * C)
    for u in range(8):
        wide("ret_vg", u % 2, A["ret_w_in"][0], (4 + u) * C)
    for u, s in enumerate((2, 0, 1, 2)):
        down("ret_out", s, A["ret_w_out"][0], 4 * u, 4)
    ffn_up(0, (0, 1))
    ffn_down(0, (2, 1, 0, 2, 1, 0))
    for u in range(4):
        wide("sb_qk", (2, 1)[u % 2], A["sb_w_in"][0], u * C)
    for u in range(2):
        wide("sb_v", (2, 1)[u], A["sb_w_in"][0], (4 + u) * C)
    for u, s in enumerate((0, 2)):
        down("sb_out", s, A["sb_w_out"][0], 4 * u, 4)
    ffn_up(1, (1, 0))
    ffn_down(1, (2, 0, 1, 2, 0, 1))
    gates = 4 * LH * LDH
    for c0, s in zip((0, C, gates + 8, gates + 8 + C, 2 * C, 3 * C, gates + 8 + 2 * C), (2, 0, 1, 2, 0, 1, 2)):
        wide("mix_in", s, A["w_in_2"][0], c0)
    for u, s in enumerate((0, 1)):
        down("mix_out", s, A["w_out_2"][0], 4 * u, 4)
    return units


class Link:

    def __init__(self, eng, sem):
        self.eng, self.sem, self.n, self.off = eng, sem, 0, None

    def __call__(self, ins):
        ins.then_inc(self.sem, 1)
        self.n += 1
        self.eng.wait_ge(self.sem, self.n if self.off is None else self.off + self.n)

    def enter(self, i, per):
        self.start, self.per, self.off = self.n, per, i * per

    def leave(self, trips):
        assert self.n - self.start == self.per, (self.n - self.start, self.per)
        self.n, self.off = self.start + trips * self.per, None


def build(nc, A, out):
    units = weight_plan(A)
    phases = {}
    for n, (phase, slot, _) in enumerate(units):
        phases.setdefault(phase, []).append(n)
    halves, n_halves = {}, 0
    for phase in ("ret_qk", "ret_vg", "up0", "sb_qk", "sb_v", "up1", "mix_in"):
        halves[phase] = n_halves
        n_halves += 2 * len(phases[phase])
    holder, before = [None] * 6, []
    for n, (_, slot, _) in enumerate(units):
        before.append(holder[slot])
        holder[slot] = n

    with ExitStack() as ctx:
        def sb(name, shape, dt=F32):
            return ctx.enter_context(nc.sbuf_tensor(name, shape, dt))

        names = set()

        def sem(name):
            assert name not in names
            names.add(name)
            return ctx.enter_context(nc.semaphore(name))

        ring = [sb(f"ring{s}", [P, KD * C]) for s in range(3)]
        x = sb("x", [P, NT, D])
        xn = sb("xn", [P, NT, D])
        hT = sb("hT", [P, KD, T])
        const = sb("const", [P, NCONST])
        small = sb("small", [P, NSMALL])
        stat = sb("stat", [P, 64])
        credit = sb("credit", [P, 8])
        rowv = sb("rowv", [P, D])
        mods = sb("mods", [P, 4, KD])
        modr = sb("modr", [P, 4 * KD])
        gates = sb("gates", [P, 2, D])
        ARENA = 14912
        arena = sb("arena", [P, ARENA])
        with ExitStack() as split:
            hTh = split.enter_context(nc.sbuf_tensor("h_high", [P, KD, T], F32R))
            hTl = split.enter_context(nc.sbuf_tensor("h_low", [P, KD, T], F32R))
            w_hi = [split.enter_context(nc.sbuf_tensor(f"w_high{i}", [P, KD, T], F32R)) for i in range(2)]
            w_lo = [split.enter_context(nc.sbuf_tensor(f"w_low{i}", [P, KD, T], F32R)) for i in range(2)]
        ring += [sb(f"ring{s}", [P, KD * C]) for s in range(3, 6)]
        wide = [r[:, :].rearrange("p (k n) -> p k n", k=KD) for r in ring]
        tall = [r[:, :].rearrange("p (k n) -> p k n", k=4) for r in ring]

        def carve(start, *dims):
            n = int(np.prod(dims))
            assert start + n <= ARENA, (start, dims)
            v = arena[:, start:start + n]
            if len(dims) == 2:
                v = v.rearrange("p (a b) -> p a b", a=dims[0])
            if len(dims) == 3:
                v = v.rearrange("p (a b c) -> p a b c", a=dims[0], b=dims[1])
            return v

        ps = ctx.enter_context(nc.psum_tensor("ps", [P, 8, C], F32))

        def k_(name):
            a, b = CONST[name]
            return const[:, a:b]

        def s_(name):
            a, b = SMALL[name]
            return small[:, a:b]

        ident, ones, after, before_m, upto = (k_(n) for n in ("ident", "ones", "after", "before", "upto"))
        iota = k_("iota")

        ring_in = [sem(f"ring_in{s}") for s in range(6)]
        x_in, ident_in, const_in, small_in, row_in = sem("x_in"), sem("ident_in"), sem("const_in"), sem("small_in"), sem("row_in")
        out_done = sem("out_done")
        x_new = sem("x_new")
        dve_chain, act_chain, over_chain = sem("dve_chain"), sem("act_chain"), sem("over_chain")
        norm_ss, norm_ms, norm_sd, norm_xn = sem("norm_ss"), sem("norm_ms"), sem("norm_sd"), sem("norm_xn")
        norm_tr, norm_ha, norm_hv = sem("norm_tr"), sem("norm_ha"), sem("norm_hv")
        norm_hi, norm_lo = sem("norm_high"), sem("norm_low")
        hi_done, lo_done, wide_mm = sem("hi_done"), sem("lo_done"), sem("wide_mm")

        def update(k):
            return 4 * (k + 1)

        block = ctx.enter_context(nc.Block())

        b_ada = s_("b_ada")
        norm_src = [
            ((x_in, 16, 0), s_("ret_norm"), None),
            ((x_new, update(0), 2), s_("ffn_norm")[:, 0:KD], None),
            ((x_new, update(1), 2), s_("sb_norm"), None),
            ((x_new, update(2), 2), s_("ffn_norm")[:, KD:2 * KD], None),
            ((x_new, update(3), 2), None, None),
            ((x_new, update(3) + 2, 1), mods[:, 0, :], mods[:, 1, :]),
            ((x_new, update(4) + 2, 2), mods[:, 2, :], mods[:, 3, :]),
            ((x_new, update(5) + 2, 0), None, None),
        ]
        N_TR = [0, 1, 2, 3, None, 4, 5, None]

        def norm_act(act, r):
            s, whole, tile = norm_src[r][0]
            nc.scalar.activation(credit[:, 7:8], small[:, 0:1], ACT.Sqrt)
            for t in range(NT):
                act.wait_ge(s, whole if t else whole - tile)
                nc.scalar.activation(xn[:, t, :], x[:, t, :], ACT.Square,
                                     accum_out=stat[:, t:t + 1]).then_inc(norm_ss, 1)
            act.wait_ge(norm_ms, r + 1)
            nc.scalar.activation(stat[:, 4:6], stat[:, 2:4], ACT.Sqrt).then_inc(norm_sd, 1)

        def norm_dve(dve, link, r):
            dve.wait_ge(norm_ss, NT * (r + 1))
            nc.vector.tensor_scalar(stat[:, 2:4], stat[:, 0:2], 1.0 / D, EPS, ALU.mult, ALU.add)\
                .then_inc(norm_ms, 1)
            dve.wait_ge(norm_sd, r + 1)
            link(nc.vector.reciprocal(stat[:, 6:8], stat[:, 4:6]))
            if N_TR[r] is None:
                return
            for t in range(NT):
                nc.vector.tensor_scalar(xn[:, t, :], x[:, t, :], stat[:, 6 + t:7 + t], None, ALU.mult)\
                    .then_inc(norm_xn, 1)

        def norm_pe(pe, r):
            n = N_TR[r]
            pe.wait_ge(norm_xn, NT * (n + 1))
            for j in range(4):
                for k in (2 * j, 2 * j + 1):
                    for t in range(NT):
                        last = nc.tensor.transpose(ps[:, j, (k % 2) * T + t * P:(k % 2) * T + (t + 1) * P],
                                                   xn[:, t, k * P:(k + 1) * P], ident)
                last.then_inc(norm_tr, 1)

        def split_norm(eng, r, which):
            n, (_, g, b) = N_TR[r], norm_src[r]
            if b is not None:
                norm_evict(eng, r, which)
                eng.wait_ge(norm_ha, 2 * (n - N_TR[5] + 1))
                eng.wait_ge(norm_hv, 2 * (n - N_TR[5] + 1))
            for j in range(4):
                if b is None and which == 0:
                    eng.wait_ge(norm_tr, 4 * n + j + 1)
                if which:
                    eng.wait_ge(norm_hi, 4 * n + j + 1)
                if b is not None:
                    ks = slice(2 * j, 2 * j + 2)
                    if which == 0:
                        last = nc.scalar.activation(hTh[:, ks, :], hT[:, ks, :], ACT.Copy)
                    else:
                        last = nc.vector.tensor_tensor(hTl[:, ks, :], hT[:, ks, :], hTh[:, ks, :].bitcast(F32),
                                                       ALU.subtract)
                else:
                    for k in (2 * j, 2 * j + 1):
                        src = ps[:, j, (k % 2) * T:(k % 2 + 1) * T]
                        if which == 0:
                            last = nc.scalar.activation(hTh[:, k, :], src, ACT.Identity, scale=g[:, k:k + 1])
                        else:
                            last = nc.vector.scalar_tensor_tensor(
                                out=hTl[:, k, :], in0=src, scalar=g[:, k:k + 1], in1=hTh[:, k, :].bitcast(F32),
                                op0=ALU.mult, op1=ALU.subtract)
                last.then_inc(norm_lo if which else norm_hi, 1)

        def norm_evict(eng, r, which):
            n, (_, g, b) = N_TR[r], norm_src[r]
            for j in (which, which + 2):
                eng.wait_ge(norm_tr, 4 * n + j + 1)
                for k in (2 * j, 2 * j + 1):
                    src = ps[:, j, (k % 2) * T:(k % 2 + 1) * T]
                    if which == 0:
                        last = nc.scalar.activation(hT[:, k, :], src, ACT.Identity, scale=g[:, k:k + 1],
                                                    bias=b[:, k:k + 1])
                    else:
                        last = nc.vector.tensor_scalar(hT[:, k, :], src, g[:, k:k + 1], b[:, k:k + 1],
                                                       ALU.mult, ALU.add)
                last.then_inc(norm_hv if which else norm_ha, 1)

        def normed(pe, r):
            pe.wait_ge(norm_lo, 4 * (N_TR[r] + 1))

        def normed_whole(pe, r):
            pe.wait_ge(norm_ha, 2 * (r - 4))
            pe.wait_ge(norm_hv, 2 * (r - 4))

        def arrivals(n):
            slot = units[n][1]
            return 16 * sum(len(units[m][2]) for m in range(n + 1) if units[m][1] == slot)

        last_fill = [arrivals(holder[s]) if s < 3 else 0 for s in range(6)]

        def arrived(eng, n):
            eng.wait_ge(ring_in[units[n][1]], arrivals(n))

        def half_of(slot, j, up):
            if up:
                return ring[slot][:, :].rearrange("p (k g j n) -> p k g j n", k=KD, g=2, j=2)[:, :, :, j, :]
            return wide[slot][:, :, j * T:(j + 1) * T]

        def part(buf, up, k0, k1):
            v = buf[:, k0:k1, :]
            return v.rearrange("p k (g n) -> p k g n", g=2) if up else v

        def split_high(act, phase, h, i=None, per=0):
            u, j, up = h // 2, h % 2, phase.startswith("up")
            n = phases[phase][u]
            slot, off = units[n][1], (0 if i is None else i * (per // 4 * 16 * len(units[n][2])))
            m = halves[phase] + h
            act.wait_ge(ring_in[slot], off + arrivals(n))
            if m >= 2:
                act.wait_ge(wide_mm, (m - 1) if i is None else i * per + (m - 1))
            for k0 in (0, KD // 2):
                nc.scalar.activation(part(w_hi[m % 2], up, k0, k0 + KD // 2), half_of(slot, j, up)[:, k0:k0 + KD // 2],
                                     ACT.Copy).then_inc(hi_done, 1)

        def split_low(dve, phase, h, i=None, per=0):
            u, j, up = h // 2, h % 2, phase.startswith("up")
            n, m = phases[phase][u], halves[phase] + h
            slot = units[n][1]
            for c, k0 in enumerate((0, KD // 2)):
                ks = (k0, k0 + KD // 2)
                dve.wait_ge(hi_done, (2 * m + c + 1) if i is None else i * (2 * per) + (2 * m + c + 1))
                last = nc.vector.tensor_tensor(part(w_lo[m % 2], up, *ks), half_of(slot, j, up)[:, ks[0]:ks[1]],
                                               part(w_hi[m % 2], up, *ks).bitcast(F32), ALU.subtract)
            last.then_inc(lo_done, 1)

        def split_first(split, eng, phase):
            for h in range(2):
                split(eng, phase, h)

        def wide_done(eng, count, i=None, per=0):
            eng.wait_ge(wide_mm, count if i is None else i * per + count)

        def split_ready(pe, phase, h, i=None, per=0):
            m = halves[phase] + h
            pe.wait_ge(lo_done, (m + 1) if i is None else i * per + (m + 1))
            return m % 2

        def by_feature(bank, buf):
            for f in range(2):
                o = ps[:, bank, f * T:(f + 1) * T]
                for k in range(KD):
                    hi, lo = w_hi[buf][:, k, f * P:(f + 1) * P], w_lo[buf][:, k, f * P:(f + 1) * P]
                    nc.tensor.matmul(o, hi, hTh[:, k, :], start=(k == 0), stop=False)
                    nc.tensor.matmul(o, hi, hTl[:, k, :], start=False, stop=False)
                    last = nc.tensor.matmul(o, lo, hTh[:, k, :], start=False, stop=(k == KD - 1))
            return last

        def by_token(bank, buf, c):
            for t in range(NT):
                o = ps[:, bank + t, c * T:(c + 1) * T]
                for k in range(KD):
                    hi, lo = hTh[:, k, t * P:(t + 1) * P], hTl[:, k, t * P:(t + 1) * P]
                    nc.tensor.matmul(o, hi, w_hi[buf][:, k, :], start=(k == 0), stop=False)
                    nc.tensor.matmul(o, hi, w_lo[buf][:, k, :], start=False, stop=False)
                    last = nc.tensor.matmul(o, lo, w_hi[buf][:, k, :], start=False, stop=(k == KD - 1))
            return last

        def project(pe, phase, src, chunks, done):
            k = 0
            for i, n in enumerate(phases[phase]):
                arrived(pe, n)
                slot = units[n][1]
                for kc in range(min(4, chunks - k)):
                    for t in range(NT):
                        for half in range(2):
                            last = nc.tensor.matmul(ps[:, 4 + 2 * t + half, :], src[:, k, t * P:(t + 1) * P],
                                                    tall[slot][:, kc, half * C:(half + 1) * C],
                                                    start=(k == 0), stop=(k == chunks - 1))
                    k += 1
                last.then_inc(done, 1)

        def gated_residual(link, g, bank, tmp, signal):
            for t in range(NT):
                for half in range(2):
                    last = nc.vector.tensor_tensor(tmp[:, t, half * C:(half + 1) * C], ps[:, bank + 2 * t + half, :],
                                                   gates[:, g, half * C:(half + 1) * C], ALU.mult)
            link(last)
            for t in range(NT):
                ins = nc.vector.tensor_tensor(x[:, t, :], x[:, t, :], tmp[:, t, :], ALU.add)
                if signal:
                    ins.then_inc(x_new, 2)
            if not signal:
                link(ins)

        def residual(dve, done, n):
            dve.wait_ge(done, n)
            for t in range(NT):
                for half in range(2):
                    xs = x[:, t, half * C:(half + 1) * C]
                    nc.vector.tensor_tensor(xs, ps[:, 4 + 2 * t + half, :], xs, ALU.add).then_inc(x_new, 1)

        freed = {}

        def free_by(phase, s, per, base=0):
            for i, n in enumerate(phases[phase]):
                freed[n] = (s, base + per * (i + 1))

        for phase, m in halves.items():
            free_by(phase, lo_done, 2, m)

        qk = carve(0, 8, C)
        vg = carve(4096, NT, 2 * RV)
        yT = carve(0, 2 * KD, T)
        rot_a, rot_b = xn[:, 0, 0:C], xn[:, 0, C:2 * C]
        r_sc = carve(12288, 2, TRI)
        rqk_free, rqk_out = sem("rqk_free"), sem("rqk_out")
        rvg_fa, rvg_fv = sem("rvg_fa"), sem("rvg_fv")
        rg_silu = sem("rg_silu")
        r_s, r_d, r_o, r_sq, r_ms, r_sd, r_y, r_t, r_ta, r_tv, rout_mm = (
            sem("r_" + n) for n in ("scores", "decayed", "o", "squares", "means", "roots", "y", "turned",
                                    "yT_a", "yT_v", "out_mm"))
        free_by("ret_out", rout_mm, 1)

        hff = carve(0, FP, T)
        cv = carve(5632, 2, C)
        ada_w = [carve(6656, 4, C), gates[:, :, :].rearrange("p a (b n) -> p (a b) n", n=C)]
        ada_acc = carve(8704, 12 * C)
        ADA_POOL = 6
        up_id, up_cv, up_free, up_si, up_h, down_mm = (
            sem("up_" + n) for n in ("identity", "convolved", "free", "silu", "h", "down_mm"))
        for l in range(2):
            free_by(f"down{l}", down_mm, 1, 6 * l)
        ada_in = [sem("ada_in0"), sem("ada_in1")]
        ada_chain, ada_used, ada_sum, ada_mods, ada_gate, ada_c, bias_in = (
            sem("ada_" + n) for n in ("chain", "used", "sum", "mods", "gate", "c", "bias_in"))

        sqk = carve(0, 8, C)
        sqk_t = sqk.rearrange("p a (b t) -> p (a b) t", b=2)
        sv = carve(4096, NT, D)
        z_b = [carve(6144 + 768 * i, 2, TRI) for i in range(2)]
        l_b = [carve(7680 + 768 * i, 2, TRI) for i in range(2)]
        sp_b = [carve(9216 + 768 * i, 2, TRI) for i in range(2)]
        a_b = [carve(10752 + 768 * i, 2, TRI) for i in range(2)]
        soT = carve(12288, KD, T)
        sqk_fa, sqk_fv, sv_a, sv_v = (
            sem("s_" + n) for n in ("qk_fa", "qk_fv", "v_a", "v_v"))
        s_z, s_zc, s_l, s_sp, s_m1, s_ex, s_la, s_a, s_m2, s_o, s_ot, sout_mm = (
            sem("s_" + n) for n in ("z", "zcopy", "log", "softplus", "masked", "excl", "log_a", "a", "a_masked",
                                    "o", "oT", "out_mm"))
        free_by("sb_out", sout_mm, 1)

        qkm = carve(0, 2 * LH, T)
        qka = carve(2048, 2 * MH // 2, T)
        vm = carve(4096, NT, LH * (LDH + 1))
        om = carve(5128, NT, C)
        va = carve(6152, NT, C)
        hm = carve(7176, NT, C)
        mixT = xn[:, :, :].rearrange("p a (b t) -> p (a b) t", t=T)
        cvm = carve(8200, 2, T)
        w8 = carve(8712, KD, 8)
        bg = carve(8776, 4)
        ghead = carve(8780, C)
        rows4 = carve(9292, 9, T)
        acol = carve(11596, NT, 4)
        fcol = carve(11604, NT, 4)
        sel4 = carve(11612, 4, P)
        wt = carve(12124, 2, TRI)
        pt = carve(12892, 2, TRI)
        m_sc = carve(13660, 2, TRI)
        mst = carve(14428, 128)
        mi_id, mi_cv, mi_si, mi_ev_a, mi_ev_v, mi_g = (
            sem("mi_" + n) for n in ("identity", "convolved", "silu", "ev_a", "ev_v", "gates"))
        mix_small = sem("mix_small")
        MIX = 2 * len(phases["mix_in"])
        l_f, l_floor, l_ln, l_rows, l_tr, l_cols, l_sig = (
            sem("l_" + n) for n in ("forget", "floor", "ln", "rows", "turned", "cols", "sigmoid"))
        l_s, l_w, l_e, l_p, l_o, l_h, l_sq, l_ms, l_sd, l_hn, l_t, l_mt = (
            sem("l_" + n) for n in ("scores", "w", "expw", "p", "o", "h", "squares", "means", "roots", "hn",
                                    "hT", "mixT"))
        b_s, b_mx, b_e, b_p, b_t, b_tc, b_o, b_oc, mo_mm = (
            sem("b_" + n) for n in ("scores", "max", "exp", "p", "pT", "pT_copy", "o", "oT", "mo_mm"))
        free_by("mix_out", mo_mm, 1)

        EP = NE + 4
        wr = carve(14560, KD, NG + NE)
        br = carve(14848, NG + NE)
        lg = carve(324, NT, NG + NE)
        g8 = carve(396, NT, 8)
        m8 = carve(412, NT, 8)
        i8 = carve(428, NT, 8).bitcast(U32)
        f8 = carve(444, NT, 8)
        oh = carve(460, NT, NG)
        em = carve(476, NT, NE)
        oh1 = carve(540, NT, NE)
        oh2 = carve(604, NT, NE)
        asg = carve(668, NT, NE)
        wgt = carve(732, NT, EP)
        pos = carve(804, NT, EP)
        rst = carve(876, 64)
        flag = carve(940, 1).bitcast(I32)
        sel = carve(1024, NT, P)
        selw = carve(1280, NT, P)
        selT = carve(1536, T)
        gtmp = carve(4864, NT, D)
        xg = carve(1792, KD, P)
        hs = carve(2816, DE)
        hg = carve(3328, DE)
        hgT = carve(6912, KE, P)
        ye = carve(3840, D)
        r_in, t_lg, t_rank, t_flag, t_top, t_exp = (sem("t_" + n) for n in ("router_in", "logits", "rank", "flag", "top", "exp"))
        m_zero, m_start, m_s, m_sw, m_ga, m_xa, m_xv, m_gu, m_si, m_h, m_ht, m_hc, m_tr, m_sct, m_swt, m_dn, m_ya, m_yv = (
            sem("m_" + n) for n in ("zeroed", "started", "select", "select_w", "gathered", "xg_a", "xg_v", "gate_up",
                                    "silu", "h", "h_turned", "hT", "turned", "scattered", "selT", "down", "y_a", "y_v"))

        @block.sync
        def _(sp):
            sp.dma_start(x[:, :, :], A["x"][0].rearrange("(t p) d -> p t d", p=P)).then_inc(x_in, 16)
            sp.dma_start(const[:, 0:P], A["const"][:, 0:P]).then_inc(ident_in, 16)
            sp.dma_start(small[:, :], A["small"]).then_inc(small_in, 16)

            def fill(n):
                _, slot, parts = units[n]
                return [sp.dma_start(wide[slot][:, :, part[1][0]:part[1][1]] if part[0] is not None
                                     else tall[slot][:, 0:part[1], :], part[2]) for part in parts]

            for n in range(len(units)):
                if before[n] is not None:
                    sp.wait_ge(*freed[before[n]])
                if n == 1:
                    sp.dma_start(const[:, P:], A["const"][:, P:]).then_inc(const_in, 16)
                _, slot, parts = units[n]
                if len(parts) == 1:
                    fill(n)[0].then_inc(ring_in[slot], 16)
                else:
                    for half, d in enumerate(fill(n)):
                        d.then_inc(ring_in[slot], 16)

            def expert_unit(slot, e):
                name, shape = (("w_expert_gate_2", 0), ("w_expert_up_2", 0), ("w_expert_down_2", 1))[slot % 3]
                w = A[name][0]
                if shape:
                    src = w[bass.ds(e, 1)].rearrange("a (k p) n -> p (a k) n", p=P)
                    sp.dma_start(tall[slot][:, :, :], src).then_inc(ring_in[slot], 16)
                else:
                    src = w[bass.ds(e, 1)].rearrange("a (k p) n -> p (a k) n", p=P)
                    sp.dma_start(wide[slot][:, :, :], src).then_inc(ring_in[slot], 16)

            LOADS = (0, 3, 1, 4, 2, 5)

            def expert_pairs(r):
                def one(i, first):
                    for slot in (3, 4, 5, 2, 0, 1) if first else LOADS:
                        if first and slot >= 3:
                            sp.wait_ge(wide_mm, n_halves)
                        elif first:
                            sp.wait_ge(*freed[holder[slot]])
                        elif slot % 3 < 2:
                            sp.wait_ge(m_gu, i * 2 + (PAIRS * 2 * r - 1 + slot % 3))
                        else:
                            sp.wait_ge(m_dn, i + PAIRS * r)
                        expert_unit(slot, i * 2 + slot // 3)
                if r == 0:
                    one(0, True)
                with sp.Fori(1 if r == 0 else 0, PAIRS) as i:
                    one(i, False)

            expert_pairs(0)
            sp.wait_ge(t_flag, 1)
            most = sp.value_load(flag[0:1, 0:1])
            with sp.If(most > R):
                for r in range(1, PASSES):
                    expert_pairs(r)
            sp.wait_ge(x_new, update(5) + 4)
            sp.dma_start(out[0].rearrange("(t p) d -> p t d", p=P), x[:, :, :]).then_inc(out_done, 16)
            sp.wait_ge(out_done, 16)

        @block.gpsimd
        def _(pool):
            pool.dma_start(rowv[:, :], A["final_norm"].rearrange("(a d) -> a d", a=1).broadcast_to([P, D]))\
                .then_inc(row_in, 16)
            w_ada = A["w_ada_2"][0].rearrange("(p c) n -> p c n", p=P)
            pool.wait_ge(x_new, update(0))
            for kh in range(2):
                pool.dma_start(ada_w[kh], w_ada[:, 4 * kh:4 * kh + 4, 0:C]).then_inc(ada_in[kh], 16)
            pool.wait_ge(ada_c, 1)

            def ada_load(nb, kh):
                pool.dma_start(ada_w[kh], w_ada[:, 4 * kh:4 * kh + 4, bass.ds(nb * C, C)]).then_inc(ada_in[kh], 16)

            n = 0
            for nb in range(ADA_POOL):
                for kh, w in enumerate(ada_w):
                    acc = ada_acc[:, nb * C:(nb + 1) * C]
                    scale = stat[:, 16 + 4 * kh:20 + 4 * kh].unsqueeze(2).broadcast_to([P, 4, C])
                    pool.wait_ge(ada_in[kh], nb * 16 + 16)
                    steps = [(w, w, scale, ALU.mult), (w[:, 0:2, :], w[:, 0:2, :], w[:, 2:4, :], ALU.add)]
                    if kh == 0:
                        steps += [(acc, w[:, 0, :], w[:, 1, :], ALU.add)]
                    else:
                        steps += [(w[:, 0, :], w[:, 0, :], w[:, 1, :], ALU.add), (acc, acc, w[:, 0, :], ALU.add)]
                    for o, in0, in1, op in steps:
                        nc.gpsimd.tensor_tensor(o, in0, in1, op).then_inc(ada_chain, 1)
                        n += 1
                        pool.wait_ge(ada_chain, n)
                    ada_load(nb + 1, kh)
            nc.gpsimd.memset(credit[:, 1:2], 0.0).then_inc(ada_sum, 1)
            with pool.Fori(ADA_POOL + 1, 12) as nb:
                for kh in range(2):
                    pool.wait_ge(ada_used, nb * 2 + (kh + 1 - 2 * (ADA_POOL + 1)))
                    ada_load(nb, kh)
            pool.wait_ge(ada_used, 2 * (12 - ADA_POOL))
            for g, m in enumerate((2, 5)):
                pool.dma_start(gates[:, g, :], A["b_ada_2"][0:1, m * D:(m + 1) * D].broadcast_to([P, D]))\
                    .then_inc(bias_in, 16)

            def mask(buf, g, ready, done):
                pool.wait_ge(ready, g + 1)
                diag = buf[:, :, :].rearrange("p h (b t) -> p h b t", b=3)[:, :, 0:3:2, :]
                m = before_m.unsqueeze(1).unsqueeze(1).broadcast_to([P, 2, 2, P])
                nc.gpsimd.tensor_tensor(diag, diag, m, ALU.mult).then_inc(done, 1)

            pool.wait_ge(const_in, 16)
            for g in range(SH // 2):
                if g == 0:
                    mask(sp_b[0], 0, s_sp, s_m1)
                    mask(sp_b[1], 1, s_sp, s_m1)
                mask(a_b[g % 2], g, s_a, s_m2)
                if g + 2 < SH // 2:
                    mask(sp_b[g % 2], g + 2, s_sp, s_m1)

            pool.wait_ge(x_new, update(2))
            pool.dma_start(w8, A["w_in_2"][0].rearrange("(k p) n -> p k n", p=P)[:, :, 4 * LH * LDH:4 * LH * LDH + 8])\
                .then_inc(mix_small, 16)
            pool.dma_start(bg[0:LH, 0:1], A["b_gates_2"][0:1, 0:LH].rearrange("a h -> h a")).then_inc(mix_small, 16)
            pool.dma_start(bg[0:LH, 1:2], A["b_gates_2"][0:1, LH:2 * LH].rearrange("a h -> h a")).then_inc(mix_small, 16)
            pool.dma_start(ghead, A["g_mlstm_head_2"][0:1, :].broadcast_to([P, C])).then_inc(mix_small, 16)
            pool.dma_start(sel4[0:LH, :, :].rearrange("p a b -> p (a b)"), A["sel4"]).then_inc(mix_small, 16)
            pool.dma_start(wr[:, :, 0:NG], A["w_router_group_2"][0].rearrange("(k p) n -> p k n", p=P)).then_inc(r_in, 16)
            pool.dma_start(wr[:, :, NG:], A["w_router_expert_2"][0].rearrange("(k p) n -> p k n", p=P)).then_inc(r_in, 16)
            pool.dma_start(br[:, 0:NG], A["b_router_group_2"][0:1, :].broadcast_to([P, NG])).then_inc(r_in, 16)
            pool.dma_start(br[:, NG:], A["b_router_expert_2"][0:1, :].broadcast_to([P, NE])).then_inc(r_in, 16)
            pool.wait_ge(x_new, update(3) + 2)
            pool.dma_start(rowv[:, :], A["g_final_2"].rearrange("(a d) -> a d", a=1).broadcast_to([P, D]))\
                .then_inc(row_in, 16)

        @block.tensor
        def _(pe):
            pe.wait_ge(ident_in, 16)
            norm_pe(pe, 0)
            normed(pe, 0)

            with pe.Fori(0, 2) as i:
                for h in range(4):
                    buf = split_ready(pe, "ret_qk", h, i, 4)
                    pe.wait_ge(rqk_free, i * 4 + (h + 1))
                    by_feature(h, buf).then_inc(wide_mm, 1)
            with pe.Fori(0, 4) as i:
                for b in range(2):
                    pe.wait_ge(rvg_fa, i * 2 + (b + 1))
                    pe.wait_ge(rvg_fv, i * 2 + (b + 1))
                    for c in range(2):
                        buf = split_ready(pe, "ret_vg", 2 * b + c, i, 4)
                        by_token(2 * b + 4, buf, c).then_inc(wide_mm, 1)

            def ret_scores(h):
                if h >= 2:
                    pe.wait_ge(r_d, h - 1)
                for f in range(2):
                    nc.tensor.matmul(ps[:, h % 2, 0:T], qk[:, RH + h, f * T:f * T + P], qk[:, h, f * T:(f + 1) * T],
                                     start=(f == 0), stop=(f == 1))
                for f in range(2):
                    last = nc.tensor.matmul(ps[:, h % 2, T:TRI], qk[:, RH + h, f * T + P:(f + 1) * T],
                                            qk[:, h, f * T + P:(f + 1) * T], start=(f == 0), stop=(f == 1))
                last.then_inc(r_s, 1)

            def ret_out(h):
                pe.wait_ge(r_d, h + 1)
                if h >= 2:
                    pe.wait_ge(r_y, 2 * (h - 1))
                sc, v = r_sc[:, h % 2, :], vg[:, :, h * RDV:(h + 1) * RDV]
                ob = 2 + 2 * (h % 2)
                nc.tensor.matmul(ps[:, ob, :], sc[:, 0:P], v[:, 0, :], start=True, stop=True).then_inc(r_o, 1)
                nc.tensor.matmul(ps[:, ob + 1, :], sc[:, P:T], v[:, 0, :], start=True, stop=False)
                nc.tensor.matmul(ps[:, ob + 1, :], sc[:, T:TRI], v[:, 1, :], start=False, stop=True).then_inc(r_o, 1)

            def ret_turn(h):
                pe.wait_ge(r_y, 2 * (h + 1))
                for j in range(2):
                    if h >= 1:
                        pe.wait_ge(r_tv if j else r_ta, h)
                    for f in range(2):
                        for t in range(NT):
                            last = nc.tensor.transpose(
                                ps[:, 6 + j, f * T + t * P:f * T + (t + 1) * P],
                                vg[:, t, RV + h * RDV + (2 * j + f) * P:RV + h * RDV + (2 * j + f + 1) * P], ident)
                    last.then_inc(r_t, 1)

            pe.wait_ge(rqk_out, 8)
            ret_scores(0)
            ret_scores(1)
            pe.wait_ge(rvg_fa, 2 + 8)
            pe.wait_ge(rvg_fv, 2 + 8)
            for h in range(RH):
                ret_out(h)
                if h + 2 < RH:
                    ret_scores(h + 2)
                if h >= 1:
                    ret_turn(h - 1)
            ret_turn(RH - 1)
            pe.wait_ge(r_ta, RH)
            pe.wait_ge(r_tv, RH)
            project(pe, "ret_out", yT, 2 * KD, rout_mm)

            def ffn(l):
                normed(pe, 2 * l + 1)

                with pe.Fori(0, 5) as i:
                    for h in range(4):
                        buf = split_ready(pe, f"up{l}", h, i, 4)
                        pe.wait_ge(up_free, i * 4 + ((FP + 4) * l + h + 1))
                        by_feature(h, buf).then_inc(wide_mm, 1)
                for h in (20, 21):
                    buf = split_ready(pe, f"up{l}", h)
                    pe.wait_ge(up_free, (FP + 4) * l + h + 1)
                    by_feature(h % 4, buf).then_inc(wide_mm, 1)
                pe.wait_ge(up_h, FP * (l + 1))
                project(pe, f"down{l}", hff, FP, down_mm)

            norm_pe(pe, 1)
            ffn(0)

            pe.wait_ge(const_in, 16)
            pe.wait_ge(ada_sum, 2)
            pe.wait_ge(x_new, update(1))
            for m, q in enumerate((0, 1, 3, 4)):
                for k in range(KD):
                    last = nc.tensor.matmul(ps[:, 3, m * KD + k:m * KD + k + 1],
                                            ada_acc[:, q * D + k * P:q * D + (k + 1) * P], ones[:, 0:1],
                                            start=True, stop=True)
            last.then_inc(ada_mods, 1)
            for g, q in enumerate((2, 5)):
                for half in range(2):
                    last = nc.tensor.matmul(ps[:, 4 + 2 * g + half, :], ones,
                                            ada_acc[:, q * D + half * C:q * D + (half + 1) * C],
                                            start=True, stop=True)
            last.then_inc(ada_mods, 1)
            pe.wait_ge(ada_gate, 1)
            norm_pe(pe, 2)
            normed(pe, 2)

            with pe.Fori(0, 2) as i:
                for h in range(4):
                    buf = split_ready(pe, "sb_qk", h, i, 4)
                    pe.wait_ge(sqk_fv if h % 2 else sqk_fa, i * 2 + (h // 2 + 1))
                    by_feature(h, buf).then_inc(wide_mm, 1)
            pe.wait_ge(ada_gate, 5)
            for h in range(4):
                buf = split_ready(pe, "sb_v", h)
                by_token(4 + 2 * (h // 2), buf, h % 2).then_inc(wide_mm, 1)

            def sb_z(g):
                if g == 0:
                    pe.wait_ge(sqk_fa, 2 + 4)
                    pe.wait_ge(sqk_fv, 2 + 4)
                if g >= 2:
                    pe.wait_ge(s_zc, g - 1)
                for hh in range(2):
                    rows = slice(hh * SDH, (hh + 1) * SDH)
                    q, k = sqk_t[rows, g, :], sqk_t[rows, KD + g, :]
                    bank = 2 * (g % 2) + hh
                    nc.tensor.matmul(ps[:, bank, 0:T], k[:, 0:P], q, start=True, stop=True)
                    last = nc.tensor.matmul(ps[:, bank, T:TRI], k[:, P:T], q[:, P:T], start=True, stop=True)
                last.then_inc(s_z, 1)

            def sb_excl(g):
                pe.wait_ge(s_m1, g + 1)
                if g == 0:
                    pe.wait_ge(sv_a, 2)
                    pe.wait_ge(sv_v, 2)
                else:
                    pe.wait_ge(s_la, g)
                for hh in range(2):
                    sp = sp_b[g % 2][:, hh, :]
                    nc.tensor.matmul(ps[:, 4 + hh, 0:T], after, sp[:, 0:T], start=True, stop=False)
                    nc.tensor.matmul(ps[:, 4 + hh, P:T], ones, sp[:, T:TRI], start=False, stop=True)
                    last = nc.tensor.matmul(ps[:, 4 + hh, T:TRI], after, sp[:, T:TRI], start=True, stop=True)
                last.then_inc(s_ex, 1)

            def sb_o(g):
                pe.wait_ge(s_m2, g + 1)
                if g >= 2:
                    pe.wait_ge(s_ot, g - 1)
                for hh in range(2):
                    h = 2 * g + hh
                    a = a_b[g % 2][:, hh, :]
                    o = ps[hh * SDH:(hh + 1) * SDH, 6 + g % 2, :]
                    nc.tensor.matmul(o[:, 0:T], sv[:, 0, h * SDH:(h + 1) * SDH], a[:, 0:T], start=True, stop=False)
                    last = nc.tensor.matmul(o[:, P:T], sv[:, 1, h * SDH:(h + 1) * SDH], a[:, T:TRI],
                                            start=False, stop=True)
                last.then_inc(s_o, 1)

            sb_z(0)
            sb_z(1)
            for g in range(SH // 2):
                sb_excl(g)
                if g >= 1:
                    sb_o(g - 1)
                if g + 2 < SH // 2:
                    sb_z(g + 2)
            sb_o(SH // 2 - 1)
            pe.wait_ge(s_ot, SH // 2)
            project(pe, "sb_out", soT, KD, sout_mm)

            norm_pe(pe, 3)
            ffn(1)

            norm_pe(pe, 5)
            normed_whole(pe, 5)
            pe.wait_ge(mix_small, 80)
            for g in range(2):
                for k in range(KD):
                    last = nc.tensor.matmul(ps[0:LH, 4 + g, 0:T], w8[:, k, g * LH:(g + 1) * LH], hT[:, k, :],
                                            start=(k == 0), stop=(k == KD - 1))
            last.then_inc(mi_g, 1)
            normed(pe, 5)
            for h in range(MIX):
                buf = split_ready(pe, "mix_in", h)
                if 4 <= h < 8:
                    pe.wait_ge(mi_cv, h - 3)
                if h >= 8 and h % 2 == 0:
                    pe.wait_ge(mi_ev_a, (h - 8) // 2 + 1)
                    pe.wait_ge(mi_ev_v, (h - 8) // 2 + 1)
                if h < 8:
                    by_feature(h % 4, buf).then_inc(wide_mm, 1)
                else:
                    by_token(2 * (h // 2 % 2), buf, h % 2).then_inc(wide_mm, 1)

            pe.wait_ge(l_rows, 1)
            for n, row in enumerate((4, 7)):
                for t in range(NT):
                    last = nc.tensor.transpose(ps[:, 6, (2 * n + t) * 4:(2 * n + t) * 4 + 4],
                                               rows4[0:LH, row, t * P:(t + 1) * P], ident[0:LH, 0:LH])
            last.then_inc(l_tr, 1)
            pe.wait_ge(mi_ev_a, 5)
            pe.wait_ge(mi_ev_v, 5)
            pe.wait_ge(mi_si, 4)

            def ls_scores(h):
                b = 3 * (h % 2)
                if h >= 2:
                    pe.wait_ge(l_p, h - 1)
                nc.tensor.matmul(ps[:, b, 0:T], sel4[0:LH, h, :], rows4[0:LH, 6, :], start=True, stop=True)
                nc.tensor.matmul(ps[:, b + 1, 0:T], qkm[:, LH + h, 0:P], qkm[:, h, :], start=True, stop=True)
                nc.tensor.matmul(ps[:, b + 1, T:TRI], qkm[:, LH + h, P:T], qkm[:, h, P:T], start=True, stop=True)\
                    .then_inc(l_s, 1)

            def ls_out(h):
                b = 3 * (h % 2) + 2
                pe.wait_ge(l_p, h + 1)
                if h >= 2:
                    pe.wait_ge(l_h, h - 1)
                v = vm.rearrange("p t (h e) -> p t h e", h=LH)
                E1 = LDH + 1
                nc.tensor.matmul(ps[:, b, 0:E1], pt[:, h % 2, 0:P], v[:, 0, h, :], start=True, stop=True)
                nc.tensor.matmul(ps[:, b, T:T + E1], pt[:, h % 2, P:T], v[:, 0, h, :], start=True, stop=False)
                nc.tensor.matmul(ps[:, b, T:T + E1], pt[:, h % 2, T:TRI], v[:, 1, h, :], start=False, stop=True)\
                    .then_inc(l_o, 1)

            ls_scores(0)
            ls_scores(1)
            for h in range(LH):
                ls_out(h)
                if h + 2 < LH:
                    ls_scores(h + 2)

            def mb_scores(h):
                if h == 0:
                    pe.wait_ge(l_cols, 1)
                if h >= 2:
                    pe.wait_ge(b_mx, h - 1)
                rows = slice((h % 2) * MDH, (h % 2 + 1) * MDH)
                q, k = qka[rows, h // 2, :], qka[rows, MH // 2 + h // 2, :]
                bank = 6 + h % 2
                nc.tensor.matmul(ps[:, bank, 0:P], q[:, 0:P], k[:, 0:P], start=True, stop=True)
                nc.tensor.matmul(ps[:, bank, P:TRI], q[:, P:T], k, start=True, stop=True).then_inc(b_s, 1)

            def mb_turn(h):
                pe.wait_ge(b_p, h + 1)
                if h >= 2:
                    pe.wait_ge(b_tc, h - 1)
                if h == 0:
                    pe.wait_ge(l_h, LH)
                sc = m_sc[:, h % 2, :]
                for blk in range(3):
                    last = nc.tensor.transpose(ps[:, h % 2, blk * P:(blk + 1) * P], sc[:, blk * P:(blk + 1) * P], ident)
                last.then_inc(b_t, 1)

            def mb_out(h):
                pe.wait_ge(b_tc, h + 1)
                if h >= 4 and h % 2 == 0:
                    pe.wait_ge(b_oc, h // 2 - 1)
                o = ps[(h % 2) * MDH:(h % 2 + 1) * MDH, 3 + (h // 2) % 2, :]
                p_ = wt[:, h % 2, :]
                cols = slice(h * MDH, (h + 1) * MDH)
                nc.tensor.matmul(o[:, 0:T], va[:, 0, cols], p_[:, 0:T], start=True, stop=False)
                nc.tensor.matmul(o[:, P:T], va[:, 1, cols], p_[:, T:TRI], start=False, stop=True).then_inc(b_o, 1)

            mb_scores(0)
            mb_scores(1)
            for h in range(MH):
                mb_turn(h)
                if h >= 1:
                    mb_out(h - 1)
                if h + 2 < MH:
                    mb_scores(h + 2)
            mb_out(MH - 1)

            pe.wait_ge(l_hn, 2 * LH)
            pe.wait_ge(b_tc, MH)
            for j in range(2):
                for f in range(2):
                    for t in range(NT):
                        last = nc.tensor.transpose(ps[:, j, f * T + t * P:f * T + (t + 1) * P],
                                                   hm[:, t, (2 * j + f) * P:(2 * j + f + 1) * P], ident)
                last.then_inc(l_t, 1)
            pe.wait_ge(l_mt, 2)
            pe.wait_ge(b_oc, MH // 2)
            project(pe, "mix_out", mixT, KD, mo_mm)

            norm_pe(pe, 6)
            normed_whole(pe, 6)
            pe.wait_ge(r_in, 64)
            for t in range(NT):
                for k in range(KD):
                    last = nc.tensor.matmul(ps[:, 4, t * 64:t * 64 + NG + NE], hT[:, k, t * P:(t + 1) * P],
                                            wr[:, k, :], start=(k == 0), stop=(k == KD - 1))
            last.then_inc(t_lg, 1)
            pe.wait_ge(t_rank, 1)
            nc.tensor.matmul(ps[:, 5, 0:NE], before_m, asg[:, 0, :], start=True, stop=True)
            nc.tensor.matmul(ps[:, 5, 64:64 + NE], ones, asg[:, 0, :], start=True, stop=False)
            nc.tensor.matmul(ps[:, 5, 64:64 + NE], before_m, asg[:, 1, :], start=False, stop=True)
            nc.tensor.matmul(ps[:, 5, 128:128 + NE], ones, asg[:, 0, :], start=True, stop=False)
            nc.tensor.matmul(ps[:, 5, 128:128 + NE], ones, asg[:, 1, :], start=False, stop=True).then_inc(t_lg, 1)

            def gather(value, hgt):
                pe.wait_ge(m_s, value)
                for half in (1, 0):
                    if half == 0 and hgt is not None:
                        pe.wait_ge(m_hc, hgt)
                    for k in range(4 * half, 4 * half + 4):
                        for t in range(NT):
                            last = nc.tensor.matmul(ps[:, 4 + half, (k % 4) * P:(k % 4 + 1) * P],
                                                    xn[:, t, k * P:(k + 1) * P], sel[:, t, :],
                                                    start=(t == 0), stop=(t == NT - 1))
                    last.then_inc(m_ga, 1)

            def scatter(stop):
                for t in range(NT):
                    for half in range(2):
                        last = nc.tensor.matmul(ps[:, 2 * t + half, :], selT[:, t * P:(t + 1) * P],
                                                ye[:, half * C:(half + 1) * C], start=False, stop=stop,
                                                skip_group_check=True)
                last.then_inc(m_sct, 1)

            def expert_pass(r):
                pe.wait_ge(m_zero, 3 * (r + 1))
                for b in range(4):
                    last = nc.tensor.matmul(ps[:, b, :], selT[:, 0:P], ye[:, 0:C], start=True, stop=False,
                                            skip_group_check=True)
                last.then_inc(m_start, 1)
                gather((PAIRS + 2) * r + 1, None)
                with pe.Fori(0, PAIRS) as i:
                    pe.wait_ge(m_xa, i + ((PAIRS + 1) * r + 1))
                    pe.wait_ge(m_xv, i + ((PAIRS + 1) * r + 1))
                    for g in range(2):
                        for s in (g, 3 + g):
                            pe.wait_ge(ring_in[s], i * 16 + (last_fill[s] + 16 * (PAIRS * r + 1)))
                        for k in range(KD):
                            for e in range(2):
                                last = nc.tensor.matmul(ps[e * R:(e + 1) * R, 4 + g, :], xg[:, k, e * R:(e + 1) * R],
                                                        wide[3 * e + g][:, k, :], start=(k == 0), stop=(k == KD - 1))
                        last.then_inc(m_gu, 1)
                    pe.wait_ge(m_sw, i + ((PAIRS + 1) * r + 1))
                    pe.wait_ge(m_ya, i + ((PAIRS + 1) * r + 1))
                    for t in range(NT):
                        last = nc.tensor.transpose(ps[:, 6, t * P:(t + 1) * P], selw[:, t, :], ident)
                    last.then_inc(m_tr, 1)
                    pe.wait_ge(m_yv, i + ((PAIRS + 1) * r + 1))
                    scatter(False)
                    pe.wait_ge(m_h, i + (PAIRS * r + 1))
                    for k in range(KE):
                        last = nc.tensor.transpose(ps[:, 4, k * P:(k + 1) * P], hg[:, k * P:(k + 1) * P], ident)
                    last.then_inc(m_ht, 1)
                    gather(i + ((PAIRS + 2) * r + 2), i + (PAIRS * r + 1))
                    pe.wait_ge(m_swt, i + (PAIRS * r + 1))
                    for s in (2, 5):
                        pe.wait_ge(ring_in[s], i * 16 + (last_fill[s] + 16 * (PAIRS * r + 1)))
                    for half in range(2):
                        for k in range(KE):
                            for e in range(2):
                                last = nc.tensor.matmul(ps[e * R:(e + 1) * R, 6 + half, :],
                                                        hgT[:, k, e * R:(e + 1) * R],
                                                        tall[3 * e + 2][:, k, half * C:(half + 1) * C],
                                                        start=(k == 0), stop=(k == KE - 1))
                    last.then_inc(m_dn, 1)
                pe.wait_ge(m_ya, (PAIRS + 1) * (r + 1))
                pe.wait_ge(m_yv, (PAIRS + 1) * (r + 1))
                scatter(True)

            expert_pass(0)
            pe.wait_ge(t_flag, 1)
            most = pe.value_load(flag[0:1, 0:1])
            with pe.If(most > R):
                for r in range(1, PASSES):
                    expert_pass(r)

        @block.scalar
        def _(act):
            link = Link(act, act_chain)
            act.wait_ge(small_in, 16)
            norm_act(act, 0)
            split_norm(act, 0, 0)
            nc.scalar.activation(credit[:, 3:4], small[:, 0:1], ACT.Copy).then_inc(rvg_fa, 2)
            split_high(act, "ret_qk", 0)
            split_high(act, "ret_qk", 1)
            with act.Fori(0, 2) as i:
                for h in range(4):
                    split_high(act, "ret_qk", h + 2, i, 4)

            def v_group(i, more):
                for h in range(4):
                    wide_done(act, halves["ret_vg"] + h + 1, i, 4)
                    if h % 2:
                        nc.scalar.activation(vg[:, 0, bass.ds(i * 2 * C + h // 2 * C, C)], ps[:, 4 + h - 1, :],
                                             ACT.Copy).then_inc(rvg_fa, 1)
                    if more or h < 2:
                        split_high(act, "ret_vg", h + 2, i, 4)

            with act.Fori(0, 3) as i:
                v_group(i, True)
            v_group(3, False)
            act.wait_ge(rvg_fv, 2 + 8)
            act.wait_ge(rvg_fa, 2 + 8)
            for t in range(NT):
                nc.scalar.activation(vg[:, t, RV:2 * RV], vg[:, t, RV:2 * RV], ACT.Silu).then_inc(rg_silu, 1)
            nc.scalar.activation(stat[:, 16:24], s_("c"), ACT.Silu).then_inc(ada_c, 1)

            def ret_squares(h):
                for t in range(NT):
                    act.wait_ge(r_o, 2 * h + t + 1)
                    nc.scalar.activation(xn[:, 1, 0:C], ps[:, 2 + 2 * (h % 2) + t, :], ACT.Square,
                                         accum_out=stat[:, 8 + t:9 + t]).then_inc(r_sq, 1)
                    act.wait_ge(r_sq, 2 * h + t + 1)
                act.wait_ge(r_ms, h + 1)
                nc.scalar.activation(stat[:, 12:14], stat[:, 10:12], ACT.Sqrt).then_inc(r_sd, 1)

            def ret_copy(h):
                act.wait_ge(r_t, 2 * h + 1)
                nc.scalar.activation(yT[:, 4 * h:4 * h + 2, :].rearrange("p a b -> p (a b)"), ps[:, 6, :], ACT.Copy)\
                    .then_inc(r_ta, 1)

            for h in range(RH):
                ret_squares(h)
                if h >= 1:
                    ret_copy(h - 1)
            ret_copy(RH - 1)

            def ffn(l):
                def pair(b, j, off, split):
                    n = off + (2 * b + j)
                    w0, b0 = SMALL["conv_w"][0], SMALL["conv_b"][0]
                    act.wait_ge(wide_mm, off + (halves[f"up{l}"] + 2 * b + j + 1))
                    for gv in range(2):
                        at = (l * 2 + gv) * FP
                        last = nc.scalar.activation(
                            cv[:, j, gv * T:(gv + 1) * T], ps[:, 2 * b + j, gv * T:(gv + 1) * T], ACT.Identity,
                            scale=small[:, bass.ds(n * 3 + (w0 + at * 3 + 2), 1)],
                            bias=small[:, bass.ds(n + (b0 + at), 1)])
                    last.then_inc(up_id, 1)
                    if split is not None:
                        split_high(act, f"up{l}", 2 * b + j + 2, split, 4)
                    act.wait_ge(up_cv, off + (FP * l + 2 * b + j + 1))
                    nc.scalar.activation(cv[:, j, 0:T], cv[:, j, 0:T], ACT.Silu).then_inc(up_si, 1)

                with act.Fori(0, 5) as i:
                    for b in range(2):
                        for j in range(2):
                            pair(b, j, i * 4, i)
                for j in range(2):
                    pair(0, j, 20, None)

            split_first(split_high, act, "up0")
            norm_act(act, 1)
            split_norm(act, 1, 0)
            ffn(0)
            split_first(split_high, act, "sb_qk")
            norm_act(act, 2)
            split_norm(act, 2, 0)

            nc.scalar.activation(credit[:, 4:5], small[:, 0:1], ACT.Copy).then_inc(sqk_fa, 2)
            with act.Fori(0, 2) as i:
                for h in range(4):
                    wide_done(act, halves["sb_qk"] + h + 1, i, 4)
                    if h % 2 == 0:
                        nc.scalar.activation(sqk[:, i * 4 + h, :], ps[:, h, :], ACT.Copy).then_inc(sqk_fa, 1)
                    split_high(act, "sb_qk", h + 2, i, 4)
            for h in range(4):
                wide_done(act, halves["sb_v"] + h + 1)
                if h % 2:
                    u = h // 2
                    nc.scalar.activation(sv[:, 0, u * C:(u + 1) * C], ps[:, 4 + 2 * u, :], ACT.Copy).then_inc(sv_a, 1)
                if h < 2:
                    split_high(act, "sb_v", h + 2)

            def sb_log(g):
                z = ps[:, 2 * (g % 2):2 * (g % 2) + 2, 0:TRI]
                act.wait_ge(s_z, g + 1)
                if g >= 2:
                    act.wait_ge(s_la, g - 1)
                link(nc.scalar.activation(l_b[g % 2], z, ACT.Abs, scale=SDH ** -0.5))
                nc.scalar.activation(z_b[g % 2], z, ACT.Copy, scale=SDH ** -0.5).then_inc(s_zc, 1)
                link(nc.scalar.activation(l_b[g % 2], l_b[g % 2], ACT.Exp, scale=-1.0))
                nc.scalar.activation(l_b[g % 2], l_b[g % 2], ACT.Ln, bias=1.0).then_inc(s_l, 1)

            def sb_exp(g):
                act.wait_ge(s_la, g + 1)
                nc.scalar.activation(a_b[g % 2], a_b[g % 2], ACT.Exp).then_inc(s_a, 1)

            sb_log(0)
            sb_log(1)
            for g in range(SH // 2):
                sb_exp(g)
                if g + 2 < SH // 2:
                    sb_log(g + 2)

            split_first(split_high, act, "up1")
            norm_act(act, 3)
            split_norm(act, 3, 0)
            ffn(1)
            split_first(split_high, act, "mix_in")
            norm_act(act, 4)
            norm_act(act, 5)
            split_norm(act, 5, 0)

            act.wait_ge(l_f, 1)
            link(nc.scalar.activation(rows4[0:LH, 2, :], rows4[0:LH, 1, :], ACT.Abs))
            link(nc.scalar.activation(rows4[0:LH, 2, :], rows4[0:LH, 2, :], ACT.Exp, scale=-1.0))
            nc.scalar.activation(rows4[0:LH, 2, :], rows4[0:LH, 2, :], ACT.Ln, bias=1.0).then_inc(l_ln, 1)
            w0, b0 = SMALL["conv2_w"][0], SMALL["conv2_b"][0]
            for q in range(4):
                wide_done(act, halves["mix_in"] + q + 1)
                if q:
                    act.wait_ge(mi_si, q)
                for f in range(2):
                    n = 2 * q + f
                    last = nc.scalar.activation(cvm[:, f, :], ps[:, q, f * T:(f + 1) * T], ACT.Identity,
                                                scale=small[:, w0 + 4 * n + 3:w0 + 4 * n + 4],
                                                bias=small[:, b0 + n:b0 + n + 1])
                last.then_inc(mi_id, 1)
                split_high(act, "mix_in", q + 2)
                act.wait_ge(mi_cv, q + 1)
                nc.scalar.activation(qkm[:, 2 * q:2 * q + 2, :], cvm[:, :, :], ACT.Silu).then_inc(mi_si, 1)
            for h in range(4, MIX):
                wide_done(act, halves["mix_in"] + h + 1)
                if h in (4, 6):
                    nc.scalar.activation(qka[:, 2 * (h - 4):2 * (h - 4) + 2, :].rearrange("p a b -> p (a b)"),
                                         ps[:, h % 4, :], ACT.Copy).then_inc(mi_ev_a, 1)
                if h == 9:
                    nc.scalar.activation(vm[:, 0, :].rearrange("p (h e) -> p h e", h=LH)[:, :, 0:LDH],
                                         ps[:, 0, :].rearrange("p (h e) -> p h e", h=LH), ACT.Copy)\
                        .then_inc(mi_ev_a, 1)
                if h == 11:
                    nc.scalar.activation(om[:, 0, :], ps[:, 2, :], ACT.Copy).then_inc(mi_ev_a, 1)
                if h == 13:
                    nc.scalar.activation(va[:, 0, :], ps[:, 0, :], ACT.Copy).then_inc(mi_ev_a, 1)
                if h + 2 < MIX:
                    split_high(act, "mix_in", h + 2)
            act.wait_ge(mi_ev_a, 5)
            act.wait_ge(mi_ev_v, 5)
            nc.scalar.activation(om[:, :, :], om[:, :, :], ACT.Sigmoid).then_inc(l_sig, 1)
            act.wait_ge(l_rows, 1)
            act.wait_ge(l_cols, 1)
            nc.scalar.activation(fcol[:, :, :], fcol[:, :, :], ACT.Exp).then_inc(l_floor, 1)
            for h in range(LH):
                act.wait_ge(l_w, h + 1)
                nc.scalar.activation(wt[:, h % 2, :], wt[:, h % 2, :], ACT.Exp).then_inc(l_e, 1)
            for h in range(MH):
                act.wait_ge(b_mx, h + 1)
                for blk, (c0, c1) in enumerate(((0, P), (P, TRI))):
                    last = nc.scalar.activation(m_sc[:, h % 2, c0:c1], m_sc[:, h % 2, c0:c1], ACT.Exp,
                                                bias=mst[:, 4 * h + blk:4 * h + blk + 1],
                                                accum_out=mst[:, 4 * h + 2 + blk:4 * h + 3 + blk])
                last.then_inc(b_e, 1)
            act.wait_ge(l_h, LH)
            for h in range(LH):
                for t in range(NT):
                    link(nc.scalar.activation(pt[:, 0, 0:LDH], hm[:, t, h * LDH:(h + 1) * LDH], ACT.Square,
                                              accum_out=mst[:, 64 + 2 * h + t:65 + 2 * h + t]))
            nc.scalar.activation(credit[:, 5:6], small[:, 0:1], ACT.Copy).then_inc(l_sq, 1)
            act.wait_ge(l_ms, 1)
            nc.scalar.activation(mst[:, 72:80], mst[:, 64:72], ACT.Sqrt).then_inc(l_sd, 1)

            norm_act(act, 6)
            norm_evict(act, 6, 0)
            act.wait_ge(t_top, 1)
            for t in range(NT):
                last = nc.scalar.activation(g8[:, t, 0:NG], g8[:, t, 0:NG], ACT.Exp, accum_out=rst[:, 4 + t:5 + t])
            link(last)
            nc.scalar.activation(rst[:, 8:10], rst[:, 6:8], ACT.Exp).then_inc(t_exp, 1)

            def expert_pass(r):
                def xg_evict(value):
                    act.wait_ge(m_ga, value)
                    for k in range(4):
                        last = nc.scalar.activation(xg[:, k, :], ps[:, 4, k * P:(k + 1) * P], ACT.Identity,
                                                    scale=mods[:, 2, k:k + 1], bias=mods[:, 3, k:k + 1])
                    last.then_inc(m_xa, 1)

                act.wait_ge(m_zero, 3 * (r + 1))
                nc.scalar.activation(credit[:, 6:7], small[:, 0:1], ACT.Copy).then_inc(m_ya, 1)
                xg_evict((PAIRS + 1) * 2 * r + 2)
                with act.Fori(0, PAIRS) as i:
                    act.wait_ge(m_gu, i * 2 + (PAIRS * 2 * r + 1))
                    nc.scalar.activation(hs, ps[:, 4, :], ACT.Silu).then_inc(m_si, 1)
                    act.wait_ge(m_ht, i + (PAIRS * r + 1))
                    nc.scalar.activation(hgT[:, :, :].rearrange("p k n -> p (k n)"), ps[:, 4, :], ACT.Copy)\
                        .then_inc(m_hc, 1)
                    xg_evict(i * 2 + ((PAIRS + 1) * 2 * r + 4))
                    act.wait_ge(m_dn, i + (PAIRS * r + 1))
                    nc.scalar.activation(ye[:, 0:C], ps[:, 6, :], ACT.Copy).then_inc(m_ya, 1)

            expert_pass(0)
            act.wait_ge(t_flag, 1)
            most = act.value_load(flag[0:1, 0:1])
            with act.If(most > R):
                for r in range(1, PASSES):
                    expert_pass(r)
            norm_act(act, 7)

        @block.vector
        def _(dve):
            link = Link(dve, dve_chain)
            norm_dve(dve, link, 0)
            dve.wait_ge(small_in, 16)
            split_norm(dve, 0, 1)
            split_low(dve, "ret_qk", 0)
            split_low(dve, "ret_qk", 1)
            nc.vector.memset(credit[:, 0:1], 0.0).then_inc(rqk_free, 4)
            cos, sin = k_("cos"), k_("sin")
            dve.wait_ge(const_in, 16)
            with dve.Fori(0, 2) as i:
                link.enter(i, 4)
                for b in range(2):
                    for j in range(2):
                        q = i * 4 + (2 * b + j)
                        u = ps[:, 2 * b + j, :]
                        wide_done(dve, 2 * b + j + 1, i, 4)
                        nc.vector.tensor_tensor(rot_a, u, cos, ALU.mult)
                        nc.vector.tensor_tensor(rot_b[:, 0:T], u[:, T:C], sin[:, 0:T], ALU.mult)
                        nc.vector.tensor_tensor(rot_b[:, T:C], u[:, 0:T], sin[:, T:C], ALU.mult)\
                            .then_inc(rqk_free, 1)
                        dve.wait_ge(rqk_free, i * 4 + (4 + 2 * b + j + 1))
                        link(nc.vector.tensor_tensor(qk[:, q, :], rot_a, rot_b, ALU.add))
                        split_low(dve, "ret_qk", 2 * b + j + 2, i, 4)
            link.leave(2)
            nc.vector.memset(credit[:, 0:1], 0.0).then_inc(rqk_out, 8)
            nc.vector.memset(credit[:, 2:3], 0.0).then_inc(rvg_fv, 2)

            def v_group(i, more):
                for h in range(4):
                    if h % 2:
                        wide_done(dve, halves["ret_vg"] + h + 1, i, 4)
                        nc.vector.tensor_copy(vg[:, 1, bass.ds(i * 2 * C + h // 2 * C, C)], ps[:, 4 + h, :])\
                            .then_inc(rvg_fv, 1)
                    if more or h < 2:
                        split_low(dve, "ret_vg", h + 2, i, 4)

            with dve.Fori(0, 3) as i:
                v_group(i, True)
            v_group(3, False)

            decay = k_("decay").rearrange("p (h t) -> p h t", h=RH)

            def ret_decay(h):
                dve.wait_ge(r_s, h + 1)
                if h >= 2:
                    dve.wait_ge(r_o, 2 * (h - 1))
                nc.vector.tensor_tensor(r_sc[:, h % 2, :], ps[:, h % 2, 0:TRI], decay[:, h, :], ALU.mult)\
                    .then_inc(r_d, 1)

            def ret_y(h):
                dve.wait_ge(r_sq, 2 * (h + 1))
                nc.vector.tensor_scalar(stat[:, 10:12], stat[:, 8:10], 1.0 / RDV, EPS, ALU.mult, ALU.add)\
                    .then_inc(r_ms, 1)
                dve.wait_ge(r_sd, h + 1)
                link(nc.vector.reciprocal(stat[:, 14:16], stat[:, 12:14]))
                if h == 0:
                    dve.wait_ge(rg_silu, 2)
                for t in range(NT):
                    g = vg[:, t, RV + h * RDV:RV + (h + 1) * RDV]
                    nc.vector.scalar_tensor_tensor(out=g, in0=ps[:, 2 + 2 * (h % 2) + t, :], scalar=stat[:, 14 + t:15 + t],
                                                   in1=g, op0=ALU.mult, op1=ALU.mult).then_inc(r_y, 1)

            def ret_copy(h):
                dve.wait_ge(r_t, 2 * h + 2)
                nc.vector.tensor_copy(yT[:, 4 * h + 2:4 * h + 4, :].rearrange("p a b -> p (a b)"), ps[:, 7, :])\
                    .then_inc(r_tv, 1)

            ret_decay(0)
            ret_decay(1)
            for h in range(RH):
                ret_y(h)
                if h + 2 < RH:
                    ret_decay(h + 2)
                if h >= 1:
                    ret_copy(h - 1)
            ret_copy(RH - 1)
            split_first(split_low, dve, "up0")
            residual(dve, rout_mm, 4)
            norm_dve(dve, link, 1)
            split_norm(dve, 1, 1)

            def adaptive():
                with dve.Fori(0, 12 - ADA_POOL) as i:
                    link.enter(i, 6)
                    acc = ada_acc[:, bass.ds(i * C + ADA_POOL * C, C)]
                    for kh, w in enumerate(ada_w):
                        dve.wait_ge(ada_in[kh], i * 16 + 16 * (ADA_POOL + 1))
                        for k in range(4):
                            sc = stat[:, 16 + 4 * kh + k:17 + 4 * kh + k]
                            if kh == 0 and k == 0:
                                ins = nc.vector.tensor_scalar(acc, w[:, k, :], sc, None, ALU.mult)
                            else:
                                ins = nc.vector.scalar_tensor_tensor(out=acc, in0=w[:, k, :], scalar=sc, in1=acc,
                                                                     op0=ALU.mult, op1=ALU.add)
                            if k < 3:
                                link(ins)
                        ins.then_inc(ada_used, 1)
                        dve.wait_ge(ada_used, i * 2 + (kh + 1))
                link.leave(12 - ADA_POOL)
                nc.vector.memset(credit[:, 2:3], 0.0).then_inc(ada_sum, 1)

            def ffn(l):
                base = (FP + 4) * l
                nc.vector.memset(credit[:, 0:1], 0.0).then_inc(up_free, 4)

                def pair(b, j, off, split):
                    n = off + (2 * b + j)
                    w0 = SMALL["conv_w"][0]
                    tap = lambda gv, k: small[:, bass.ds(n * 3 + (w0 + (l * 2 + gv) * FP * 3 + k), 1)]
                    c, u = cv[:, j, :], ps[:, 2 * b + j, :]
                    dve.wait_ge(up_id, off + (FP * l + 2 * b + j + 1))
                    for gv in range(2):
                        o = gv * T
                        last = nc.vector.scalar_tensor_tensor(
                            out=c[:, o + 1:o + T], in0=u[:, o:o + T - 1], scalar=tap(gv, 1), in1=c[:, o + 1:o + T],
                            op0=ALU.mult, op1=ALU.add)
                    link(last)
                    for gv in range(2):
                        o = gv * T
                        last = nc.vector.scalar_tensor_tensor(
                            out=c[:, o + 2:o + T], in0=u[:, o:o + T - 2], scalar=tap(gv, 0), in1=c[:, o + 2:o + T],
                            op0=ALU.mult, op1=ALU.add)
                        if gv == 0:
                            last.then_inc(up_cv, 1)
                    last.then_inc(up_free, 1)
                    if split is not None:
                        split_low(dve, f"up{l}", 2 * b + j + 2, split, 4)
                    dve.wait_ge(up_free, off + (base + 4 + 2 * b + j + 1))
                    dve.wait_ge(up_si, off + (FP * l + 2 * b + j + 1))
                    nc.vector.tensor_tensor(hff[:, n, :], c[:, 0:T], c[:, T:C], ALU.mult).then_inc(up_h, 1)

                with dve.Fori(0, 5) as i:
                    link.enter(i, 4)
                    for b in range(2):
                        for j in range(2):
                            pair(b, j, i * 4, i)
                link.leave(5)
                for j in range(2):
                    pair(0, j, 20, None)
                if l == 0:
                    adaptive()
                split_first(split_low, dve, ("sb_qk", "mix_in")[l])
                residual(dve, down_mm, 6 * (l + 1))

            ffn(0)

            def modulations():
                mr = modr[:, :].rearrange("p (m k) -> p m k", m=4)
                dve.wait_ge(ada_mods, 1)
                ba = b_ada.rearrange("p (m k) -> p m k", m=6)
                for m, q in enumerate((0, 1, 3, 4)):
                    last = nc.vector.tensor_tensor(mr[:, m, :], ps[:, 3, m * KD:(m + 1) * KD], ba[:, q, :], ALU.add)
                last.then_inc(ada_gate, 1)
                dve.wait_ge(ada_gate, 1)
                for n, (sh, scl, g) in enumerate(((0, 1, "g1"), (2, 3, "g2"))):
                    nc.vector.tensor_copy(mods[:, 2 * n + 1, :], mr[:, sh, :])
                    link(nc.vector.scalar_tensor_tensor(out=mods[:, 2 * n, :], in0=mr[:, scl, :], scalar=1.0,
                                                        in1=s_(g), op0=ALU.add, op1=ALU.mult))

            modulations()
            norm_dve(dve, link, 2)
            split_norm(dve, 2, 1)
            dve.wait_ge(ada_mods, 2)
            dve.wait_ge(bias_in, 32)
            for half in range(4):
                gt = gates[:, half // 2, (half % 2) * C:(half % 2 + 1) * C]
                nc.vector.tensor_tensor(gt, ps[:, 4 + half, :], gt, ALU.add).then_inc(ada_gate, 1)

            nc.vector.memset(credit[:, 0:1], 0.0).then_inc(sqk_fv, 2)
            with dve.Fori(0, 2) as i:
                for h in range(4):
                    if h % 2:
                        wide_done(dve, halves["sb_qk"] + h + 1, i, 4)
                        nc.vector.tensor_copy(sqk[:, i * 4 + h, :], ps[:, h, :]).then_inc(sqk_fv, 1)
                    split_low(dve, "sb_qk", h + 2, i, 4)
            for h in range(4):
                if h % 2:
                    wide_done(dve, halves["sb_v"] + h + 1)
                    u = h // 2
                    nc.vector.tensor_copy(sv[:, 1, u * C:(u + 1) * C], ps[:, 5 + 2 * u, :]).then_inc(sv_v, 1)
                if h < 2:
                    split_low(dve, "sb_v", h + 2)

            def sb_softplus(g):
                dve.wait_ge(s_zc, g + 1)
                dve.wait_ge(s_l, g + 1)
                if g >= 2:
                    dve.wait_ge(s_ex, g - 1)
                nc.vector.scalar_tensor_tensor(out=sp_b[g % 2], in0=z_b[g % 2], scalar=0.0, in1=l_b[g % 2],
                                               op0=ALU.max, op1=ALU.add).then_inc(s_sp, 1)

            def sb_log_a(g):
                link(nc.vector.scalar_tensor_tensor(out=z_b[g % 2], in0=z_b[g % 2], scalar=0.0, in1=l_b[g % 2],
                                                    op0=ALU.min, op1=ALU.subtract))
                dve.wait_ge(s_ex, g + 1)
                if g >= 2:
                    dve.wait_ge(s_o, g - 1)
                nc.vector.tensor_tensor(a_b[g % 2], z_b[g % 2], ps[:, 4:6, 0:TRI], ALU.subtract).then_inc(s_la, 1)

            def sb_copy(g):
                dve.wait_ge(s_o, g + 1)
                nc.vector.tensor_copy(soT[:, g, :], ps[:, 6 + g % 2, 0:T]).then_inc(s_ot, 1)

            sb_softplus(0)
            sb_softplus(1)
            for g in range(SH // 2):
                dve.wait_ge(s_sp, g + 1)
                sb_log_a(g)
                if g + 2 < SH // 2:
                    sb_softplus(g + 2)
                if g >= 1:
                    sb_copy(g - 1)
            sb_copy(SH // 2 - 1)
            split_first(split_low, dve, "up1")
            residual(dve, sout_mm, 2)
            norm_dve(dve, link, 3)
            split_norm(dve, 3, 1)
            ffn(1)

            def scale_rows():
                for t in range(NT):
                    nc.vector.scalar_tensor_tensor(out=x[:, t, :], in0=x[:, t, :], scalar=stat[:, 6 + t:7 + t],
                                                   in1=rowv[:, :], op0=ALU.mult, op1=ALU.mult).then_inc(x_new, 1)

            norm_dve(dve, link, 4)
            dve.wait_ge(row_in, 16)
            dve.wait_ge(x_new, update(3))
            scale_rows()
            norm_dve(dve, link, 5)
            split_norm(dve, 5, 1)

            row = lambda n: rows4[0:LH, n, :]
            dve.wait_ge(mix_small, 80)
            nc.vector.memset(vm[:, :, :], 1.0)
            nc.vector.memset(row(8), 1.0)
            dve.wait_ge(mi_g, 1)
            link(nc.vector.tensor_scalar(row(0), ps[0:LH, 4, 0:T], bg[0:LH, 0:1], None, ALU.add))
            nc.vector.tensor_scalar(row(1), ps[0:LH, 5, 0:T], bg[0:LH, 1:2], None, ALU.add).then_inc(l_f, 1)
            dve.wait_ge(l_ln, 1)
            dve.wait_ge(l_f, 1)
            link(nc.vector.scalar_tensor_tensor(out=row(1), in0=row(1), scalar=0.0, in1=row(2), op0=ALU.min,
                                                op1=ALU.subtract))
            link(nc.vector.tensor_tensor_scan(row(3), row(8), row(1), 0.0, ALU.mult, ALU.add))
            link(nc.vector.tensor_tensor(row(4), row(0), row(3), ALU.subtract))
            link(nc.vector.tensor_tensor_scan(row(5), row(8), row(4), 0.0, ALU.mult, ALU.max))
            nc.vector.tensor_scalar(row(6), row(5), -1.0, None, ALU.mult)
            nc.vector.scalar_tensor_tensor(out=row(7), in0=row(3), scalar=-1.0, in1=row(5), op0=ALU.mult,
                                           op1=ALU.subtract).then_inc(l_rows, 1)

            w0 = SMALL["conv2_w"][0]
            for q in range(4):
                dve.wait_ge(mi_id, q + 1)
                for k in (2, 1, 0):
                    for f in range(2):
                        n, d = 2 * q + f, 3 - k
                        ins = nc.vector.scalar_tensor_tensor(
                            out=cvm[:, f, d:T], in0=ps[:, q, f * T:(f + 1) * T - d],
                            scalar=small[:, w0 + 4 * n + k:w0 + 4 * n + k + 1], in1=cvm[:, f, d:T],
                            op0=ALU.mult, op1=ALU.add)
                    if k:
                        link(ins)
                ins.then_inc(mi_cv, 1)
                split_low(dve, "mix_in", q + 2)
            for h in range(4, 12):
                if h in (5, 7, 9, 11):
                    wide_done(dve, halves["mix_in"] + h + 1)
                if h in (5, 7):
                    nc.vector.tensor_copy(qka[:, 2 * (h - 4):2 * (h - 4) + 2, :].rearrange("p a b -> p (a b)"),
                                          ps[:, h % 4, :]).then_inc(mi_ev_v, 1)
                if h == 9:
                    nc.vector.tensor_copy(vm[:, 1, :].rearrange("p (h e) -> p h e", h=LH)[:, :, 0:LDH],
                                          ps[:, 1, :].rearrange("p (h e) -> p h e", h=LH)).then_inc(mi_ev_v, 1)
                if h == 11:
                    nc.vector.tensor_copy(om[:, 1, :], ps[:, 3, :]).then_inc(mi_ev_v, 1)
                if h + 2 < MIX:
                    split_low(dve, "mix_in", h + 2)
            dve.wait_ge(l_tr, 1)
            nc.vector.tensor_copy(acol[:, :, :].rearrange("p a b -> p (a b)"), ps[:, 6, 0:8])
            nc.vector.tensor_copy(fcol[:, :, :].rearrange("p a b -> p (a b)"), ps[:, 6, 8:16]).then_inc(l_cols, 1)
            wide_done(dve, halves["mix_in"] + 14)
            nc.vector.tensor_copy(va[:, 1, :], ps[:, 1, :]).then_inc(mi_ev_v, 1)
            dve.wait_ge(l_sig, 1)
            gh = ghead.unsqueeze(1).broadcast_to([P, NT, C])
            link(nc.vector.tensor_tensor(om[:, :, :], om[:, :, :], gh, ALU.mult))
            dve.wait_ge(l_cols, 1)

            def ls_w(h):
                b = 3 * (h % 2)
                dve.wait_ge(l_s, h + 1)
                if h >= 2:
                    dve.wait_ge(l_p, h - 1)
                nc.vector.tensor_scalar(wt[:, h % 2, 0:T], ps[:, b, 0:T], acol[:, 0, h:h + 1], 0.0, ALU.add, ALU.min)
                nc.vector.tensor_scalar(wt[:, h % 2, T:TRI], ps[:, b, P:T], acol[:, 1, h:h + 1], 0.0, ALU.add, ALU.min)\
                    .then_inc(l_w, 1)

            def ls_p(h):
                b = 3 * (h % 2) + 1
                dve.wait_ge(l_e, h + 1)
                diag = wt[:, h % 2, :].rearrange("p (b t) -> p b t", b=3)[:, 0:3:2, :]
                link(nc.vector.tensor_tensor(diag, diag, upto.unsqueeze(1).broadcast_to([P, 2, P]), ALU.mult))
                if h >= 2:
                    dve.wait_ge(l_o, h - 1)
                nc.vector.scalar_tensor_tensor(out=pt[:, h % 2, :], in0=ps[:, b, 0:TRI], scalar=LDH ** -0.5,
                                               in1=wt[:, h % 2, :], op0=ALU.mult, op1=ALU.mult).then_inc(l_p, 1)

            def ls_h(h):
                b = 3 * (h % 2) + 2
                dve.wait_ge(l_o, h + 1)
                if h == 0:
                    dve.wait_ge(l_floor, 1)
                den = lambda t: mst[:, 80 + 2 * h + t:81 + 2 * h + t]
                for t in range(NT):
                    last = nc.vector.tensor_scalar(den(t), ps[:, b, t * T + LDH:t * T + LDH + 1], -1.0,
                                                   fcol[:, t, h:h + 1], ALU.mult, ALU.max)
                link(last)
                for t in range(NT):
                    last = nc.vector.tensor_tensor(den(t), ps[:, b, t * T + LDH:t * T + LDH + 1], den(t), ALU.max)
                link(last)
                link(nc.vector.reciprocal(mst[:, 88 + 2 * h:90 + 2 * h], mst[:, 80 + 2 * h:82 + 2 * h]))
                for t in range(NT):
                    last = nc.vector.tensor_scalar(hm[:, t, h * LDH:(h + 1) * LDH], ps[:, b, t * T:t * T + LDH],
                                                   mst[:, 88 + 2 * h + t:89 + 2 * h + t], None, ALU.mult)
                last.then_inc(l_h, 1)

            ls_w(0)
            ls_w(1)
            for h in range(LH):
                ls_p(h)
                if h + 2 < LH:
                    dve.wait_ge(l_p, h + 1)
                    ls_w(h + 2)
                ls_h(h)

            future = k_("future")

            def mb_max(h):
                dve.wait_ge(b_s, h + 1)
                if h >= 2:
                    dve.wait_ge(b_t, h - 1)
                sc = m_sc[:, h % 2, :]
                link(nc.vector.scalar_tensor_tensor(out=sc, in0=ps[:, 6 + h % 2, 0:TRI], scalar=MDH ** -0.5, in1=future,
                                                    op0=ALU.mult, op1=ALU.add))
                nc.vector.tensor_reduce(mst[:, 4 * h:4 * h + 1], sc[:, 0:P], AX, ALU.max, negate=True)
                nc.vector.tensor_reduce(mst[:, 4 * h + 1:4 * h + 2], sc[:, P:TRI], AX, ALU.max, negate=True)\
                    .then_inc(b_mx, 1)

            def mb_p(h):
                dve.wait_ge(b_e, h + 1)
                link(nc.vector.reciprocal(mst[:, 4 * h + 2:4 * h + 4], mst[:, 4 * h + 2:4 * h + 4]))
                for blk, (c0, c1) in enumerate(((0, P), (P, TRI))):
                    last = nc.vector.tensor_scalar(m_sc[:, h % 2, c0:c1], m_sc[:, h % 2, c0:c1],
                                                   mst[:, 4 * h + 2 + blk:4 * h + 3 + blk], None, ALU.mult)
                last.then_inc(b_p, 1)

            def mb_copy(h):
                dve.wait_ge(b_t, h + 1)
                if h >= 2:
                    dve.wait_ge(b_o, h - 1)
                nc.vector.tensor_copy(wt[:, h % 2, :], ps[:, h % 2, 0:TRI]).then_inc(b_tc, 1)

            def mb_o(g):
                dve.wait_ge(b_o, 2 * (g + 1))
                nc.vector.tensor_copy(mixT[:, 4 + g, :], ps[:, 3 + g % 2, 0:T]).then_inc(b_oc, 1)

            mb_max(0)
            mb_max(1)
            for h in range(MH):
                mb_p(h)
                mb_copy(h)
                if h + 2 < MH:
                    mb_max(h + 2)
                if h >= 1 and h % 2 == 0:
                    mb_o(h // 2 - 1)
            mb_o(MH // 2 - 1)

            dve.wait_ge(l_sq, 1)
            nc.vector.tensor_scalar(mst[:, 64:72], mst[:, 64:72], 1.0 / LDH, EPS, ALU.mult, ALU.add).then_inc(l_ms, 1)
            dve.wait_ge(l_sd, 1)
            link(nc.vector.reciprocal(mst[:, 96:104], mst[:, 72:80]))
            for h in range(LH):
                for t in range(NT):
                    cols = slice(h * LDH, (h + 1) * LDH)
                    nc.vector.scalar_tensor_tensor(out=hm[:, t, cols], in0=hm[:, t, cols],
                                                   scalar=mst[:, 96 + 2 * h + t:97 + 2 * h + t], in1=om[:, t, cols],
                                                   op0=ALU.mult, op1=ALU.mult).then_inc(l_hn, 1)
            for j in range(2):
                dve.wait_ge(l_t, j + 1)
                nc.vector.tensor_copy(mixT[:, 2 * j:2 * j + 2, :].rearrange("p a b -> p (a b)"), ps[:, j, :])\
                    .then_inc(l_mt, 1)

            dve.wait_ge(mo_mm, 2)
            gated_residual(link, 0, 4, xn, True)

            norm_dve(dve, link, 6)
            norm_evict(dve, 6, 1)

            dve.wait_ge(t_lg, 1)
            dve.wait_ge(r_in, 64)
            lgp = ps[:, 4, 0:P].rearrange("p (t n) -> p t n", t=NT)[:, :, 0:NG + NE]
            nc.vector.memset(g8[:, :, :], NEG)
            nc.vector.memset(pos[:, :, :], -1.0)
            nc.vector.memset(wgt[:, :, :], 0.0)
            link(nc.vector.tensor_tensor(lg[:, :, :], lgp, br.unsqueeze(1).broadcast_to([P, NT, NG + NE]), ALU.add))
            link(nc.vector.tensor_copy(g8[:, :, 0:NG], lg[:, :, 0:NG]))
            for t in range(NT):
                link(nc.vector.max(m8[:, t, :], g8[:, t, :]))
                link(nc.vector.max_index(i8[:, t, :], m8[:, t, :], g8[:, t, :]))
            link(nc.vector.tensor_copy(f8[:, :, :], i8[:, :, :]))
            for t in range(NT):
                nc.vector.tensor_scalar(oh[:, t, :], iota[:, 0:NG], f8[:, t, 0:1], None, ALU.is_equal)
                link(nc.vector.tensor_scalar(g8[:, t, 0:NG], g8[:, t, 0:NG], m8[:, t, 0:1], None, ALU.subtract))
            link(nc.vector.tensor_scalar(oh[:, :, :], oh[:, :, :], -1.0, -NEG, ALU.add, ALU.mult))
            for t in range(NT):
                pen = oh[:, t, :].unsqueeze(2).broadcast_to([P, NG, EPG])
                link(nc.vector.tensor_tensor(em[:, t, :].rearrange("p (g e) -> p g e", g=NG),
                                             lg[:, t, NG:].rearrange("p (g e) -> p g e", g=NG), pen, ALU.add))
                link(nc.vector.max(m8[:, t, :], em[:, t, :]))
                link(nc.vector.max_index(i8[:, t, :], m8[:, t, :], em[:, t, :]))
            link(nc.vector.tensor_copy(f8[:, :, :], i8[:, :, :]))
            for t in range(NT):
                last = nc.vector.tensor_tensor(rst[:, 6 + t:7 + t], m8[:, t, 1:2], m8[:, t, 0:1], ALU.subtract)
                link(nc.vector.tensor_scalar(oh1[:, t, :], iota[:, 0:NE], f8[:, t, 0:1], None, ALU.is_equal))
                link(nc.vector.tensor_scalar(oh2[:, t, :], iota[:, 0:NE], f8[:, t, 1:2], None, ALU.is_equal))
            nc.vector.memset(credit[:, 0:1], 0.0).then_inc(t_top, 1)
            nc.vector.tensor_tensor(asg[:, :, :], oh1[:, :, :], oh2[:, :, :], ALU.add).then_inc(t_rank, 1)
            dve.wait_ge(t_exp, 1)
            link(nc.vector.tensor_scalar(rst[:, 10:12], rst[:, 8:10], 1.0, None, ALU.add))
            link(nc.vector.tensor_tensor(rst[:, 10:12], rst[:, 10:12], rst[:, 4:6], ALU.mult))
            link(nc.vector.reciprocal(rst[:, 12:14], rst[:, 10:12]))
            link(nc.vector.tensor_tensor(rst[:, 14:16], rst[:, 12:14], rst[:, 8:10], ALU.mult))
            for t in range(NT):
                link(nc.vector.tensor_scalar(oh2[:, t, :], oh2[:, t, :], rst[:, 14 + t:15 + t], None, ALU.mult))
                link(nc.vector.scalar_tensor_tensor(out=wgt[:, t, 0:NE], in0=oh1[:, t, :], scalar=rst[:, 12 + t:13 + t],
                                                    in1=oh2[:, t, :], op0=ALU.mult, op1=ALU.add))
            dve.wait_ge(t_lg, 2)
            dve.wait_ge(t_rank, 1)
            rank = ps[:, 5, 0:P].rearrange("p (t n) -> p t n", t=NT)[:, :, 0:NE]
            link(nc.vector.scalar_tensor_tensor(out=em[:, :, :], in0=rank, scalar=1.0, in1=asg[:, :, :],
                                                op0=ALU.add, op1=ALU.mult))
            link(nc.vector.tensor_scalar(pos[:, :, 0:NE], em[:, :, :], -1.0, None, ALU.add))
            link(nc.vector.tensor_reduce(rst[:, 20:21], ps[:, 5, 128:128 + NE], AX, ALU.max))
            nc.vector.tensor_copy(flag, rst[:, 20:21]).then_inc(t_flag, 1)
            dve.wait_ge(norm_ha, 4)

            def expert_pass(r, link):
                slots = iota[:, r * R:(r + 1) * R]

                def select(buf, i, weigh, done):
                    for t in range(NT):
                        for e in range(2):
                            col = i * 2 + e
                            if weigh:
                                ins = nc.vector.tensor_scalar(buf[:, t, e * R:(e + 1) * R], slots,
                                                              pos[:, t, bass.ds(col, 1)], wgt[:, t, bass.ds(col, 1)],
                                                              ALU.is_equal, ALU.mult)
                            else:
                                ins = nc.vector.tensor_scalar(buf[:, t, e * R:(e + 1) * R], slots,
                                                              pos[:, t, bass.ds(col, 1)], None, ALU.is_equal)
                    ins.then_inc(done, 1)

                def xg_evict(value):
                    dve.wait_ge(m_ga, value)
                    for k in range(4, 8):
                        last = nc.vector.tensor_scalar(xg[:, k, :], ps[:, 5, (k - 4) * P:(k - 3) * P],
                                                       mods[:, 2, k:k + 1], mods[:, 3, k:k + 1], ALU.mult, ALU.add)
                    last.then_inc(m_xv, 1)

                nc.vector.memset(selT[:, :], 0.0).then_inc(m_zero, 1)
                nc.vector.memset(ye[:, :], 0.0).then_inc(m_zero, 1)
                nc.vector.memset(credit[:, 0:1], 0.0).then_inc(m_zero, 1)
                dve.wait_ge(m_zero, 3 * (r + 1))
                nc.vector.memset(credit[:, 1:2], 0.0).then_inc(m_yv, 1)
                dve.wait_ge(m_start, r + 1)
                select(sel, 0, False, m_s)
                select(selw, 0, True, m_sw)
                xg_evict((PAIRS + 1) * 2 * r + 1)
                dve.wait_ge(m_ga, (PAIRS + 1) * 2 * r + 2)
                select(sel, 1, False, m_s)
                with dve.Fori(0, PAIRS) as i:
                    dve.wait_ge(m_si, i + (PAIRS * r + 1))
                    dve.wait_ge(m_gu, i * 2 + (PAIRS * 2 * r + 2))
                    nc.vector.tensor_tensor(hg, hs, ps[:, 5, :], ALU.mult).then_inc(m_h, 1)
                    dve.wait_ge(m_sct, i + ((PAIRS + 1) * r + 1))
                    nc.vector.tensor_copy(selT[:, :], ps[:, 6, 0:T]).then_inc(m_swt, 1)
                    xg_evict(i * 2 + ((PAIRS + 1) * 2 * r + 3))
                    dve.wait_ge(m_ga, i * 2 + ((PAIRS + 1) * 2 * r + 4))
                    select(sel, i + 2, False, m_s)
                    select(selw, i + 1, True, m_sw)
                    dve.wait_ge(m_dn, i + (PAIRS * r + 1))
                    nc.vector.tensor_copy(ye[:, C:2 * C], ps[:, 7, :]).then_inc(m_yv, 1)
                dve.wait_ge(m_sct, (PAIRS + 1) * (r + 1))
                gated_residual(link, 1, 0, gtmp, False)

            expert_pass(0, link)
            most = dve.value_load(flag[0:1, 0:1])
            with dve.If(most > R):
                more = Link(dve, over_chain)
                for r in range(1, PASSES):
                    expert_pass(r, more)
            nc.vector.memset(credit[:, 0:1], 0.0).then_inc(x_new, 4)
            norm_dve(dve, link, 7)
            dve.wait_ge(row_in, 32)
            scale_rows()


_DIRECT = ["x", "ret_w_in", "ret_w_out", "sb_w_in", "sb_w_out", "ffn_w_up", "ffn_w_down", "final_norm", "w_ada_2",
           "b_ada_2", "w_in_2", "w_out_2", "b_gates_2", "g_mlstm_head_2", "w_router_group_2", "b_router_group_2",
           "w_router_expert_2", "b_router_expert_2", "w_expert_gate_2", "w_expert_up_2", "w_expert_down_2",
           "g_final_2"]


def small_weights(inputs):
    get = lambda n: np.asarray(inputs[n])
    feat = lambda a: a.reshape(-1, P).T
    tiles = lambda a: a.reshape(-1, P).T
    cw = get("ffn_conv_w").reshape(2, 3, 2, FP, P).transpose(4, 0, 2, 3, 1).reshape(P, -1)
    parts = {
        "ret_norm": feat(get("ret_norm")[0]), "sb_norm": feat(get("sb_norm")[0]), "ffn_norm": feat(get("ffn_norm")),
        "g1": feat(get("g_norm1_2")[0]), "g2": feat(get("g_norm2_2")[0]), "c": get("c_2").reshape(P, KD),
        "b_ada": feat(get("b_ada_2")[0]), "conv_w": cw, "conv_b": tiles(get("ffn_conv_b")),
        "conv2_w": get("w_conv_2")[0].reshape(4, 2 * LH, P).transpose(2, 1, 0).reshape(P, -1),
        "conv2_b": feat(get("b_conv_2")[0]),
    }
    return np.ascontiguousarray(np.concatenate([parts[n] for n in SMALL], axis=1))


def kernel(**inputs):
    import concourse.bacc as _bacc
    from concourse.bass_utils import run_bass_kernel_spmd as _run

    nc = _bacc.Bacc("TRN2", target_bir_lowering=False, num_devices=1)
    arrays = {f"in_{n}_dram": np.ascontiguousarray(inputs[n]) for n in _DIRECT}
    arrays["in_small_dram"] = small_weights(inputs)
    arrays["in_const_dram"] = shape_constants()
    arrays["in_sel4_dram"] = np.repeat(np.eye(LH, dtype=np.float32), P, axis=1)
    A = {n[3:-5]: nc.dram_tensor(n, a.shape, mybir.dt.from_np(a.dtype), kind="ExternalInput").ap()
         for n, a in arrays.items()}
    out = nc.dram_tensor("out_0_dram", (1, T, D), F32, kind="ExternalOutput").ap()
    build(nc, A, out)
    r = _run(nc, [arrays], core_ids=[0])
    return r.results[0]["out_0_dram"]
```

```python
from contextlib import ExitStack

import numpy as np

import concourse.bass as bass
from concourse import mybir

P = 128
D = 1024
T = 256
NT = T // P
KD = D // P
C = 512
EPS = 1e-6
RH, RDK, RDV = 4, 256, 512
RV = RH * RDV
SH, SDH = 16, 64
FF = 2816
FP = FF // P
LH, LDH = 4, 128
MH, MDH = 8, 64
NE, NG, EPG = 32, 4, 8
DE = 512
KE = DE // P
R = 64
PASSES = T // R
PAIRS = NE // 2
TRI = 3 * P
NEG = -1e30

F32 = mybir.dt.float32
F32R = mybir.dt.float32r
I32 = mybir.dt.int32
U32 = mybir.dt.uint32
ALU = mybir.AluOpType
ACT = mybir.ActivationFunctionType
AX = mybir.AxisListType.X

CONST = {}
_at = 0
for _name, _n in (("ident", P), ("ones", P), ("after", P), ("before", P), ("upto", P), ("future", TRI),
                  ("decay", RH * TRI), ("cos", 2 * T), ("sin", 2 * T), ("iota", T)):
    CONST[_name] = (_at, _at + _n)
    _at += _n
NCONST = _at

SMALL = {}
_at = 0
for _name, _n in (("ret_norm", KD), ("sb_norm", KD), ("ffn_norm", 2 * KD), ("g1", KD), ("g2", KD), ("c", KD),
                  ("b_ada", 6 * KD), ("conv_w", 2 * 2 * FP * 3), ("conv_b", 2 * 2 * FP),
                  ("conv2_w", 2 * LH * 4), ("conv2_b", 2 * LH)):
    SMALL[_name] = (_at, _at + _n)
    _at += _n
NSMALL = _at


def shape_constants():
    i = np.arange(P)
    s, t = i[:, None], i[None, :]
    out = np.zeros((P, NCONST), np.float32)

    def put(name, value):
        a, b = CONST[name]
        out[:, a:b] = value.reshape(P, b - a)

    put("ident", np.eye(P))
    put("ones", np.ones((P, P)))
    put("after", (s > t))
    put("before", (s < t))
    put("upto", (s <= t))
    put("future", np.concatenate([np.where(t > s, NEG, 0.0), np.zeros((P, P)), np.where(t > s, NEG, 0.0)], 1))
    decay = np.zeros((P, RH, TRI))
    for h in range(RH):
        log_g = np.log(1.0 - 2.0 ** (-5.0 - h))
        diag = np.where(s <= t, np.exp((t - s) * log_g), 0.0)
        decay[:, h] = np.concatenate([diag, np.exp((t - s + P) * log_g), diag], 1) * RDK ** -0.5
    put("decay", decay)
    freq = np.float32(10000.0) ** (-np.arange(0, RDK, 2, dtype=np.float32) / np.float32(RDK))
    ang = (freq.astype(np.float32)[:, None] * np.arange(T, dtype=np.float32)[None, :]).astype(np.float64)
    put("cos", np.concatenate([np.cos(ang), np.cos(ang)], 1))
    put("sin", np.concatenate([-np.sin(ang), np.sin(ang)], 1))
    put("iota", np.broadcast_to(np.arange(T), (P, T)))
    return out


def weight_plan(A):
    rows = lambda w: w.rearrange("(k p) n -> p k n", p=P)
    units = []

    def wide(phase, slot, w, c0):
        units.append((phase, slot, [((0, KD), (0, C), rows(w)[:, :, c0:c0 + C])]))

    def down(phase, slot, w, k0, n):
        units.append((phase, slot, [(None, n, rows(w)[:, k0:k0 + n, :])]))

    def ffn_up(l, slots):
        w = rows(A["ffn_w_up"][l])
        for u in range(FP // 2):
            s = slots[u % 2]
            units.append((f"up{l}", s, [((0, KD), (0, T), w[:, :, u * T:(u + 1) * T]),
                                        ((0, KD), (T, C), w[:, :, FF + u * T:FF + (u + 1) * T])]))

    def ffn_down(l, slots):
        for u, s in enumerate(slots):
            down(f"down{l}", s, A["ffn_w_down"][l], 4 * u, min(4, FP - 4 * u))

    for u in range(4):
        wide("ret_qk", u % 2, A["ret_w_in"][0], u * C)
    for u in range(8):
        wide("ret_vg", u % 2, A["ret_w_in"][0], (4 + u) * C)
    for u, s in enumerate((2, 0, 1, 2)):
        down("ret_out", s, A["ret_w_out"][0], 4 * u, 4)
    ffn_up(0, (0, 1))
    ffn_down(0, (2, 1, 0, 2, 1, 0))
    for u in range(4):
        wide("sb_qk", (2, 1)[u % 2], A["sb_w_in"][0], u * C)
    for u in range(2):
        wide("sb_v", (2, 1)[u], A["sb_w_in"][0], (4 + u) * C)
    for u, s in enumerate((0, 2)):
        down("sb_out", s, A["sb_w_out"][0], 4 * u, 4)
    ffn_up(1, (1, 0))
    ffn_down(1, (2, 0, 1, 2, 0, 1))
    gates = 4 * LH * LDH
    for c0, s in zip((0, C, gates + 8, gates + 8 + C, 2 * C, 3 * C, gates + 8 + 2 * C), (2, 0, 1, 2, 0, 1, 2)):
        wide("mix_in", s, A["w_in_2"][0], c0)
    for u, s in enumerate((0, 1)):
        down("mix_out", s, A["w_out_2"][0], 4 * u, 4)
    return units


class Link:

    def __init__(self, eng, sem):
        self.eng, self.sem, self.n, self.off = eng, sem, 0, None

    def __call__(self, ins):
        ins.then_inc(self.sem, 1)
        self.n += 1
        self.eng.wait_ge(self.sem, self.n if self.off is None else self.off + self.n)

    def enter(self, i, per):
        self.start, self.per, self.off = self.n, per, i * per

    def leave(self, trips):
        assert self.n - self.start == self.per, (self.n - self.start, self.per)
        self.n, self.off = self.start + trips * self.per, None


def build(nc, A, out):
    units = weight_plan(A)
    phases = {}
    for n, (phase, slot, _) in enumerate(units):
        phases.setdefault(phase, []).append(n)
    halves, count, n_halves = {}, {}, 0
    for phase, ns in phases.items():
        tail = units[ns[-1]][2][0][1]
        halves[phase], count[phase] = n_halves, 2 * len(ns) - (1 if tail == 2 else 0)
        n_halves += count[phase]
    PROJECTIONS = ("ret_out", "down0", "sb_out", "down1", "mix_out")
    holder, before = [None] * 6, []
    for n, (_, slot, _) in enumerate(units):
        before.append(holder[slot])
        holder[slot] = n

    with ExitStack() as ctx:
        def sb(name, shape, dt=F32):
            return ctx.enter_context(nc.sbuf_tensor(name, shape, dt))

        names = set()

        def sem(name):
            assert name not in names
            names.add(name)
            return ctx.enter_context(nc.semaphore(name))

        ring = [sb(f"ring{s}", [P, KD * C]) for s in range(3)]
        x = sb("x", [P, NT, D])
        xn = sb("xn", [P, NT, D])
        hT = sb("hT", [P, KD, T])
        const = sb("const", [P, NCONST])
        small = sb("small", [P, NSMALL])
        stat = sb("stat", [P, 64])
        credit = sb("credit", [P, 8])
        rowv = sb("rowv", [P, D])
        mods = sb("mods", [P, 4, KD])
        modr = sb("modr", [P, 4 * KD])
        gates = sb("gates", [P, 2, D])
        ARENA = 14912
        arena = sb("arena", [P, ARENA])
        with ExitStack() as split:
            hTh = split.enter_context(nc.sbuf_tensor("h_high", [P, KD, T], F32R))
            hTl = split.enter_context(nc.sbuf_tensor("h_low", [P, KD, T], F32R))
            w_hi = [split.enter_context(nc.sbuf_tensor(f"w_high{i}", [P, KD, T], F32R)) for i in range(2)]
            w_lo = [split.enter_context(nc.sbuf_tensor(f"w_low{i}", [P, KD, T], F32R)) for i in range(2)]
        ring += [sb(f"ring{s}", [P, KD * C]) for s in range(3, 6)]
        wide = [r[:, :].rearrange("p (k n) -> p k n", k=KD) for r in ring]
        tall = [r[:, :].rearrange("p (k n) -> p k n", k=4) for r in ring]

        def carve(start, *dims):
            n = int(np.prod(dims))
            assert start + n <= ARENA, (start, dims)
            v = arena[:, start:start + n]
            if len(dims) == 2:
                v = v.rearrange("p (a b) -> p a b", a=dims[0])
            if len(dims) == 3:
                v = v.rearrange("p (a b c) -> p a b c", a=dims[0], b=dims[1])
            return v

        ps = ctx.enter_context(nc.psum_tensor("ps", [P, 8, C], F32))

        def k_(name):
            a, b = CONST[name]
            return const[:, a:b]

        def s_(name):
            a, b = SMALL[name]
            return small[:, a:b]

        ident, ones, after, before_m, upto = (k_(n) for n in ("ident", "ones", "after", "before", "upto"))
        iota = k_("iota")

        ring_in = [sem(f"ring_in{s}") for s in range(6)]
        x_in, ident_in, const_in, small_in, row_in = [sem("x_in0"), sem("x_in1")], sem("ident_in"), sem("const_in"), sem("small_in"), sem("row_in")
        out_done = sem("out_done")
        x_new = sem("x_new")
        dve_chain, act_chain, over_chain = sem("dve_chain"), sem("act_chain"), sem("over_chain")
        norm_ss, norm_ms, norm_sd, norm_xn = sem("norm_ss"), sem("norm_ms"), sem("norm_sd"), sem("norm_xn")
        norm_tr, norm_ha, norm_hv = sem("norm_tr"), sem("norm_ha"), sem("norm_hv")
        norm_hi, norm_lo = sem("norm_high"), sem("norm_low")
        hi_done, lo_done, wide_mm = sem("hi_done"), sem("lo_done"), sem("wide_mm")
        src_hi, src_lo, tile0_mm = sem("src_high"), sem("src_low"), sem("tile0_mm")

        def update(k):
            return 4 * (k + 1)

        block = ctx.enter_context(nc.Block())

        b_ada = s_("b_ada")
        norm_src = [
            ((None, 16, 0), s_("ret_norm"), None),
            ((x_new, update(0), 2), s_("ffn_norm")[:, 0:KD], None),
            ((x_new, update(1), 2), s_("sb_norm"), None),
            ((x_new, update(2), 2), s_("ffn_norm")[:, KD:2 * KD], None),
            ((x_new, update(3), 2), None, None),
            ((x_new, update(3) + 2, 1), mods[:, 0, :], mods[:, 1, :]),
            ((x_new, update(4) + 2, 2), mods[:, 2, :], mods[:, 3, :]),
            ((x_new, update(5) + 2, 0), None, None),
        ]
        N_TR = [0, 1, 2, 3, None, 4, 5, None]

        def norm_act(act, r):
            s, whole, tile = norm_src[r][0]
            nc.scalar.activation(credit[:, 7:8], small[:, 0:1], ACT.Sqrt)
            for t in range(NT):
                act.wait_ge(x_in[t] if r == 0 else s, whole if t else whole - tile)
                nc.scalar.activation(xn[:, t, :], x[:, t, :], ACT.Square,
                                     accum_out=stat[:, t:t + 1]).then_inc(norm_ss, 1)
            act.wait_ge(norm_ms, r + 1)
            nc.scalar.activation(stat[:, 4:6], stat[:, 2:4], ACT.Sqrt).then_inc(norm_sd, 1)

        def norm_dve(dve, link, r):
            dve.wait_ge(norm_ss, NT * (r + 1))
            nc.vector.tensor_scalar(stat[:, 2:4], stat[:, 0:2], 1.0 / D, EPS, ALU.mult, ALU.add)\
                .then_inc(norm_ms, 1)
            dve.wait_ge(norm_sd, r + 1)
            link(nc.vector.reciprocal(stat[:, 6:8], stat[:, 4:6]))
            if N_TR[r] is None:
                return
            for t in range(NT):
                nc.vector.tensor_scalar(xn[:, t, :], x[:, t, :], stat[:, 6 + t:7 + t], None, ALU.mult)\
                    .then_inc(norm_xn, 1)

        def norm_pe(pe, r):
            n = N_TR[r]
            pe.wait_ge(norm_xn, NT * (n + 1))
            for j in range(4):
                for k in (2 * j, 2 * j + 1):
                    for t in range(NT):
                        last = nc.tensor.transpose(ps[:, j, (k % 2) * T + t * P:(k % 2) * T + (t + 1) * P],
                                                   xn[:, t, k * P:(k + 1) * P], ident)
                last.then_inc(norm_tr, 1)

        def split_norm(eng, r, which):
            n, (_, g, b) = N_TR[r], norm_src[r]
            if b is not None:
                norm_evict(eng, r, which)
                eng.wait_ge(norm_ha, 2 * (n - N_TR[5] + 1))
                eng.wait_ge(norm_hv, 2 * (n - N_TR[5] + 1))
            for j in range(4):
                if b is None and which == 0:
                    eng.wait_ge(norm_tr, 4 * n + j + 1)
                if which:
                    eng.wait_ge(norm_hi, 4 * n + j + 1)
                if b is not None:
                    ks = slice(2 * j, 2 * j + 2)
                    if which == 0:
                        last = nc.scalar.activation(hTh[:, ks, :], hT[:, ks, :], ACT.Copy)
                    else:
                        last = nc.vector.tensor_tensor(hTl[:, ks, :], hT[:, ks, :], hTh[:, ks, :].bitcast(F32),
                                                       ALU.subtract)
                else:
                    for k in (2 * j, 2 * j + 1):
                        src = ps[:, j, (k % 2) * T:(k % 2 + 1) * T]
                        if which == 0:
                            last = nc.scalar.activation(hTh[:, k, :], src, ACT.Identity, scale=g[:, k:k + 1])
                        else:
                            last = nc.vector.scalar_tensor_tensor(
                                out=hTl[:, k, :], in0=src, scalar=g[:, k:k + 1], in1=hTh[:, k, :].bitcast(F32),
                                op0=ALU.mult, op1=ALU.subtract)
                last.then_inc(norm_lo if which else norm_hi, 1)

        def norm_evict(eng, r, which):
            n, (_, g, b) = N_TR[r], norm_src[r]
            for j in (which, which + 2):
                eng.wait_ge(norm_tr, 4 * n + j + 1)
                for k in (2 * j, 2 * j + 1):
                    src = ps[:, j, (k % 2) * T:(k % 2 + 1) * T]
                    if which == 0:
                        last = nc.scalar.activation(hT[:, k, :], src, ACT.Identity, scale=g[:, k:k + 1],
                                                    bias=b[:, k:k + 1])
                    else:
                        last = nc.vector.tensor_scalar(hT[:, k, :], src, g[:, k:k + 1], b[:, k:k + 1],
                                                       ALU.mult, ALU.add)
                last.then_inc(norm_hv if which else norm_ha, 1)

        def normed(pe, r):
            pe.wait_ge(norm_lo, 4 * (N_TR[r] + 1))

        def tiles_normed(pe, r, k):
            pe.wait_ge(norm_lo, 4 * N_TR[r] + k // 2 + 1)

        def normed_whole(pe, r):
            pe.wait_ge(norm_ha, 2 * (r - 4))
            pe.wait_ge(norm_hv, 2 * (r - 4))

        def arrivals(n):
            slot = units[n][1]
            return 16 * sum(len(units[m][2]) for m in range(n + 1) if units[m][1] == slot)

        last_fill = [arrivals(holder[s]) if s < 3 else 0 for s in range(6)]

        def pieces(phase, slot, j, bufs):
            for c in range(2):
                ks = slice(c * (KD // 2), (c + 1) * (KD // 2))
                if phase in PROJECTIONS:
                    flat = [b[:, :, :].rearrange("p k n -> p (k n)")[:, c * D:(c + 1) * D] for b in bufs]
                    yield tall[slot][:, 2 * j + c, :], flat
                elif phase.startswith("up"):
                    raw = ring[slot][:, :].rearrange("p (k g j n) -> p k g j n", k=KD, g=2, j=2)[:, ks, :, j, :]
                    yield raw, [b[:, ks, :].rearrange("p k (g n) -> p k g n", g=2) for b in bufs]
                else:
                    yield wide[slot][:, ks, j * T:(j + 1) * T], [b[:, ks, :] for b in bufs]

        def split_high(act, phase, h, i=None, per=0):
            n, m = phases[phase][h // 2], halves[phase] + h
            slot, off = units[n][1], (0 if i is None else i * (per // 4 * 16 * len(units[n][2])))
            act.wait_ge(ring_in[slot], off + arrivals(n))
            if m >= 2:
                act.wait_ge(wide_mm, (m - 1) if i is None else i * per + (m - 1))
            for raw, (hi,) in pieces(phase, slot, h % 2, (w_hi[m % 2],)):
                nc.scalar.activation(hi, raw, ACT.Copy).then_inc(hi_done, 1)

        def split_low(dve, phase, h, i=None, per=0, eng=nc.vector):
            n, m = phases[phase][h // 2], halves[phase] + h
            slot = units[n][1]
            for c, (raw, (hi, lo)) in enumerate(pieces(phase, slot, h % 2, (w_hi[m % 2], w_lo[m % 2]))):
                dve.wait_ge(hi_done, (2 * m + c + 1) if i is None else i * (2 * per) + (2 * m + c + 1))
                last = eng.tensor_tensor(lo, raw, hi.bitcast(F32), ALU.subtract)
            last.then_inc(lo_done, 1)

        def src_count(phase, h):
            return sum(count[p] for p in PROJECTIONS[:PROJECTIONS.index(phase)]) + h

        def src_high(act, phase, src, h, ready):
            act.wait_ge(*ready(h))
            ks = slice(2 * (h % 4), 2 * (h % 4) + 2)
            nc.scalar.activation(hTh[:, ks, :], src[:, 2 * h:2 * h + 2, :], ACT.Copy).then_inc(src_hi, 1)

        def src_low(dve, phase, src, h):
            dve.wait_ge(src_hi, src_count(phase, h) + 1)
            ks = slice(2 * (h % 4), 2 * (h % 4) + 2)
            nc.vector.tensor_tensor(hTl[:, ks, :], src[:, 2 * h:2 * h + 2, :], hTh[:, ks, :].bitcast(F32),
                                    ALU.subtract).then_inc(src_lo, 1)

        def project_act(act, phase, src, ready, done=0):
            n = count[phase]
            wide_done(act, halves[phase])
            for h in range(done, min(4, n)):
                src_high(act, phase, src, h, ready)
            for h in range(n):
                if h + 2 < n:
                    wide_done(act, halves[phase] + h + 1)
                    split_high(act, phase, h + 2)
                if h + 4 < n:
                    src_high(act, phase, src, h + 4, ready)

        def project_dve(dve, phase, src, between=None, done=0):
            n = count[phase]
            for h in range(done, min(4, n)):
                src_low(dve, phase, src, h)
            for h in range(n):
                if h + 2 < n:
                    split_low(dve, phase, h + 2)
                if h + 4 < n:
                    src_low(dve, phase, src, h + 4)
                if between is not None:
                    between(h)

        def wide_done(eng, n, i=None, per=0):
            eng.wait_ge(wide_mm, n if i is None else i * per + n)

        def split_ready(pe, phase, h, i=None, per=0):
            m = halves[phase] + h
            pe.wait_ge(lo_done, (m + 1) if i is None else i * per + (m + 1))
            return m % 2

        def by_feature(bank, buf, r=None):
            for f in range(2):
                o = ps[:, bank, f * T:(f + 1) * T]
                for k in range(KD):
                    if r is not None and f == 0 and k % 2 == 0:
                        tiles_normed(nc.tensor, r, k)
                    hi, lo = w_hi[buf][:, k, f * P:(f + 1) * P], w_lo[buf][:, k, f * P:(f + 1) * P]
                    nc.tensor.matmul(o, hi, hTh[:, k, :], start=(k == 0), stop=False)
                    nc.tensor.matmul(o, hi, hTl[:, k, :], start=False, stop=False)
                    last = nc.tensor.matmul(o, lo, hTh[:, k, :], start=False, stop=(k == KD - 1))
            return last

        def by_token(bank, buf, c):
            for t in range(NT):
                o = ps[:, bank + t, c * T:(c + 1) * T]
                for k in range(KD):
                    hi, lo = hTh[:, k, t * P:(t + 1) * P], hTl[:, k, t * P:(t + 1) * P]
                    nc.tensor.matmul(o, hi, w_hi[buf][:, k, :], start=(k == 0), stop=False)
                    nc.tensor.matmul(o, hi, w_lo[buf][:, k, :], start=False, stop=False)
                    last = nc.tensor.matmul(o, lo, w_hi[buf][:, k, :], start=False, stop=(k == KD - 1))
            return last

        def project(pe, phase):
            n = count[phase]
            for h in range(n):
                buf = split_ready(pe, phase, h)
                pe.wait_ge(src_lo, src_count(phase, h) + 1)
                w = [b[:, :, :].rearrange("p k n -> p (k n)") for b in (w_hi[buf], w_lo[buf])]
                for t in range(NT):
                    for kc in range(2):
                        first, end = (h == 0 and kc == 0), (h == n - 1 and kc == 1)
                        hi, lo = (s[:, 2 * (h % 4) + kc, t * P:(t + 1) * P] for s in (hTh, hTl))
                        for a, b, c in ((hi, 0, 0), (hi, 1, 1), (lo, 0, 2)):
                            for half in range(2):
                                cols = slice(kc * D + half * C, kc * D + (half + 1) * C)
                                last = nc.tensor.matmul(ps[:, 4 + 2 * t + half, :], a, w[b][:, cols],
                                                        start=(first and c == 0), stop=(end and c == 2))
                    if h == n - 1 and t == 0:
                        last.then_inc(tile0_mm, 1)
                last.then_inc(wide_mm, 1)

        def gated_residual(link, g, bank, tmp, signal, tiles=range(NT)):
            for t in tiles:
                for half in range(2):
                    last = nc.vector.tensor_tensor(tmp[:, t, half * C:(half + 1) * C], ps[:, bank + 2 * t + half, :],
                                                   gates[:, g, half * C:(half + 1) * C], ALU.mult)
            link(last)
            for t in tiles:
                ins = nc.vector.tensor_tensor(x[:, t, :], x[:, t, :], tmp[:, t, :], ALU.add)
                if signal:
                    ins.then_inc(x_new, 2)
            if not signal:
                link(ins)

        def residual(dve, phase):
            for t in range(NT):
                if t == 0:
                    dve.wait_ge(tile0_mm, PROJECTIONS.index(phase) + 1)
                else:
                    wide_done(dve, halves[phase] + count[phase])
                for half in range(2):
                    xs = x[:, t, half * C:(half + 1) * C]
                    nc.vector.tensor_tensor(xs, ps[:, 4 + 2 * t + half, :], xs, ALU.add).then_inc(x_new, 1)

        freed = {}
        for phase, ns in phases.items():
            for i, n in enumerate(ns):
                freed[n] = (lo_done, halves[phase] + min(2 * (i + 1), count[phase]))

        qk = carve(0, 8, C)
        vg = carve(4096, NT, 2 * RV)
        yT = carve(0, 2 * KD, T)
        rot_a, rot_b = xn[:, 0, 0:C], xn[:, 0, C:2 * C]
        r_sc = carve(12288, 2, TRI)
        rqk_free, rqk_out = sem("rqk_free"), sem("rqk_out")
        rvg_fa, rvg_fv = sem("rvg_fa"), sem("rvg_fv")
        rg_silu = sem("rg_silu")
        r_s, r_d, r_o, r_sq, r_ms, r_sd, r_y, r_t, r_ta, r_tv = (
            sem("r_" + n) for n in ("scores", "decayed", "o", "squares", "means", "roots", "y", "turned",
                                    "yT_a", "yT_v"))

        hff = carve(0, FP, T)
        cv = carve(5632, 2, C)
        ada_w = [carve(6656, 4, C), gates[:, :, :].rearrange("p a (b n) -> p (a b) n", n=C)]
        ada_acc = carve(8704, 12 * C)
        ADA_POOL = 10
        up_id, up_cv, up_free, up_si, up_h = (
            sem("up_" + n) for n in ("identity", "convolved", "free", "silu", "h"))
        ada_in = [sem("ada_in0"), sem("ada_in1")]
        ada_chain, ada_used, ada_sum, ada_mods, ada_gate, ada_c, bias_in = (
            sem("ada_" + n) for n in ("chain", "used", "sum", "mods", "gate", "c", "bias_in"))

        def sb_extra(buf):
            flat = buf[:, :, :].rearrange("p a b -> p (a b)")
            return [flat[:, 2 * TRI * i:2 * TRI * (i + 1)].rearrange("p (a b) -> p a b", a=2) for i in range(2)]

        sqk = carve(0, 8, C)
        sqk_t = sqk.rearrange("p a (b t) -> p (a b) t", b=2)
        sv = carve(4096, NT, D)
        z_b = [carve(6144 + 768 * i, 2, TRI) for i in range(2)] + sb_extra(xn)
        l_b = [carve(7680 + 768 * i, 2, TRI) for i in range(2)] + sb_extra(hT)
        sp_b = [carve(9216 + 768 * i, 2, TRI) for i in range(2)]
        a_b = [carve(10752 + 768 * i, 2, TRI) for i in range(2)]
        soT = carve(12288, KD, T)
        sqk_fa, sqk_fv, sv_a, sv_v = (
            sem("s_" + n) for n in ("qk_fa", "qk_fv", "v_a", "v_v"))
        s_z, s_zc, s_l, s_sp, s_m1, s_ex, s_la, s_a, s_m2, s_o, s_ot = (
            sem("s_" + n) for n in ("z", "zcopy", "log", "softplus", "masked", "excl", "log_a", "a", "a_masked",
                                    "o", "oT"))

        qkm = carve(0, 2 * LH, T)
        qka = carve(2048, 2 * MH // 2, T)
        vm = carve(4096, NT, LH * (LDH + 1))
        om = carve(5128, NT, C)
        va = carve(6152, NT, C)
        hm = carve(7176, NT, C)
        mixT = xn[:, :, :].rearrange("p a (b t) -> p (a b) t", t=T)
        cvm = carve(8200, 2, T)
        w8 = carve(8712, KD, 8)
        bg = carve(8776, 4)
        ghead = carve(8780, C)
        rows4 = carve(9292, 9, T)
        acol = carve(11596, NT, 4)
        fcol = carve(11604, NT, 4)
        sel4 = carve(11612, 4, P)
        wt = carve(12124, 2, TRI)
        pt = carve(12892, 2, TRI)
        m_sc = [carve(13660, TRI), carve(13660 + TRI, TRI), hT[:, 0:2, :].rearrange("p a b -> p (a b)")[:, 0:TRI]]
        mst = carve(14428, 128)
        mi_id, mi_cv, mi_si, mi_ev_a, mi_ev_v, mi_g = (
            sem("mi_" + n) for n in ("identity", "convolved", "silu", "ev_a", "ev_v", "gates"))
        mix_small = sem("mix_small")
        MIX = 2 * len(phases["mix_in"])
        l_f, l_floor, l_ln, l_rows, l_tr, l_cols, l_sig = (
            sem("l_" + n) for n in ("forget", "floor", "ln", "rows", "turned", "cols", "sigmoid"))
        l_s, l_w, l_e, l_p, l_o, l_h, l_sq, l_ms, l_sd, l_hn, l_t, l_mt = (
            sem("l_" + n) for n in ("scores", "w", "expw", "p", "o", "h", "squares", "means", "roots", "hn",
                                    "hT", "mixT"))
        b_s, b_mx, b_e, b_p, b_t, b_tc, b_o, b_oc = (
            sem("b_" + n) for n in ("scores", "max", "exp", "p", "pT", "pT_copy", "o", "oT"))

        EP = NE + 4
        wr = carve(14560, KD, NG + NE)
        br = carve(14848, NG + NE)
        lg = carve(324, NT, NG + NE)
        g8 = carve(396, NT, 8)
        m8 = carve(412, NT, 8)
        i8 = carve(428, NT, 8).bitcast(U32)
        f8 = carve(444, NT, 8)
        oh = carve(460, NT, NG)
        em = carve(476, NT, NE)
        oh1 = carve(540, NT, NE)
        oh2 = carve(604, NT, NE)
        asg = carve(668, NT, NE)
        wgt = carve(732, NT, EP)
        pos = carve(804, NT, EP)
        rst = carve(876, 64)
        flag = carve(940, 1).bitcast(I32)
        sel = carve(1024, NT, P)
        selw = carve(1280, NT, P)
        selT = carve(1536, T)
        gtmp = carve(4864, NT, D)
        xg = carve(1792, KD, P)
        hs = carve(2816, DE)
        hg = carve(3328, DE)
        hgT = carve(6912, KE, P)
        ye = carve(3840, D)
        r_in, t_lg, t_rank, t_flag, t_top, t_exp = (sem("t_" + n) for n in ("router_in", "logits", "rank", "flag", "top", "exp"))
        m_zero, m_start, m_s, m_sw, m_ga, m_xa, m_xv, m_gu, m_si, m_h, m_ht, m_hc, m_tr, m_sct, m_swt, m_dn, m_ya, m_yv = (
            sem("m_" + n) for n in ("zeroed", "started", "select", "select_w", "gathered", "xg_a", "xg_v", "gate_up",
                                    "silu", "h", "h_turned", "hT", "turned", "scattered", "selT", "down", "y_a", "y_v"))

        def yT_ready(h):
            return (r_tv if h % 2 else r_ta), h // 2 + 1

        def hff_ready(l):
            return lambda h: (up_h, FP * l + 2 * h + 2)

        def soT_ready(h):
            return s_ot, 2 * h + 2

        def mixT_ready(h):
            return (l_mt, h + 1) if h < 2 else (b_oc, 2 * (h - 2) + 2)

        @block.sync
        def _(sp):
            x_tiles = A["x"][0].rearrange("(t p) d -> p t d", p=P)
            sp.dma_start(x[:, 0, :], x_tiles[:, 0, :]).then_inc(x_in[0], 16)
            sp.dma_start(x[:, 1, :], x_tiles[:, 1, :]).then_inc(x_in[1], 16)
            sp.dma_start(const[:, 0:P], A["const"][:, 0:P]).then_inc(ident_in, 16)
            sp.dma_start(small[:, :], A["small"]).then_inc(small_in, 16)

            def fill(n):
                _, slot, parts = units[n]
                return [sp.dma_start(wide[slot][:, :, part[1][0]:part[1][1]] if part[0] is not None
                                     else tall[slot][:, 0:part[1], :], part[2]) for part in parts]

            for n in range(len(units)):
                if before[n] is not None:
                    sp.wait_ge(*freed[before[n]])
                if n == 1:
                    sp.dma_start(const[:, P:], A["const"][:, P:]).then_inc(const_in, 16)
                _, slot, parts = units[n]
                if len(parts) == 1:
                    fill(n)[0].then_inc(ring_in[slot], 16)
                else:
                    for half, d in enumerate(fill(n)):
                        d.then_inc(ring_in[slot], 16)

            def expert_unit(slot, e):
                name, shape = (("w_expert_gate_2", 0), ("w_expert_up_2", 0), ("w_expert_down_2", 1))[slot % 3]
                w = A[name][0]
                if shape:
                    src = w[bass.ds(e, 1)].rearrange("a (k p) n -> p (a k) n", p=P)
                    sp.dma_start(tall[slot][:, :, :], src).then_inc(ring_in[slot], 16)
                else:
                    src = w[bass.ds(e, 1)].rearrange("a (k p) n -> p (a k) n", p=P)
                    sp.dma_start(wide[slot][:, :, :], src).then_inc(ring_in[slot], 16)

            LOADS = (0, 3, 1, 4, 2, 5)

            def expert_pairs(r):
                def one(i, first):
                    for slot in (2, 0, 1, 3, 4, 5) if first else LOADS:
                        if first and slot >= 3:
                            sp.wait_ge(wide_mm, n_halves)
                        elif first:
                            sp.wait_ge(*freed[holder[slot]])
                        elif slot % 3 < 2:
                            sp.wait_ge(m_gu, i * 2 + (PAIRS * 2 * r - 1 + slot % 3))
                        else:
                            sp.wait_ge(m_dn, i + PAIRS * r)
                        expert_unit(slot, i * 2 + slot // 3)
                if r == 0:
                    one(0, True)
                with sp.Fori(1 if r == 0 else 0, PAIRS) as i:
                    one(i, False)

            expert_pairs(0)
            sp.wait_ge(t_flag, 1)
            most = sp.value_load(flag[0:1, 0:1])
            with sp.If(most > R):
                for r in range(1, PASSES):
                    expert_pairs(r)
            for t in range(NT):
                sp.wait_ge(x_new, update(5) + 3 + t)
                sp.dma_start(out[0].rearrange("(t p) d -> p t d", p=P)[:, t, :], x[:, t, :]).then_inc(out_done, 16)
            sp.wait_ge(out_done, 16 * NT)

        @block.gpsimd
        def _(pool):
            pool.dma_start(rowv[:, :], A["final_norm"].rearrange("(a d) -> a d", a=1).broadcast_to([P, D]))\
                .then_inc(row_in, 16)
            w_ada = A["w_ada_2"][0].rearrange("(p c) n -> p c n", p=P)
            pool.wait_ge(r_t, 2 * RH)
            for kh in range(2):
                pool.dma_start(ada_w[kh], w_ada[:, 4 * kh:4 * kh + 4, 0:C]).then_inc(ada_in[kh], 16)
            pool.wait_ge(ada_c, 1)

            def ada_load(nb, kh):
                pool.dma_start(ada_w[kh], w_ada[:, 4 * kh:4 * kh + 4, bass.ds(nb * C, C)]).then_inc(ada_in[kh], 16)

            n = 0
            for nb in range(ADA_POOL):
                for kh, w in enumerate(ada_w):
                    acc = ada_acc[:, nb * C:(nb + 1) * C]
                    scale = stat[:, 16 + 4 * kh:20 + 4 * kh].unsqueeze(2).broadcast_to([P, 4, C])
                    pool.wait_ge(ada_in[kh], nb * 16 + 16)
                    steps = [(w, w, scale, ALU.mult), (w[:, 0:2, :], w[:, 0:2, :], w[:, 2:4, :], ALU.add)]
                    if kh == 0:
                        steps += [(acc, w[:, 0, :], w[:, 1, :], ALU.add)]
                    else:
                        steps += [(w[:, 0, :], w[:, 0, :], w[:, 1, :], ALU.add), (acc, acc, w[:, 0, :], ALU.add)]
                    for o, in0, in1, op in steps:
                        nc.gpsimd.tensor_tensor(o, in0, in1, op).then_inc(ada_chain, 1)
                        n += 1
                        pool.wait_ge(ada_chain, n)
                    ada_load(nb + 1, kh)
            nc.gpsimd.memset(credit[:, 1:2], 0.0).then_inc(ada_sum, 1)
            with pool.Fori(ADA_POOL + 1, 12) as nb:
                for kh in range(2):
                    pool.wait_ge(ada_used, nb * 2 + (kh + 1 - 2 * (ADA_POOL + 1)))
                    ada_load(nb, kh)
            pool.wait_ge(ada_used, 2 * (12 - ADA_POOL))
            for g, m in enumerate((2, 5)):
                pool.dma_start(gates[:, g, :], A["b_ada_2"][0:1, m * D:(m + 1) * D].broadcast_to([P, D]))\
                    .then_inc(bias_in, 16)

            def mask(buf, g, ready, done):
                pool.wait_ge(ready, g + 1)
                diag = buf[:, :, :].rearrange("p h (b t) -> p h b t", b=3)[:, :, 0:3:2, :]
                m = before_m.unsqueeze(1).unsqueeze(1).broadcast_to([P, 2, 2, P])
                nc.gpsimd.tensor_tensor(diag, diag, m, ALU.mult).then_inc(done, 1)

            pool.wait_ge(const_in, 16)
            for g in range(0, SH // 2, 2):
                for d in range(2):
                    mask(sp_b[d], g + d, s_sp, s_m1)
                if g >= 2:
                    for d in range(2):
                        mask(a_b[d], g - 2 + d, s_a, s_m2)
            for d in range(2):
                mask(a_b[d], SH // 2 - 2 + d, s_a, s_m2)

            pool.wait_ge(x_new, update(2))
            pool.dma_start(w8, A["w_in_2"][0].rearrange("(k p) n -> p k n", p=P)[:, :, 4 * LH * LDH:4 * LH * LDH + 8])\
                .then_inc(mix_small, 16)
            pool.dma_start(bg[0:LH, 0:1], A["b_gates_2"][0:1, 0:LH].rearrange("a h -> h a")).then_inc(mix_small, 16)
            pool.dma_start(bg[0:LH, 1:2], A["b_gates_2"][0:1, LH:2 * LH].rearrange("a h -> h a")).then_inc(mix_small, 16)
            pool.dma_start(ghead, A["g_mlstm_head_2"][0:1, :].broadcast_to([P, C])).then_inc(mix_small, 16)
            pool.dma_start(sel4[0:LH, :, :].rearrange("p a b -> p (a b)"), A["sel4"]).then_inc(mix_small, 16)
            pool.dma_start(wr[:, :, 0:NG], A["w_router_group_2"][0].rearrange("(k p) n -> p k n", p=P)).then_inc(r_in, 16)
            pool.dma_start(wr[:, :, NG:], A["w_router_expert_2"][0].rearrange("(k p) n -> p k n", p=P)).then_inc(r_in, 16)
            pool.dma_start(br[:, 0:NG], A["b_router_group_2"][0:1, :].broadcast_to([P, NG])).then_inc(r_in, 16)
            pool.dma_start(br[:, NG:], A["b_router_expert_2"][0:1, :].broadcast_to([P, NE])).then_inc(r_in, 16)
            pool.wait_ge(x_new, update(3) + 2)
            pool.dma_start(rowv[:, :], A["g_final_2"].rearrange("(a d) -> a d", a=1).broadcast_to([P, D]))\
                .then_inc(row_in, 16)
            pool.wait_ge(lo_done, halves["mix_out"])
            for h in range(2):
                split_low(pool, "mix_out", h, eng=nc.gpsimd)

        @block.tensor
        def _(pe):
            pe.wait_ge(ident_in, 16)
            norm_pe(pe, 0)

            with pe.Fori(0, 2) as i:
                for h in range(4):
                    buf = split_ready(pe, "ret_qk", h, i, 4)
                    pe.wait_ge(rqk_free, i * 4 + (h + 1))
                    by_feature(h, buf, None if h else 0).then_inc(wide_mm, 1)
            with pe.Fori(0, 4) as i:
                for b in range(2):
                    pe.wait_ge(rvg_fa, i * 2 + (b + 1))
                    pe.wait_ge(rvg_fv, i * 2 + (b + 1))
                    for c in range(2):
                        buf = split_ready(pe, "ret_vg", 2 * b + c, i, 4)
                        by_token(2 * b + 4, buf, c).then_inc(wide_mm, 1)

            def ret_scores(h):
                if h >= 2:
                    pe.wait_ge(r_d, h - 1)
                for f in range(2):
                    nc.tensor.matmul(ps[:, h % 2, 0:T], qk[:, RH + h, f * T:f * T + P], qk[:, h, f * T:(f + 1) * T],
                                     start=(f == 0), stop=(f == 1))
                for f in range(2):
                    last = nc.tensor.matmul(ps[:, h % 2, T:TRI], qk[:, RH + h, f * T + P:(f + 1) * T],
                                            qk[:, h, f * T + P:(f + 1) * T], start=(f == 0), stop=(f == 1))
                last.then_inc(r_s, 1)

            def ret_out(h):
                pe.wait_ge(r_d, h + 1)
                if h >= 2:
                    pe.wait_ge(r_y, 2 * (h - 1))
                sc, v = r_sc[:, h % 2, :], vg[:, :, h * RDV:(h + 1) * RDV]
                ob = 2 + 2 * (h % 2)
                nc.tensor.matmul(ps[:, ob, :], sc[:, 0:P], v[:, 0, :], start=True, stop=True).then_inc(r_o, 1)
                nc.tensor.matmul(ps[:, ob + 1, :], sc[:, P:T], v[:, 0, :], start=True, stop=False)
                nc.tensor.matmul(ps[:, ob + 1, :], sc[:, T:TRI], v[:, 1, :], start=False, stop=True).then_inc(r_o, 1)

            def ret_turn(h):
                pe.wait_ge(r_y, 2 * (h + 1))
                for j in range(2):
                    if h >= 1:
                        pe.wait_ge(r_tv if j else r_ta, h)
                    for f in range(2):
                        for t in range(NT):
                            last = nc.tensor.transpose(
                                ps[:, 6 + j, f * T + t * P:f * T + (t + 1) * P],
                                vg[:, t, RV + h * RDV + (2 * j + f) * P:RV + h * RDV + (2 * j + f + 1) * P], ident)
                    last.then_inc(r_t, 1)

            pe.wait_ge(rqk_out, 8)
            ret_scores(0)
            ret_scores(1)
            pe.wait_ge(rvg_fa, 2 + 8)
            pe.wait_ge(rvg_fv, 2 + 8)
            for h in range(RH):
                ret_out(h)
                if h + 2 < RH:
                    ret_scores(h + 2)
                if h >= 1:
                    ret_turn(h - 1)
            ret_turn(RH - 1)
            pe.wait_ge(r_ta, RH)
            pe.wait_ge(r_tv, RH)
            project(pe, "ret_out")

            def ffn(l):

                with pe.Fori(0, 5) as i:
                    for h in range(4):
                        buf = split_ready(pe, f"up{l}", h, i, 4)
                        pe.wait_ge(up_free, i * 4 + ((FP + 4) * l + h + 1))
                        by_feature(h, buf, None if h else 2 * l + 1).then_inc(wide_mm, 1)
                for h in (20, 21):
                    buf = split_ready(pe, f"up{l}", h)
                    pe.wait_ge(up_free, (FP + 4) * l + h + 1)
                    by_feature(h % 4, buf).then_inc(wide_mm, 1)
                project(pe, f"down{l}")

            norm_pe(pe, 1)
            ffn(0)

            pe.wait_ge(const_in, 16)
            pe.wait_ge(ada_sum, 2)
            pe.wait_ge(x_new, update(1))
            for m, q in enumerate((0, 1, 3, 4)):
                for k in range(KD):
                    last = nc.tensor.matmul(ps[:, 3, m * KD + k:m * KD + k + 1],
                                            ada_acc[:, q * D + k * P:q * D + (k + 1) * P], ones[:, 0:1],
                                            start=True, stop=True)
            last.then_inc(ada_mods, 1)
            for g, q in enumerate((2, 5)):
                for half in range(2):
                    last = nc.tensor.matmul(ps[:, 4 + 2 * g + half, :], ones,
                                            ada_acc[:, q * D + half * C:q * D + (half + 1) * C],
                                            start=True, stop=True)
            last.then_inc(ada_mods, 1)
            pe.wait_ge(ada_gate, 1)
            norm_pe(pe, 2)

            with pe.Fori(0, 2) as i:
                for h in range(4):
                    buf = split_ready(pe, "sb_qk", h, i, 4)
                    pe.wait_ge(sqk_fv if h % 2 else sqk_fa, i * 2 + (h // 2 + 1))
                    by_feature(h, buf, None if h else 2).then_inc(wide_mm, 1)
            pe.wait_ge(ada_gate, 5)
            for h in range(4):
                buf = split_ready(pe, "sb_v", h)
                by_token(4 + 2 * (h // 2), buf, h % 2).then_inc(wide_mm, 1)

            def sb_z(g):
                if g == 0:
                    pe.wait_ge(sqk_fa, 2 + 4)
                    pe.wait_ge(sqk_fv, 2 + 4)
                if g >= 2:
                    pe.wait_ge(s_zc, g - 1)
                for hh in range(2):
                    rows = slice(hh * SDH, (hh + 1) * SDH)
                    q, k = sqk_t[rows, g, :], sqk_t[rows, KD + g, :]
                    bank = 2 * (g % 2) + hh
                    nc.tensor.matmul(ps[:, bank, 0:T], k[:, 0:P], q, start=True, stop=True)
                    last = nc.tensor.matmul(ps[:, bank, T:TRI], k[:, P:T], q[:, P:T], start=True, stop=True)
                last.then_inc(s_z, 1)

            def sb_excl(g):
                pe.wait_ge(s_m1, g + 1)
                if g == 0:
                    pe.wait_ge(sv_a, 2)
                    pe.wait_ge(sv_v, 2)
                else:
                    pe.wait_ge(s_la, g)
                for hh in range(2):
                    sp = sp_b[g % 2][:, hh, :]
                    nc.tensor.matmul(ps[:, 4 + hh, 0:T], after, sp[:, 0:T], start=True, stop=False)
                    nc.tensor.matmul(ps[:, 4 + hh, P:T], ones, sp[:, T:TRI], start=False, stop=True)
                    last = nc.tensor.matmul(ps[:, 4 + hh, T:TRI], after, sp[:, T:TRI], start=True, stop=True)
                last.then_inc(s_ex, 1)

            def sb_o(g):
                pe.wait_ge(s_m2, g + 1)
                if g >= 2:
                    pe.wait_ge(s_ot, g - 1)
                for hh in range(2):
                    h = 2 * g + hh
                    a = a_b[g % 2][:, hh, :]
                    o = ps[hh * SDH:(hh + 1) * SDH, 6 + g % 2, :]
                    nc.tensor.matmul(o[:, 0:T], sv[:, 0, h * SDH:(h + 1) * SDH], a[:, 0:T], start=True, stop=False)
                    last = nc.tensor.matmul(o[:, P:T], sv[:, 1, h * SDH:(h + 1) * SDH], a[:, T:TRI],
                                            start=False, stop=True)
                last.then_inc(s_o, 1)

            GROUPS = SH // 2
            for g in range(4):
                sb_z(g)
            for g in range(0, GROUPS, 2):
                sb_excl(g)
                if g >= 2:
                    sb_o(g - 2)
                    sb_o(g - 1)
                sb_excl(g + 1)
                for z in (g + 4, g + 5):
                    if z < GROUPS:
                        sb_z(z)
            sb_o(GROUPS - 2)
            sb_o(GROUPS - 1)
            pe.wait_ge(s_ot, SH // 2)
            project(pe, "sb_out")

            norm_pe(pe, 3)
            ffn(1)

            norm_pe(pe, 5)
            normed_whole(pe, 5)
            pe.wait_ge(mix_small, 80)
            for g in range(2):
                for k in range(KD):
                    last = nc.tensor.matmul(ps[0:LH, 4 + g, 0:T], w8[:, k, g * LH:(g + 1) * LH], hT[:, k, :],
                                            start=(k == 0), stop=(k == KD - 1))
            last.then_inc(mi_g, 1)
            normed(pe, 5)
            for h in range(MIX):
                buf = split_ready(pe, "mix_in", h)
                if 4 <= h < 8:
                    pe.wait_ge(mi_cv, h - 3)
                if h >= 8 and h % 2 == 0:
                    pe.wait_ge(mi_ev_a, (h - 8) // 2 + 1)
                    pe.wait_ge(mi_ev_v, (h - 8) // 2 + 1)
                if h < 8:
                    by_feature(h % 4, buf).then_inc(wide_mm, 1)
                else:
                    by_token(2 * (h // 2 % 2), buf, h % 2).then_inc(wide_mm, 1)

            pe.wait_ge(l_rows, 1)
            for n, row in enumerate((4, 7)):
                for t in range(NT):
                    last = nc.tensor.transpose(ps[:, 6, (2 * n + t) * 4:(2 * n + t) * 4 + 4],
                                               rows4[0:LH, row, t * P:(t + 1) * P], ident[0:LH, 0:LH])
            last.then_inc(l_tr, 1)
            pe.wait_ge(mi_ev_a, 5)
            pe.wait_ge(mi_ev_v, 5)
            pe.wait_ge(mi_si, 4)

            def ls_scores(h):
                b = 3 * (h % 2)
                if h >= 2:
                    pe.wait_ge(l_p, h - 1)
                nc.tensor.matmul(ps[:, b, 0:T], sel4[0:LH, h, :], rows4[0:LH, 6, :], start=True, stop=True)
                nc.tensor.matmul(ps[:, b + 1, 0:T], qkm[:, LH + h, 0:P], qkm[:, h, :], start=True, stop=True)
                nc.tensor.matmul(ps[:, b + 1, T:TRI], qkm[:, LH + h, P:T], qkm[:, h, P:T], start=True, stop=True)\
                    .then_inc(l_s, 1)

            def ls_out(h):
                b = 3 * (h % 2) + 2
                pe.wait_ge(l_p, h + 1)
                if h >= 2:
                    pe.wait_ge(l_h, h - 1)
                v = vm.rearrange("p t (h e) -> p t h e", h=LH)
                E1 = LDH + 1
                nc.tensor.matmul(ps[:, b, 0:E1], pt[:, h % 2, 0:P], v[:, 0, h, :], start=True, stop=True)
                nc.tensor.matmul(ps[:, b, T:T + E1], pt[:, h % 2, P:T], v[:, 0, h, :], start=True, stop=False)
                nc.tensor.matmul(ps[:, b, T:T + E1], pt[:, h % 2, T:TRI], v[:, 1, h, :], start=False, stop=True)\
                    .then_inc(l_o, 1)

            ls_scores(0)
            ls_scores(1)
            for h in range(LH):
                ls_out(h)
                if h + 2 < LH:
                    ls_scores(h + 2)

            def mb_scores(h):
                if h == 0:
                    pe.wait_ge(l_cols, 1)
                if h >= 2:
                    pe.wait_ge(b_mx, h - 1)
                rows = slice((h % 2) * MDH, (h % 2 + 1) * MDH)
                q, k = qka[rows, h // 2, :], qka[rows, MH // 2 + h // 2, :]
                bank = 6 + h % 2
                nc.tensor.matmul(ps[:, bank, 0:P], q[:, 0:P], k[:, 0:P], start=True, stop=True)
                nc.tensor.matmul(ps[:, bank, P:TRI], q[:, P:T], k, start=True, stop=True).then_inc(b_s, 1)

            def mb_turn(h):
                pe.wait_ge(b_p, h + 1)
                if h >= 2:
                    pe.wait_ge(b_tc, h - 1)
                if h == 0:
                    pe.wait_ge(l_h, LH)
                sc = m_sc[h % 3]
                for blk in range(3):
                    last = nc.tensor.transpose(ps[:, h % 2, blk * P:(blk + 1) * P], sc[:, blk * P:(blk + 1) * P], ident)
                last.then_inc(b_t, 1)

            def mb_out(h):
                pe.wait_ge(b_tc, h + 1)
                if h >= 4 and h % 2 == 0:
                    pe.wait_ge(b_oc, h // 2 - 1)
                o = ps[(h % 2) * MDH:(h % 2 + 1) * MDH, 3 + (h // 2) % 2, :]
                p_ = wt[:, h % 2, :]
                cols = slice(h * MDH, (h + 1) * MDH)
                nc.tensor.matmul(o[:, 0:T], va[:, 0, cols], p_[:, 0:T], start=True, stop=False)
                nc.tensor.matmul(o[:, P:T], va[:, 1, cols], p_[:, T:TRI], start=False, stop=True).then_inc(b_o, 1)

            mb_scores(0)
            mb_scores(1)
            for h in range(MH):
                if h + 2 < MH:
                    mb_scores(h + 2)
                mb_turn(h)
                if h >= 1:
                    mb_out(h - 1)
            mb_out(MH - 1)

            pe.wait_ge(l_hn, 2 * LH)
            pe.wait_ge(b_tc, MH)
            for j in range(2):
                for f in range(2):
                    for t in range(NT):
                        last = nc.tensor.transpose(ps[:, j, f * T + t * P:f * T + (t + 1) * P],
                                                   hm[:, t, (2 * j + f) * P:(2 * j + f + 1) * P], ident)
                last.then_inc(l_t, 1)
            pe.wait_ge(l_mt, 2)
            pe.wait_ge(b_oc, MH // 2)
            project(pe, "mix_out")

            norm_pe(pe, 6)
            normed_whole(pe, 6)
            pe.wait_ge(r_in, 64)
            for t in range(NT):
                for k in range(KD):
                    last = nc.tensor.matmul(ps[:, 4, t * 64:t * 64 + NG + NE], hT[:, k, t * P:(t + 1) * P],
                                            wr[:, k, :], start=(k == 0), stop=(k == KD - 1))
            last.then_inc(t_lg, 1)
            pe.wait_ge(t_rank, 1)
            nc.tensor.matmul(ps[:, 5, 0:NE], before_m, asg[:, 0, :], start=True, stop=True)
            nc.tensor.matmul(ps[:, 5, 64:64 + NE], ones, asg[:, 0, :], start=True, stop=False)
            nc.tensor.matmul(ps[:, 5, 64:64 + NE], before_m, asg[:, 1, :], start=False, stop=True)
            nc.tensor.matmul(ps[:, 5, 128:128 + NE], ones, asg[:, 0, :], start=True, stop=False)
            nc.tensor.matmul(ps[:, 5, 128:128 + NE], ones, asg[:, 1, :], start=False, stop=True).then_inc(t_lg, 1)

            def gather(value, hgt):
                pe.wait_ge(m_s, value)
                for half in (1, 0):
                    if half == 0 and hgt is not None:
                        pe.wait_ge(m_hc, hgt)
                    for k in range(4 * half, 4 * half + 4):
                        for t in range(NT):
                            last = nc.tensor.matmul(ps[:, 4 + half, (k % 4) * P:(k % 4 + 1) * P],
                                                    xn[:, t, k * P:(k + 1) * P], sel[:, t, :],
                                                    start=(t == 0), stop=(t == NT - 1))
                    last.then_inc(m_ga, 1)

            def scatter(stop):
                for t in range(NT):
                    for half in range(2):
                        last = nc.tensor.matmul(ps[:, 2 * t + half, :], selT[:, t * P:(t + 1) * P],
                                                ye[:, half * C:(half + 1) * C], start=False, stop=stop,
                                                skip_group_check=True)
                last.then_inc(m_sct, 1)

            def expert_pass(r):
                pe.wait_ge(m_zero, 3 * (r + 1))
                for b in range(4):
                    last = nc.tensor.matmul(ps[:, b, :], selT[:, 0:P], ye[:, 0:C], start=True, stop=False,
                                            skip_group_check=True)
                last.then_inc(m_start, 1)
                gather((PAIRS + 2) * r + 1, None)
                with pe.Fori(0, PAIRS) as i:
                    pe.wait_ge(m_xa, i + ((PAIRS + 1) * r + 1))
                    pe.wait_ge(m_xv, i + ((PAIRS + 1) * r + 1))
                    for g in range(2):
                        for s in (g, 3 + g):
                            pe.wait_ge(ring_in[s], i * 16 + (last_fill[s] + 16 * (PAIRS * r + 1)))
                        for k in range(KD):
                            for e in range(2):
                                last = nc.tensor.matmul(ps[e * R:(e + 1) * R, 4 + g, :], xg[:, k, e * R:(e + 1) * R],
                                                        wide[3 * e + g][:, k, :], start=(k == 0), stop=(k == KD - 1))
                        last.then_inc(m_gu, 1)
                    pe.wait_ge(m_sw, i + ((PAIRS + 1) * r + 1))
                    pe.wait_ge(m_ya, i + ((PAIRS + 1) * r + 1))
                    for t in range(NT):
                        last = nc.tensor.transpose(ps[:, 6, t * P:(t + 1) * P], selw[:, t, :], ident)
                    last.then_inc(m_tr, 1)
                    pe.wait_ge(m_yv, i + ((PAIRS + 1) * r + 1))
                    scatter(False)
                    pe.wait_ge(m_h, i + (PAIRS * r + 1))
                    for k in range(KE):
                        last = nc.tensor.transpose(ps[:, 4, k * P:(k + 1) * P], hg[:, k * P:(k + 1) * P], ident)
                    last.then_inc(m_ht, 1)
                    gather(i + ((PAIRS + 2) * r + 2), i + (PAIRS * r + 1))
                    pe.wait_ge(m_swt, i + (PAIRS * r + 1))
                    for s in (2, 5):
                        pe.wait_ge(ring_in[s], i * 16 + (last_fill[s] + 16 * (PAIRS * r + 1)))
                    for half in range(2):
                        for k in range(KE):
                            for e in range(2):
                                last = nc.tensor.matmul(ps[e * R:(e + 1) * R, 6 + half, :],
                                                        hgT[:, k, e * R:(e + 1) * R],
                                                        tall[3 * e + 2][:, k, half * C:(half + 1) * C],
                                                        start=(k == 0), stop=(k == KE - 1))
                    last.then_inc(m_dn, 1)
                pe.wait_ge(m_ya, (PAIRS + 1) * (r + 1))
                pe.wait_ge(m_yv, (PAIRS + 1) * (r + 1))
                scatter(True)

            expert_pass(0)
            pe.wait_ge(t_flag, 1)
            most = pe.value_load(flag[0:1, 0:1])
            with pe.If(most > R):
                for r in range(1, PASSES):
                    expert_pass(r)

        @block.scalar
        def _(act):
            link = Link(act, act_chain)
            act.wait_ge(small_in, 16)
            norm_act(act, 0)
            nc.scalar.activation(credit[:, 3:4], small[:, 0:1], ACT.Copy).then_inc(rvg_fa, 2)
            split_high(act, "ret_qk", 0)
            split_norm(act, 0, 0)
            split_high(act, "ret_qk", 1)
            with act.Fori(0, 2) as i:
                for h in range(4):
                    split_high(act, "ret_qk", h + 2, i, 4)

            def v_group(i, more):
                for h in range(4):
                    wide_done(act, halves["ret_vg"] + h + 1, i, 4)
                    if h % 2:
                        nc.scalar.activation(vg[:, 0, bass.ds(i * 2 * C + h // 2 * C, C)], ps[:, 4 + h - 1, :],
                                             ACT.Copy).then_inc(rvg_fa, 1)
                    if more or h < 2:
                        split_high(act, "ret_vg", h + 2, i, 4)

            with act.Fori(0, 3) as i:
                v_group(i, True)
            v_group(3, False)
            act.wait_ge(rvg_fv, 2 + 8)
            act.wait_ge(rvg_fa, 2 + 8)
            for t in range(NT):
                nc.scalar.activation(vg[:, t, RV:2 * RV], vg[:, t, RV:2 * RV], ACT.Silu).then_inc(rg_silu, 1)
            nc.scalar.activation(stat[:, 16:24], s_("c"), ACT.Silu).then_inc(ada_c, 1)

            def ret_squares(h):
                for t in range(NT):
                    act.wait_ge(r_o, 2 * h + t + 1)
                    nc.scalar.activation(xn[:, 1, 0:C], ps[:, 2 + 2 * (h % 2) + t, :], ACT.Square,
                                         accum_out=stat[:, 8 + t:9 + t]).then_inc(r_sq, 1)
                    act.wait_ge(r_sq, 2 * h + t + 1)
                act.wait_ge(r_ms, h + 1)
                nc.scalar.activation(stat[:, 12:14], stat[:, 10:12], ACT.Sqrt).then_inc(r_sd, 1)

            def ret_copy(h):
                act.wait_ge(r_t, 2 * h + 1)
                nc.scalar.activation(yT[:, 4 * h:4 * h + 2, :].rearrange("p a b -> p (a b)"), ps[:, 6, :], ACT.Copy)\
                    .then_inc(r_ta, 1)

            for h in range(RH):
                ret_squares(h)
                if h >= 1:
                    ret_copy(h - 1)
                if h < 2:
                    split_high(act, "ret_out", h)
            ret_copy(RH - 1)
            project_act(act, "ret_out", yT, yT_ready)

            def ffn(l):
                def pair(b, j, off, split):
                    n = off + (2 * b + j)
                    w0, b0 = SMALL["conv_w"][0], SMALL["conv_b"][0]
                    act.wait_ge(wide_mm, off + (halves[f"up{l}"] + 2 * b + j + 1))
                    if split is not None:
                        split_high(act, f"up{l}", 2 * b + j + 2, split, 8)
                    elif b < 2:
                        split_high(act, f"up{l}", off + 2 * b + j + 2)
                    else:
                        if j == 1:
                            src_high(act, f"down{l}", hff, 0, hff_ready(l))
                        split_high(act, f"down{l}", j)
                        if j == 1:
                            src_high(act, f"down{l}", hff, 1, hff_ready(l))
                    for gv in range(2):
                        at = (l * 2 + gv) * FP
                        last = nc.scalar.activation(
                            cv[:, j, gv * T:(gv + 1) * T], ps[:, (2 * b + j) % 4, gv * T:(gv + 1) * T], ACT.Identity,
                            scale=small[:, bass.ds(n * 3 + (w0 + at * 3 + 2), 1)],
                            bias=small[:, bass.ds(n + (b0 + at), 1)])
                    last.then_inc(up_id, 1)
                    act.wait_ge(up_cv, off + (FP * l + 2 * b + j + 1))
                    nc.scalar.activation(cv[:, j, 0:T], cv[:, j, 0:T], ACT.Silu).then_inc(up_si, 1)

                with act.Fori(0, 2) as i:
                    nc.scalar.activation(credit[:, 7:8], small[:, 0:1], ACT.Silu)
                    for b in range(4):
                        for j in range(2):
                            pair(b, j, i * 8, i)
                for b in range(3):
                    for j in range(2):
                        pair(b, j, 16, None)
                project_act(act, f"down{l}", hff, hff_ready(l), 2)

            split_high(act, "up0", 0)
            norm_act(act, 1)
            split_norm(act, 1, 0)
            split_high(act, "up0", 1)
            ffn(0)
            split_high(act, "sb_qk", 0)
            norm_act(act, 2)
            nc.scalar.activation(credit[:, 4:5], small[:, 0:1], ACT.Copy).then_inc(sqk_fa, 2)
            split_norm(act, 2, 0)
            split_high(act, "sb_qk", 1)

            with act.Fori(0, 2) as i:
                for h in range(4):
                    wide_done(act, halves["sb_qk"] + h + 1, i, 4)
                    if h % 2 == 0:
                        nc.scalar.activation(sqk[:, i * 4 + h, :], ps[:, h, :], ACT.Copy).then_inc(sqk_fa, 1)
                    split_high(act, "sb_qk", h + 2, i, 4)
            for h in range(4):
                wide_done(act, halves["sb_v"] + h + 1)
                if h % 2:
                    u = h // 2
                    nc.scalar.activation(sv[:, 0, u * C:(u + 1) * C], ps[:, 4 + 2 * u, :], ACT.Copy).then_inc(sv_a, 1)
                if h < 2:
                    split_high(act, "sb_v", h + 2)

            def sb_log(gs):
                for g in gs:
                    z = ps[:, 2 * (g % 2):2 * (g % 2) + 2, 0:TRI]
                    act.wait_ge(s_z, g + 1)
                    if g >= 4:
                        act.wait_ge(s_la, g - 3)
                    link(nc.scalar.activation(l_b[g % 4], z, ACT.Abs, scale=SDH ** -0.5))
                    nc.scalar.activation(z_b[g % 4], z, ACT.Copy, scale=SDH ** -0.5).then_inc(s_zc, 1)
                    link(nc.scalar.activation(l_b[g % 4], l_b[g % 4], ACT.Exp, scale=-1.0))
                for g in gs:
                    nc.scalar.activation(l_b[g % 4], l_b[g % 4], ACT.Ln, bias=1.0).then_inc(s_l, 1)

            def sb_exp(g):
                act.wait_ge(s_la, g + 1)
                nc.scalar.activation(a_b[g % 2], a_b[g % 2], ACT.Exp).then_inc(s_a, 1)

            sb_log((0, 1))
            sb_log((2, 3))
            for g in range(0, SH // 2, 2):
                sb_exp(g)
                sb_exp(g + 1)
                if g + 4 < SH // 2:
                    sb_log((g + 4, g + 5))
                if g >= 4:
                    split_high(act, "sb_out", g // 2 - 2)
            project_act(act, "sb_out", soT, soT_ready)

            split_high(act, "up1", 0)
            norm_act(act, 3)
            split_norm(act, 3, 0)
            split_high(act, "up1", 1)
            ffn(1)
            split_high(act, "mix_in", 0)
            norm_act(act, 4)
            norm_act(act, 5)
            split_norm(act, 5, 0)
            split_high(act, "mix_in", 1)

            act.wait_ge(l_f, 1)
            link(nc.scalar.activation(rows4[0:LH, 2, :], rows4[0:LH, 1, :], ACT.Abs))
            link(nc.scalar.activation(rows4[0:LH, 2, :], rows4[0:LH, 2, :], ACT.Exp, scale=-1.0))
            nc.scalar.activation(rows4[0:LH, 2, :], rows4[0:LH, 2, :], ACT.Ln, bias=1.0).then_inc(l_ln, 1)
            w0, b0 = SMALL["conv2_w"][0], SMALL["conv2_b"][0]
            for q in range(4):
                wide_done(act, halves["mix_in"] + q + 1)
                split_high(act, "mix_in", q + 2)
                if q:
                    act.wait_ge(mi_si, q)
                for f in range(2):
                    n = 2 * q + f
                    last = nc.scalar.activation(cvm[:, f, :], ps[:, q, f * T:(f + 1) * T], ACT.Identity,
                                                scale=small[:, w0 + 4 * n + 3:w0 + 4 * n + 4],
                                                bias=small[:, b0 + n:b0 + n + 1])
                last.then_inc(mi_id, 1)
                act.wait_ge(mi_cv, q + 1)
                nc.scalar.activation(qkm[:, 2 * q:2 * q + 2, :], cvm[:, :, :], ACT.Silu).then_inc(mi_si, 1)
            for h in range(4, MIX):
                wide_done(act, halves["mix_in"] + h + 1)
                if h in (4, 6):
                    nc.scalar.activation(qka[:, 2 * (h - 4):2 * (h - 4) + 2, :].rearrange("p a b -> p (a b)"),
                                         ps[:, h % 4, :], ACT.Copy).then_inc(mi_ev_a, 1)
                if h == 9:
                    nc.scalar.activation(vm[:, 0, :].rearrange("p (h e) -> p h e", h=LH)[:, :, 0:LDH],
                                         ps[:, 0, :].rearrange("p (h e) -> p h e", h=LH), ACT.Copy)\
                        .then_inc(mi_ev_a, 1)
                if h == 11:
                    nc.scalar.activation(om[:, 0, :], ps[:, 2, :], ACT.Copy).then_inc(mi_ev_a, 1)
                if h == 13:
                    nc.scalar.activation(va[:, 0, :], ps[:, 0, :], ACT.Copy).then_inc(mi_ev_a, 1)
                if h + 2 < MIX:
                    split_high(act, "mix_in", h + 2)
            act.wait_ge(mi_ev_a, 5)
            act.wait_ge(mi_ev_v, 5)
            nc.scalar.activation(om[:, :, :], om[:, :, :], ACT.Sigmoid).then_inc(l_sig, 1)
            act.wait_ge(l_rows, 1)
            act.wait_ge(l_cols, 1)
            nc.scalar.activation(fcol[:, :, :], fcol[:, :, :], ACT.Exp).then_inc(l_floor, 1)
            for h in range(LH):
                act.wait_ge(l_w, h + 1)
                nc.scalar.activation(wt[:, h % 2, :], wt[:, h % 2, :], ACT.Exp).then_inc(l_e, 1)
                if h % 2:
                    split_high(act, "mix_out", h // 2)
            for h in range(MH):
                act.wait_ge(b_mx, h + 1)
                for blk, (c0, c1) in enumerate(((0, P), (P, TRI))):
                    last = nc.scalar.activation(m_sc[h % 3][:, c0:c1], m_sc[h % 3][:, c0:c1], ACT.Exp,
                                                bias=mst[:, 4 * h + blk:4 * h + blk + 1],
                                                accum_out=mst[:, 4 * h + 2 + blk:4 * h + 3 + blk])
                last.then_inc(b_e, 1)
            act.wait_ge(l_h, LH)
            for h in range(LH):
                for t in range(NT):
                    link(nc.scalar.activation(pt[:, 0, 0:LDH], hm[:, t, h * LDH:(h + 1) * LDH], ACT.Square,
                                              accum_out=mst[:, 64 + 2 * h + t:65 + 2 * h + t]))
            nc.scalar.activation(credit[:, 5:6], small[:, 0:1], ACT.Copy).then_inc(l_sq, 1)
            act.wait_ge(l_ms, 1)
            nc.scalar.activation(mst[:, 72:80], mst[:, 64:72], ACT.Sqrt).then_inc(l_sd, 1)

            project_act(act, "mix_out", mixT, mixT_ready)

            norm_act(act, 6)
            norm_evict(act, 6, 0)
            act.wait_ge(t_top, 1)
            for t in range(NT):
                last = nc.scalar.activation(g8[:, t, 0:NG], g8[:, t, 0:NG], ACT.Exp, accum_out=rst[:, 4 + t:5 + t])
            link(last)
            nc.scalar.activation(rst[:, 8:10], rst[:, 6:8], ACT.Exp).then_inc(t_exp, 1)

            def expert_pass(r):
                def xg_evict(value):
                    act.wait_ge(m_ga, value)
                    for k in range(4):
                        last = nc.scalar.activation(xg[:, k, :], ps[:, 4, k * P:(k + 1) * P], ACT.Identity,
                                                    scale=mods[:, 2, k:k + 1], bias=mods[:, 3, k:k + 1])
                    last.then_inc(m_xa, 1)

                act.wait_ge(m_zero, 3 * (r + 1))
                nc.scalar.activation(credit[:, 6:7], small[:, 0:1], ACT.Copy).then_inc(m_ya, 1)
                xg_evict((PAIRS + 1) * 2 * r + 2)
                with act.Fori(0, PAIRS) as i:
                    act.wait_ge(m_gu, i * 2 + (PAIRS * 2 * r + 1))
                    nc.scalar.activation(hs, ps[:, 4, :], ACT.Silu).then_inc(m_si, 1)
                    act.wait_ge(m_ht, i + (PAIRS * r + 1))
                    nc.scalar.activation(hgT[:, :, :].rearrange("p k n -> p (k n)"), ps[:, 4, :], ACT.Copy)\
                        .then_inc(m_hc, 1)
                    xg_evict(i * 2 + ((PAIRS + 1) * 2 * r + 4))
                    act.wait_ge(m_dn, i + (PAIRS * r + 1))
                    nc.scalar.activation(ye[:, 0:C], ps[:, 6, :], ACT.Copy).then_inc(m_ya, 1)

            expert_pass(0)
            act.wait_ge(t_flag, 1)
            most = act.value_load(flag[0:1, 0:1])
            with act.If(most > R):
                for r in range(1, PASSES):
                    expert_pass(r)
            norm_act(act, 7)

        @block.vector
        def _(dve):
            link = Link(dve, dve_chain)
            norm_dve(dve, link, 0)
            dve.wait_ge(small_in, 16)
            nc.vector.memset(credit[:, 0:1], 0.0).then_inc(rqk_free, 4)
            nc.vector.memset(credit[:, 2:3], 0.0).then_inc(rvg_fv, 2)
            split_low(dve, "ret_qk", 0)
            split_norm(dve, 0, 1)
            split_low(dve, "ret_qk", 1)
            cos, sin = k_("cos"), k_("sin")
            dve.wait_ge(const_in, 16)
            with dve.Fori(0, 2) as i:
                link.enter(i, 4)
                for b in range(2):
                    for j in range(2):
                        q = i * 4 + (2 * b + j)
                        u = ps[:, 2 * b + j, :]
                        split_low(dve, "ret_qk", 2 * b + j + 2, i, 4)
                        wide_done(dve, 2 * b + j + 1, i, 4)
                        nc.vector.tensor_tensor(rot_a, u, cos, ALU.mult)
                        nc.vector.tensor_tensor(rot_b[:, 0:T], u[:, T:C], sin[:, 0:T], ALU.mult)
                        nc.vector.tensor_tensor(rot_b[:, T:C], u[:, 0:T], sin[:, T:C], ALU.mult)\
                            .then_inc(rqk_free, 1)
                        dve.wait_ge(rqk_free, i * 4 + (4 + 2 * b + j + 1))
                        link(nc.vector.tensor_tensor(qk[:, q, :], rot_a, rot_b, ALU.add))
            link.leave(2)
            nc.vector.memset(credit[:, 0:1], 0.0).then_inc(rqk_out, 8)

            def v_group(i, more):
                for h in range(4):
                    if h % 2:
                        wide_done(dve, halves["ret_vg"] + h + 1, i, 4)
                        nc.vector.tensor_copy(vg[:, 1, bass.ds(i * 2 * C + h // 2 * C, C)], ps[:, 4 + h, :])\
                            .then_inc(rvg_fv, 1)
                    if more or h < 2:
                        split_low(dve, "ret_vg", h + 2, i, 4)

            with dve.Fori(0, 3) as i:
                v_group(i, True)
            v_group(3, False)

            decay = k_("decay").rearrange("p (h t) -> p h t", h=RH)

            def ret_decay(h):
                dve.wait_ge(r_s, h + 1)
                if h >= 2:
                    dve.wait_ge(r_o, 2 * (h - 1))
                nc.vector.tensor_tensor(r_sc[:, h % 2, :], ps[:, h % 2, 0:TRI], decay[:, h, :], ALU.mult)\
                    .then_inc(r_d, 1)

            def ret_y(h):
                dve.wait_ge(r_sq, 2 * (h + 1))
                nc.vector.tensor_scalar(stat[:, 10:12], stat[:, 8:10], 1.0 / RDV, EPS, ALU.mult, ALU.add)\
                    .then_inc(r_ms, 1)
                dve.wait_ge(r_sd, h + 1)
                link(nc.vector.reciprocal(stat[:, 14:16], stat[:, 12:14]))
                if h == 0:
                    dve.wait_ge(rg_silu, 2)
                for t in range(NT):
                    g = vg[:, t, RV + h * RDV:RV + (h + 1) * RDV]
                    nc.vector.scalar_tensor_tensor(out=g, in0=ps[:, 2 + 2 * (h % 2) + t, :], scalar=stat[:, 14 + t:15 + t],
                                                   in1=g, op0=ALU.mult, op1=ALU.mult).then_inc(r_y, 1)

            def ret_copy(h):
                dve.wait_ge(r_t, 2 * h + 2)
                nc.vector.tensor_copy(yT[:, 4 * h + 2:4 * h + 4, :].rearrange("p a b -> p (a b)"), ps[:, 7, :])\
                    .then_inc(r_tv, 1)

            ret_decay(0)
            ret_decay(1)
            for h in range(RH):
                ret_y(h)
                if h + 2 < RH:
                    ret_decay(h + 2)
                if h >= 1:
                    ret_copy(h - 1)
                if h < 2:
                    split_low(dve, "ret_out", h)
            ret_copy(RH - 1)
            project_dve(dve, "ret_out", yT)
            split_low(dve, "up0", 0)
            residual(dve, "ret_out")
            norm_dve(dve, link, 1)
            nc.vector.memset(credit[:, 0:1], 0.0).then_inc(up_free, 4)
            split_norm(dve, 1, 1)
            split_low(dve, "up0", 1)

            def adaptive(h):
                if h not in (4, 5, 8, 9):
                    return
                h = (4, 5, 8, 9).index(h)
                i, kh = h // 2, h % 2
                acc, w = ada_acc[:, (ADA_POOL + i) * C:(ADA_POOL + i + 1) * C], ada_w[kh]
                dve.wait_ge(ada_in[kh], 16 * (ADA_POOL + i + 1))
                for k in range(4):
                    sc = stat[:, 16 + 4 * kh + k:17 + 4 * kh + k]
                    if kh == 0 and k == 0:
                        ins = nc.vector.tensor_scalar(acc, w[:, k, :], sc, None, ALU.mult)
                    else:
                        ins = nc.vector.scalar_tensor_tensor(out=acc, in0=w[:, k, :], scalar=sc, in1=acc,
                                                             op0=ALU.mult, op1=ALU.add)
                    if k < 3:
                        link(ins)
                ins.then_inc(ada_used, 1)
                dve.wait_ge(ada_used, h + 1)
                if h + 1 == 2 * (12 - ADA_POOL):
                    nc.vector.memset(credit[:, 2:3], 0.0).then_inc(ada_sum, 1)

            def ffn(l):
                base = (FP + 4) * l
                def pair(b, j, off, split):
                    n = off + (2 * b + j)
                    w0 = SMALL["conv_w"][0]
                    tap = lambda gv, k: small[:, bass.ds(n * 3 + (w0 + (l * 2 + gv) * FP * 3 + k), 1)]
                    c, u = cv[:, j, :], ps[:, (2 * b + j) % 4, :]
                    if split is not None:
                        split_low(dve, f"up{l}", 2 * b + j + 2, split, 8)
                    elif b < 2:
                        split_low(dve, f"up{l}", off + 2 * b + j + 2)
                    else:
                        if j == 1:
                            src_low(dve, f"down{l}", hff, 0)
                        split_low(dve, f"down{l}", j)
                        if j == 1:
                            src_low(dve, f"down{l}", hff, 1)
                    dve.wait_ge(up_id, off + (FP * l + 2 * b + j + 1))
                    for gv in range(2):
                        o = gv * T
                        last = nc.vector.scalar_tensor_tensor(
                            out=c[:, o + 1:o + T], in0=u[:, o:o + T - 1], scalar=tap(gv, 1), in1=c[:, o + 1:o + T],
                            op0=ALU.mult, op1=ALU.add)
                    link(last)
                    for gv in range(2):
                        o = gv * T
                        last = nc.vector.scalar_tensor_tensor(
                            out=c[:, o + 2:o + T], in0=u[:, o:o + T - 2], scalar=tap(gv, 0), in1=c[:, o + 2:o + T],
                            op0=ALU.mult, op1=ALU.add)
                        if gv == 0:
                            last.then_inc(up_cv, 1)
                    last.then_inc(up_free, 1)
                    dve.wait_ge(up_free, off + (base + 4 + 2 * b + j + 1))
                    dve.wait_ge(up_si, off + (FP * l + 2 * b + j + 1))
                    nc.vector.tensor_tensor(hff[:, n, :], c[:, 0:T], c[:, T:C], ALU.mult).then_inc(up_h, 1)

                with dve.Fori(0, 2) as i:
                    link.enter(i, 8)
                    for b in range(4):
                        for j in range(2):
                            pair(b, j, i * 8, i)
                link.leave(2)
                for b in range(3):
                    for j in range(2):
                        pair(b, j, 16, None)
                project_dve(dve, f"down{l}", hff, adaptive if l == 0 else None, 2)
                split_low(dve, ("sb_qk", "mix_in")[l], 0)
                residual(dve, f"down{l}")

            ffn(0)

            def modulations():
                mr = modr[:, :].rearrange("p (m k) -> p m k", m=4)
                dve.wait_ge(ada_mods, 1)
                ba = b_ada.rearrange("p (m k) -> p m k", m=6)
                for m, q in enumerate((0, 1, 3, 4)):
                    last = nc.vector.tensor_tensor(mr[:, m, :], ps[:, 3, m * KD:(m + 1) * KD], ba[:, q, :], ALU.add)
                last.then_inc(ada_gate, 1)
                dve.wait_ge(ada_gate, 1)
                for n, (sh, scl, g) in enumerate(((0, 1, "g1"), (2, 3, "g2"))):
                    nc.vector.tensor_copy(mods[:, 2 * n + 1, :], mr[:, sh, :])
                    link(nc.vector.scalar_tensor_tensor(out=mods[:, 2 * n, :], in0=mr[:, scl, :], scalar=1.0,
                                                        in1=s_(g), op0=ALU.add, op1=ALU.mult))

            modulations()
            norm_dve(dve, link, 2)
            nc.vector.memset(credit[:, 0:1], 0.0).then_inc(sqk_fv, 2)
            split_norm(dve, 2, 1)
            split_low(dve, "sb_qk", 1)
            dve.wait_ge(ada_mods, 2)
            dve.wait_ge(bias_in, 32)
            for half in range(4):
                gt = gates[:, half // 2, (half % 2) * C:(half % 2 + 1) * C]
                nc.vector.tensor_tensor(gt, ps[:, 4 + half, :], gt, ALU.add).then_inc(ada_gate, 1)

            with dve.Fori(0, 2) as i:
                for h in range(4):
                    if h % 2:
                        wide_done(dve, halves["sb_qk"] + h + 1, i, 4)
                        nc.vector.tensor_copy(sqk[:, i * 4 + h, :], ps[:, h, :]).then_inc(sqk_fv, 1)
                    split_low(dve, "sb_qk", h + 2, i, 4)
            for h in range(4):
                if h % 2:
                    wide_done(dve, halves["sb_v"] + h + 1)
                    u = h // 2
                    nc.vector.tensor_copy(sv[:, 1, u * C:(u + 1) * C], ps[:, 5 + 2 * u, :]).then_inc(sv_v, 1)
                if h < 2:
                    split_low(dve, "sb_v", h + 2)

            def sb_softplus(g):
                dve.wait_ge(s_zc, g + 1)
                dve.wait_ge(s_l, g + 1)
                if g >= 2:
                    dve.wait_ge(s_ex, g - 1)
                nc.vector.scalar_tensor_tensor(out=sp_b[g % 2], in0=z_b[g % 4], scalar=0.0, in1=l_b[g % 4],
                                               op0=ALU.max, op1=ALU.add).then_inc(s_sp, 1)

            def sb_log_a(g):
                link(nc.vector.scalar_tensor_tensor(out=z_b[g % 4], in0=z_b[g % 4], scalar=0.0, in1=l_b[g % 4],
                                                    op0=ALU.min, op1=ALU.subtract))
                dve.wait_ge(s_ex, g + 1)
                if g >= 2:
                    dve.wait_ge(s_o, g - 1)
                nc.vector.tensor_tensor(a_b[g % 2], z_b[g % 4], ps[:, 4:6, 0:TRI], ALU.subtract).then_inc(s_la, 1)

            def sb_copy(g):
                dve.wait_ge(s_o, g + 1)
                nc.vector.tensor_copy(soT[:, g, :], ps[:, 6 + g % 2, 0:T]).then_inc(s_ot, 1)

            for g in range(0, SH // 2, 2):
                sb_softplus(g)
                sb_softplus(g + 1)
                dve.wait_ge(s_sp, g + 2)
                sb_log_a(g)
                sb_log_a(g + 1)
                if g >= 2:
                    sb_copy(g - 2)
                    sb_copy(g - 1)
            split_low(dve, "sb_out", 0)
            sb_copy(SH // 2 - 2)
            sb_copy(SH // 2 - 1)
            src_low(dve, "sb_out", soT, 0)
            split_low(dve, "sb_out", 1)
            project_dve(dve, "sb_out", soT, None, 1)
            split_low(dve, "up1", 0)
            residual(dve, "sb_out")
            norm_dve(dve, link, 3)
            nc.vector.memset(credit[:, 0:1], 0.0).then_inc(up_free, 4)
            split_norm(dve, 3, 1)
            split_low(dve, "up1", 1)
            ffn(1)

            def scale_rows():
                for t in range(NT):
                    nc.vector.scalar_tensor_tensor(out=x[:, t, :], in0=x[:, t, :], scalar=stat[:, 6 + t:7 + t],
                                                   in1=rowv[:, :], op0=ALU.mult, op1=ALU.mult).then_inc(x_new, 1)

            norm_dve(dve, link, 4)
            dve.wait_ge(row_in, 16)
            dve.wait_ge(x_new, update(3))
            scale_rows()
            norm_dve(dve, link, 5)
            split_norm(dve, 5, 1)
            split_low(dve, "mix_in", 1)

            row = lambda n: rows4[0:LH, n, :]
            dve.wait_ge(mix_small, 80)
            nc.vector.memset(vm[:, :, :], 1.0)
            nc.vector.memset(row(8), 1.0)
            dve.wait_ge(mi_g, 1)
            link(nc.vector.tensor_scalar(row(0), ps[0:LH, 4, 0:T], bg[0:LH, 0:1], None, ALU.add))
            nc.vector.tensor_scalar(row(1), ps[0:LH, 5, 0:T], bg[0:LH, 1:2], None, ALU.add).then_inc(l_f, 1)
            dve.wait_ge(l_ln, 1)
            dve.wait_ge(l_f, 1)
            link(nc.vector.scalar_tensor_tensor(out=row(1), in0=row(1), scalar=0.0, in1=row(2), op0=ALU.min,
                                                op1=ALU.subtract))
            link(nc.vector.tensor_tensor_scan(row(3), row(8), row(1), 0.0, ALU.mult, ALU.add))
            link(nc.vector.tensor_tensor(row(4), row(0), row(3), ALU.subtract))
            link(nc.vector.tensor_tensor_scan(row(5), row(8), row(4), 0.0, ALU.mult, ALU.max))
            nc.vector.tensor_scalar(row(6), row(5), -1.0, None, ALU.mult)
            nc.vector.scalar_tensor_tensor(out=row(7), in0=row(3), scalar=-1.0, in1=row(5), op0=ALU.mult,
                                           op1=ALU.subtract).then_inc(l_rows, 1)

            w0 = SMALL["conv2_w"][0]
            for q in range(4):
                split_low(dve, "mix_in", q + 2)
                dve.wait_ge(mi_id, q + 1)
                for k in (2, 1, 0):
                    for f in range(2):
                        n, d = 2 * q + f, 3 - k
                        ins = nc.vector.scalar_tensor_tensor(
                            out=cvm[:, f, d:T], in0=ps[:, q, f * T:(f + 1) * T - d],
                            scalar=small[:, w0 + 4 * n + k:w0 + 4 * n + k + 1], in1=cvm[:, f, d:T],
                            op0=ALU.mult, op1=ALU.add)
                    if k:
                        link(ins)
                ins.then_inc(mi_cv, 1)
            for h in range(4, 12):
                if h in (5, 7, 9, 11):
                    wide_done(dve, halves["mix_in"] + h + 1)
                if h in (5, 7):
                    nc.vector.tensor_copy(qka[:, 2 * (h - 4):2 * (h - 4) + 2, :].rearrange("p a b -> p (a b)"),
                                          ps[:, h % 4, :]).then_inc(mi_ev_v, 1)
                if h == 9:
                    nc.vector.tensor_copy(vm[:, 1, :].rearrange("p (h e) -> p h e", h=LH)[:, :, 0:LDH],
                                          ps[:, 1, :].rearrange("p (h e) -> p h e", h=LH)).then_inc(mi_ev_v, 1)
                if h == 11:
                    nc.vector.tensor_copy(om[:, 1, :], ps[:, 3, :]).then_inc(mi_ev_v, 1)
                if h + 2 < MIX:
                    split_low(dve, "mix_in", h + 2)
            dve.wait_ge(l_tr, 1)
            nc.vector.tensor_copy(acol[:, :, :].rearrange("p a b -> p (a b)"), ps[:, 6, 0:8])
            nc.vector.tensor_copy(fcol[:, :, :].rearrange("p a b -> p (a b)"), ps[:, 6, 8:16]).then_inc(l_cols, 1)
            wide_done(dve, halves["mix_in"] + 14)
            nc.vector.tensor_copy(va[:, 1, :], ps[:, 1, :]).then_inc(mi_ev_v, 1)
            dve.wait_ge(l_sig, 1)
            gh = ghead.unsqueeze(1).broadcast_to([P, NT, C])
            link(nc.vector.tensor_tensor(om[:, :, :], om[:, :, :], gh, ALU.mult))
            dve.wait_ge(l_cols, 1)

            def ls_w(h):
                b = 3 * (h % 2)
                dve.wait_ge(l_s, h + 1)
                if h >= 2:
                    dve.wait_ge(l_p, h - 1)
                nc.vector.tensor_scalar(wt[:, h % 2, 0:T], ps[:, b, 0:T], acol[:, 0, h:h + 1], 0.0, ALU.add, ALU.min)
                nc.vector.tensor_scalar(wt[:, h % 2, T:TRI], ps[:, b, P:T], acol[:, 1, h:h + 1], 0.0, ALU.add, ALU.min)\
                    .then_inc(l_w, 1)

            def ls_p(h):
                b = 3 * (h % 2) + 1
                dve.wait_ge(l_e, h + 1)
                diag = wt[:, h % 2, :].rearrange("p (b t) -> p b t", b=3)[:, 0:3:2, :]
                link(nc.vector.tensor_tensor(diag, diag, upto.unsqueeze(1).broadcast_to([P, 2, P]), ALU.mult))
                if h >= 2:
                    dve.wait_ge(l_o, h - 1)
                nc.vector.scalar_tensor_tensor(out=pt[:, h % 2, :], in0=ps[:, b, 0:TRI], scalar=LDH ** -0.5,
                                               in1=wt[:, h % 2, :], op0=ALU.mult, op1=ALU.mult).then_inc(l_p, 1)

            def ls_h(h):
                b = 3 * (h % 2) + 2
                dve.wait_ge(l_o, h + 1)
                if h == 0:
                    dve.wait_ge(l_floor, 1)
                den = lambda t: mst[:, 80 + 2 * h + t:81 + 2 * h + t]
                for t in range(NT):
                    last = nc.vector.tensor_scalar(den(t), ps[:, b, t * T + LDH:t * T + LDH + 1], -1.0,
                                                   fcol[:, t, h:h + 1], ALU.mult, ALU.max)
                link(last)
                for t in range(NT):
                    last = nc.vector.tensor_tensor(den(t), ps[:, b, t * T + LDH:t * T + LDH + 1], den(t), ALU.max)
                link(last)
                link(nc.vector.reciprocal(mst[:, 88 + 2 * h:90 + 2 * h], mst[:, 80 + 2 * h:82 + 2 * h]))
                for t in range(NT):
                    last = nc.vector.tensor_scalar(hm[:, t, h * LDH:(h + 1) * LDH], ps[:, b, t * T:t * T + LDH],
                                                   mst[:, 88 + 2 * h + t:89 + 2 * h + t], None, ALU.mult)
                last.then_inc(l_h, 1)

            ls_w(0)
            ls_w(1)
            ls_p(0)
            for h in range(LH):
                if h + 1 < LH:
                    ls_p(h + 1)
                if h + 2 < LH:
                    ls_w(h + 2)
                ls_h(h)

            future = k_("future")

            def mb_max(h):
                dve.wait_ge(b_s, h + 1)
                if h >= 3:
                    dve.wait_ge(b_t, h - 2)
                sc = m_sc[h % 3]
                link(nc.vector.scalar_tensor_tensor(out=sc, in0=ps[:, 6 + h % 2, 0:TRI], scalar=MDH ** -0.5, in1=future,
                                                    op0=ALU.mult, op1=ALU.add))
                nc.vector.tensor_reduce(mst[:, 4 * h:4 * h + 1], sc[:, 0:P], AX, ALU.max, negate=True)
                nc.vector.tensor_reduce(mst[:, 4 * h + 1:4 * h + 2], sc[:, P:TRI], AX, ALU.max, negate=True)\
                    .then_inc(b_mx, 1)

            def mb_p(h):
                dve.wait_ge(b_e, h + 1)
                link(nc.vector.reciprocal(mst[:, 4 * h + 2:4 * h + 4], mst[:, 4 * h + 2:4 * h + 4]))
                for blk, (c0, c1) in enumerate(((0, P), (P, TRI))):
                    last = nc.vector.tensor_scalar(m_sc[h % 3][:, c0:c1], m_sc[h % 3][:, c0:c1],
                                                   mst[:, 4 * h + 2 + blk:4 * h + 3 + blk], None, ALU.mult)
                last.then_inc(b_p, 1)

            def mb_copy(h):
                dve.wait_ge(b_t, h + 1)
                if h >= 2:
                    dve.wait_ge(b_o, h - 1)
                nc.vector.tensor_copy(wt[:, h % 2, :], ps[:, h % 2, 0:TRI]).then_inc(b_tc, 1)

            def mb_o(g):
                dve.wait_ge(b_o, 2 * (g + 1))
                nc.vector.tensor_copy(mixT[:, 4 + g, :], ps[:, 3 + g % 2, 0:T]).then_inc(b_oc, 1)

            mb_max(0)
            mb_max(1)
            for h in range(MH):
                mb_p(h)
                if h >= 1:
                    mb_copy(h - 1)
                if h + 2 < MH:
                    mb_max(h + 2)
                if h >= 3 and h % 2:
                    mb_o((h - 3) // 2)
            mb_copy(MH - 1)
            mb_o(MH // 2 - 1)

            dve.wait_ge(l_sq, 1)
            nc.vector.tensor_scalar(mst[:, 64:72], mst[:, 64:72], 1.0 / LDH, EPS, ALU.mult, ALU.add).then_inc(l_ms, 1)
            dve.wait_ge(l_sd, 1)
            link(nc.vector.reciprocal(mst[:, 96:104], mst[:, 72:80]))
            for h in range(LH):
                for t in range(NT):
                    cols = slice(h * LDH, (h + 1) * LDH)
                    nc.vector.scalar_tensor_tensor(out=hm[:, t, cols], in0=hm[:, t, cols],
                                                   scalar=mst[:, 96 + 2 * h + t:97 + 2 * h + t], in1=om[:, t, cols],
                                                   op0=ALU.mult, op1=ALU.mult).then_inc(l_hn, 1)
            for j in range(2):
                dve.wait_ge(l_t, j + 1)
                nc.vector.tensor_copy(mixT[:, 2 * j:2 * j + 2, :].rearrange("p a b -> p (a b)"), ps[:, j, :])\
                    .then_inc(l_mt, 1)

            def zero_experts():
                nc.vector.memset(selT[:, :], 0.0).then_inc(m_zero, 1)
                nc.vector.memset(ye[:, :], 0.0).then_inc(m_zero, 1)

            dve.wait_ge(lo_done, halves["mix_out"] + 2)
            project_dve(dve, "mix_out", mixT)
            zero_experts()
            for t in range(NT):
                if t == 0:
                    dve.wait_ge(tile0_mm, len(PROJECTIONS))
                    wide_done(dve, n_halves - 1)
                else:
                    wide_done(dve, n_halves)
                gated_residual(link, 0, 4, gtmp, True, (t,))

            norm_dve(dve, link, 6)
            norm_evict(dve, 6, 1)

            dve.wait_ge(t_lg, 1)
            dve.wait_ge(r_in, 64)
            lgp = ps[:, 4, 0:P].rearrange("p (t n) -> p t n", t=NT)[:, :, 0:NG + NE]
            nc.vector.memset(g8[:, :, :], NEG)
            nc.vector.memset(pos[:, :, :], -1.0)
            nc.vector.memset(wgt[:, :, :], 0.0)
            link(nc.vector.tensor_tensor(lg[:, :, :], lgp, br.unsqueeze(1).broadcast_to([P, NT, NG + NE]), ALU.add))
            link(nc.vector.tensor_copy(g8[:, :, 0:NG], lg[:, :, 0:NG]))
            for t in range(NT):
                link(nc.vector.max(m8[:, t, :], g8[:, t, :]))
                link(nc.vector.max_index(i8[:, t, :], m8[:, t, :], g8[:, t, :]))
            link(nc.vector.tensor_copy(f8[:, :, :], i8[:, :, :]))
            for t in range(NT):
                nc.vector.tensor_scalar(oh[:, t, :], iota[:, 0:NG], f8[:, t, 0:1], None, ALU.is_equal)
                link(nc.vector.tensor_scalar(g8[:, t, 0:NG], g8[:, t, 0:NG], m8[:, t, 0:1], None, ALU.subtract))
            link(nc.vector.tensor_scalar(oh[:, :, :], oh[:, :, :], -1.0, -NEG, ALU.add, ALU.mult))
            for t in range(NT):
                pen = oh[:, t, :].unsqueeze(2).broadcast_to([P, NG, EPG])
                link(nc.vector.tensor_tensor(em[:, t, :].rearrange("p (g e) -> p g e", g=NG),
                                             lg[:, t, NG:].rearrange("p (g e) -> p g e", g=NG), pen, ALU.add))
                link(nc.vector.max(m8[:, t, :], em[:, t, :]))
                link(nc.vector.max_index(i8[:, t, :], m8[:, t, :], em[:, t, :]))
            link(nc.vector.tensor_copy(f8[:, :, :], i8[:, :, :]))
            for t in range(NT):
                last = nc.vector.tensor_tensor(rst[:, 6 + t:7 + t], m8[:, t, 1:2], m8[:, t, 0:1], ALU.subtract)
                link(nc.vector.tensor_scalar(oh1[:, t, :], iota[:, 0:NE], f8[:, t, 0:1], None, ALU.is_equal))
                link(nc.vector.tensor_scalar(oh2[:, t, :], iota[:, 0:NE], f8[:, t, 1:2], None, ALU.is_equal))
            nc.vector.memset(credit[:, 0:1], 0.0).then_inc(t_top, 1)
            nc.vector.tensor_tensor(asg[:, :, :], oh1[:, :, :], oh2[:, :, :], ALU.add).then_inc(t_rank, 1)
            dve.wait_ge(t_exp, 1)
            link(nc.vector.tensor_scalar(rst[:, 10:12], rst[:, 8:10], 1.0, None, ALU.add))
            link(nc.vector.tensor_tensor(rst[:, 10:12], rst[:, 10:12], rst[:, 4:6], ALU.mult))
            link(nc.vector.reciprocal(rst[:, 12:14], rst[:, 10:12]))
            link(nc.vector.tensor_tensor(rst[:, 14:16], rst[:, 12:14], rst[:, 8:10], ALU.mult))
            for t in range(NT):
                link(nc.vector.tensor_scalar(oh2[:, t, :], oh2[:, t, :], rst[:, 14 + t:15 + t], None, ALU.mult))
                link(nc.vector.scalar_tensor_tensor(out=wgt[:, t, 0:NE], in0=oh1[:, t, :], scalar=rst[:, 12 + t:13 + t],
                                                    in1=oh2[:, t, :], op0=ALU.mult, op1=ALU.add))
            dve.wait_ge(t_lg, 2)
            dve.wait_ge(t_rank, 1)
            rank = ps[:, 5, 0:P].rearrange("p (t n) -> p t n", t=NT)[:, :, 0:NE]
            link(nc.vector.scalar_tensor_tensor(out=em[:, :, :], in0=rank, scalar=1.0, in1=asg[:, :, :],
                                                op0=ALU.add, op1=ALU.mult))
            link(nc.vector.tensor_scalar(pos[:, :, 0:NE], em[:, :, :], -1.0, None, ALU.add))
            link(nc.vector.tensor_reduce(rst[:, 20:21], ps[:, 5, 128:128 + NE], AX, ALU.max))
            nc.vector.tensor_copy(flag, rst[:, 20:21]).then_inc(t_flag, 1)
            dve.wait_ge(norm_ha, 4)

            def expert_pass(r, link):
                slots = iota[:, r * R:(r + 1) * R]

                def select(buf, i, weigh, done):
                    for t in range(NT):
                        for e in range(2):
                            col = i * 2 + e
                            if weigh:
                                ins = nc.vector.tensor_scalar(buf[:, t, e * R:(e + 1) * R], slots,
                                                              pos[:, t, bass.ds(col, 1)], wgt[:, t, bass.ds(col, 1)],
                                                              ALU.is_equal, ALU.mult)
                            else:
                                ins = nc.vector.tensor_scalar(buf[:, t, e * R:(e + 1) * R], slots,
                                                              pos[:, t, bass.ds(col, 1)], None, ALU.is_equal)
                    ins.then_inc(done, 1)

                def xg_evict(value):
                    dve.wait_ge(m_ga, value)
                    for k in range(4, 8):
                        last = nc.vector.tensor_scalar(xg[:, k, :], ps[:, 5, (k - 4) * P:(k - 3) * P],
                                                       mods[:, 2, k:k + 1], mods[:, 3, k:k + 1], ALU.mult, ALU.add)
                    last.then_inc(m_xv, 1)

                if r:
                    zero_experts()
                nc.vector.memset(credit[:, 0:1], 0.0).then_inc(m_zero, 1)
                dve.wait_ge(m_zero, 3 * (r + 1))
                nc.vector.memset(credit[:, 1:2], 0.0).then_inc(m_yv, 1)
                dve.wait_ge(m_start, r + 1)
                select(sel, 0, False, m_s)
                select(selw, 0, True, m_sw)
                xg_evict((PAIRS + 1) * 2 * r + 1)
                dve.wait_ge(m_ga, (PAIRS + 1) * 2 * r + 2)
                select(sel, 1, False, m_s)
                with dve.Fori(0, PAIRS) as i:
                    dve.wait_ge(m_si, i + (PAIRS * r + 1))
                    dve.wait_ge(m_gu, i * 2 + (PAIRS * 2 * r + 2))
                    nc.vector.tensor_tensor(hg, hs, ps[:, 5, :], ALU.mult).then_inc(m_h, 1)
                    dve.wait_ge(m_sct, i + ((PAIRS + 1) * r + 1))
                    nc.vector.tensor_copy(selT[:, :], ps[:, 6, 0:T]).then_inc(m_swt, 1)
                    xg_evict(i * 2 + ((PAIRS + 1) * 2 * r + 3))
                    dve.wait_ge(m_ga, i * 2 + ((PAIRS + 1) * 2 * r + 4))
                    select(sel, i + 2, False, m_s)
                    select(selw, i + 1, True, m_sw)
                    dve.wait_ge(m_dn, i + (PAIRS * r + 1))
                    nc.vector.tensor_copy(ye[:, C:2 * C], ps[:, 7, :]).then_inc(m_yv, 1)
                dve.wait_ge(m_sct, (PAIRS + 1) * (r + 1))
                gated_residual(link, 1, 0, gtmp, False)

            expert_pass(0, link)
            most = dve.value_load(flag[0:1, 0:1])
            with dve.If(most > R):
                more = Link(dve, over_chain)
                for r in range(1, PASSES):
                    expert_pass(r, more)
            nc.vector.memset(credit[:, 0:1], 0.0).then_inc(x_new, 4)
            norm_dve(dve, link, 7)
            dve.wait_ge(row_in, 32)
            scale_rows()


_DIRECT = ["x", "ret_w_in", "ret_w_out", "sb_w_in", "sb_w_out", "ffn_w_up", "ffn_w_down", "final_norm", "w_ada_2",
           "b_ada_2", "w_in_2", "w_out_2", "b_gates_2", "g_mlstm_head_2", "w_router_group_2", "b_router_group_2",
           "w_router_expert_2", "b_router_expert_2", "w_expert_gate_2", "w_expert_up_2", "w_expert_down_2",
           "g_final_2"]


def small_weights(inputs):
    get = lambda n: np.asarray(inputs[n])
    feat = lambda a: a.reshape(-1, P).T
    tiles = lambda a: a.reshape(-1, P).T
    cw = get("ffn_conv_w").reshape(2, 3, 2, FP, P).transpose(4, 0, 2, 3, 1).reshape(P, -1)
    parts = {
        "ret_norm": feat(get("ret_norm")[0]), "sb_norm": feat(get("sb_norm")[0]), "ffn_norm": feat(get("ffn_norm")),
        "g1": feat(get("g_norm1_2")[0]), "g2": feat(get("g_norm2_2")[0]), "c": get("c_2").reshape(P, KD),
        "b_ada": feat(get("b_ada_2")[0]), "conv_w": cw, "conv_b": tiles(get("ffn_conv_b")),
        "conv2_w": get("w_conv_2")[0].reshape(4, 2 * LH, P).transpose(2, 1, 0).reshape(P, -1),
        "conv2_b": feat(get("b_conv_2")[0]),
    }
    return np.ascontiguousarray(np.concatenate([parts[n] for n in SMALL], axis=1))


def kernel(**inputs):
    import concourse.bacc as _bacc
    from concourse.bass_utils import run_bass_kernel_spmd as _run

    nc = _bacc.Bacc("TRN2", target_bir_lowering=False, num_devices=1)
    arrays = {f"in_{n}_dram": np.ascontiguousarray(inputs[n]) for n in _DIRECT}
    arrays["in_small_dram"] = small_weights(inputs)
    arrays["in_const_dram"] = shape_constants()
    arrays["in_sel4_dram"] = np.repeat(np.eye(LH, dtype=np.float32), P, axis=1)
    A = {n[3:-5]: nc.dram_tensor(n, a.shape, mybir.dt.from_np(a.dtype), kind="ExternalInput").ap()
         for n, a in arrays.items()}
    out = nc.dram_tensor("out_0_dram", (1, T, D), F32, kind="ExternalOutput").ap()
    build(nc, A, out)
    r = _run(nc, [arrays], core_ids=[0])
    return r.results[0]["out_0_dram"]
```
